# Optimizing a Trainium2 kernel written in Bass

```python
import math
import jax, jax.numpy as jnp
from jax import lax
import numpy as np

D_MODEL = 2048
BATCH = 1
SEQ = 256
DEPTH = 1

N_HEADS = 16
QK_NOPE_DIM = 128
ROPE_DIM = 64
V_HEAD_DIM = 128
Q_LORA_RANK = 512
KV_LORA_RANK = 512
MLA_WIDTH = N_HEADS * V_HEAD_DIM
CONV_WIDTH = D_MODEL
CONV_K = 3
ROPE_THETA = 10000.0
RMS_EPS = 1e-6
BLOCK_Q = 128

IN_SPLIT = [
    Q_LORA_RANK,
    KV_LORA_RANK,
    ROPE_DIM,
    MLA_WIDTH,
    CONV_WIDTH,
    CONV_WIDTH,
    CONV_WIDTH,
    CONV_WIDTH,
    D_MODEL,
    D_MODEL,
]
IN_TOTAL = sum(IN_SPLIT)


def _rmsnorm(x, g):
    xf = x.astype(jnp.float32)
    r = lax.rsqrt(jnp.mean(xf * xf, axis=-1, keepdims=True) + RMS_EPS)
    return (xf * r * g.astype(jnp.float32)).astype(x.dtype)

def _rope_tables(positions):
    inv_freq = ROPE_THETA ** (-jnp.arange(0, ROPE_DIM, 2, dtype=jnp.float32) / ROPE_DIM)
    ang = positions.astype(jnp.float32)[..., None] * inv_freq
    return jnp.cos(ang), jnp.sin(ang)

def _apply_rope(x, cos, sin):
    xf = x.astype(jnp.float32)
    x1, x2 = jnp.split(xf, 2, axis=-1)
    out = jnp.concatenate([x1 * cos - x2 * sin, x1 * sin + x2 * cos], axis=-1)
    return out.astype(x.dtype)

def _causal_mla_attention(q_nope, q_rope, k_nope, k_rope, v):
    b, s, h, _ = q_nope.shape
    nb = s // BLOCK_Q
    scale = 1.0 / math.sqrt(QK_NOPE_DIM + ROPE_DIM)
    qn_blocks = q_nope.reshape(b, nb, BLOCK_Q, h, QK_NOPE_DIM).transpose(1, 0, 2, 3, 4)
    qr_blocks = q_rope.reshape(b, nb, BLOCK_Q, h, ROPE_DIM).transpose(1, 0, 2, 3, 4)
    key_pos = jnp.arange(s, dtype=jnp.int32)

    def one_block(args):
        qn, qr, blk = args
        sc = (jnp.einsum('bqhd,bkhd->bhqk', qn, k_nope)
              + jnp.einsum('bqhr,bkr->bhqk', qr, k_rope)).astype(jnp.float32) * scale
        q_pos = blk * BLOCK_Q + jnp.arange(BLOCK_Q, dtype=jnp.int32)
        mask = key_pos[None, :] <= q_pos[:, None]
        sc = jnp.where(mask[None, None], sc, -jnp.inf)
        p = jax.nn.softmax(sc, axis=-1).astype(v.dtype)
        return jnp.einsum('bhqk,bkhd->bqhd', p, v)

    out = lax.map(one_block, (qn_blocks, qr_blocks, jnp.arange(nb, dtype=jnp.int32)))
    return out.transpose(1, 0, 2, 3, 4).reshape(b, s, h, V_HEAD_DIM)

def first_inputs(seed: int = 0) -> dict:
    key = jax.random.key(seed)
    ks = jax.random.split(key, 16)
    f32 = jnp.float32

    def w(k, shape, fan_in):
        return jax.random.normal(k, shape, f32) * (fan_in ** -0.5)

    def gain(k, n):
        return 1.0 + 0.02 * jax.random.normal(k, (n,), f32)

    x = jax.random.normal(ks[0], (BATCH, SEQ, D_MODEL), f32)
    start = jax.random.randint(ks[1], (BATCH, 1), 0, 1024, dtype=jnp.int32)
    positions = start + jnp.arange(SEQ, dtype=jnp.int32)[None, :]
    return {
        "x": x,
        "positions": positions,
        "pre_norm_g": gain(ks[2], D_MODEL),
        "w_in": w(ks[3], (D_MODEL, IN_TOTAL), D_MODEL),
        "q_a_norm_g": gain(ks[4], Q_LORA_RANK),
        "w_q_b": w(ks[5], (Q_LORA_RANK, N_HEADS * (QK_NOPE_DIM + ROPE_DIM)), Q_LORA_RANK),
        "kv_a_norm_g": gain(ks[6], KV_LORA_RANK),
        "w_kv_b": w(ks[7], (KV_LORA_RANK, N_HEADS * (QK_NOPE_DIM + V_HEAD_DIM)), KV_LORA_RANK),
        "conv_w": w(ks[8], (CONV_K, CONV_WIDTH), CONV_K),
        "w_o_mla": w(ks[9], (MLA_WIDTH, D_MODEL), MLA_WIDTH),
        "w_o_conv": w(ks[10], (CONV_WIDTH, D_MODEL), CONV_WIDTH),
        "w_out": w(ks[11], (D_MODEL, D_MODEL), D_MODEL),
        "post_norm_g": gain(ks[12], D_MODEL),
    }

def first_block(x, positions, pre_norm_g, w_in, q_a_norm_g, w_q_b, kv_a_norm_g, w_kv_b,
              conv_w, w_o_mla, w_o_conv, w_out, post_norm_g):
    b, s, _ = x.shape
    cos, sin = _rope_tables(positions)
    for _layer in range(DEPTH):
        h = _rmsnorm(x, pre_norm_g)
        proj = jnp.einsum('bsd,de->bse', h, w_in)
        cuts = [int(c) for c in np.cumsum(IN_SPLIT)[:-1]]
        (q_a, c_kv, k_rope, z_mla, c_in, b_gate, c_gate, z_conv,
         g_mla, g_conv) = jnp.split(proj, cuts, axis=-1)

        q = jnp.einsum('bsr,re->bse', _rmsnorm(q_a, q_a_norm_g), w_q_b)
        q = q.reshape(b, s, N_HEADS, QK_NOPE_DIM + ROPE_DIM)
        q_nope, q_rope = q[..., :QK_NOPE_DIM], q[..., QK_NOPE_DIM:]
        kv = jnp.einsum('bsr,re->bse', _rmsnorm(c_kv, kv_a_norm_g), w_kv_b)
        kv = kv.reshape(b, s, N_HEADS, QK_NOPE_DIM + V_HEAD_DIM)
        k_nope, v = kv[..., :QK_NOPE_DIM], kv[..., QK_NOPE_DIM:]
        q_rope = _apply_rope(q_rope, cos[:, :, None, :], sin[:, :, None, :])
        k_rope = _apply_rope(k_rope, cos, sin)
        attn = _causal_mla_attention(q_nope, q_rope, k_nope, k_rope, v)
        attn = attn.reshape(b, s, MLA_WIDTH) * jax.nn.silu(z_mla)
        y_mla = jnp.einsum('bse,ed->bsd', attn, w_o_mla)

        u = c_gate * c_in
        u_pad = jnp.pad(u, ((0, 0), (CONV_K - 1, 0), (0, 0)))
        conv = sum(conv_w[k] * u_pad[:, k:k + s] for k in range(CONV_K))
        y_conv = jnp.einsum('bse,ed->bsd', b_gate * conv * jax.nn.silu(z_conv), w_o_conv)

        merged = jax.nn.sigmoid(g_mla) * y_mla + jax.nn.sigmoid(g_conv) * y_conv
        out = jnp.einsum('bsd,de->bse', merged, w_out)
        x = x + _rmsnorm(out, post_norm_g)
    return x


CHUNK = 64
N_META = 16
Q_BLOCK = 128
N_BRANCH = 2
BRANCH_WIDTH = D_MODEL // 2
HD_A = 128
H_A = BRANCH_WIDTH // HD_A
KV_A = H_A // 2
ROT_A = HD_A // 4
H_IDX = D_MODEL // 128
D_IDX = 64
ROT_IDX = D_IDX // 4
TOPK_MAX = 256
DK_B = 128
H_B = BRANCH_WIDTH // DK_B
DV_B = BRANCH_WIDTH // H_B
ROPE_THETA_2 = 500000.0
EPS = 1e-6
SPLIT_SIZES = (H_A * HD_A, KV_A * HD_A, KV_A * HD_A, BRANCH_WIDTH,
               H_IDX * D_IDX, D_IDX, H_IDX,
               H_B * DK_B, H_B * DK_B, H_B * DV_B, BRANCH_WIDTH,
               N_BRANCH * D_MODEL)
N_IN = sum(SPLIT_SIZES)


def rms_norm(x, gain):
    xf = x.astype(jnp.float32)
    y = xf * lax.rsqrt(jnp.mean(xf * xf, axis=-1, keepdims=True) + EPS)
    return (y * gain.astype(jnp.float32)).astype(x.dtype)

def rope_tables(pos, rot_dim):
    inv = jnp.power(ROPE_THETA_2, -jnp.arange(0, rot_dim, 2, dtype=jnp.float32) / rot_dim)
    ang = pos.astype(jnp.float32)[:, None] * inv[None, :]
    return jnp.cos(ang), jnp.sin(ang)

def apply_partial_rope(x, cos, sin):
    half = cos.shape[-1]
    xr = x[..., :2 * half].astype(jnp.float32)
    x1, x2 = xr[..., :half], xr[..., half:]
    c, s = cos[None, :, None, :], sin[None, :, None, :]
    rot = jnp.concatenate([x1 * c - x2 * s, x2 * c + x1 * s], axis=-1)
    return jnp.concatenate([rot.astype(x.dtype), x[..., 2 * half:]], axis=-1)

def dsa_attention(q, k, v, qi, ki, wi, chunk_ids, topk):
    B, T, H, d = q.shape
    G = k.shape[2]
    R = H // G
    nb = T // Q_BLOCK
    scale = d ** -0.5
    ki32 = ki.astype(jnp.float32)

    def block(i):
        s0 = i * Q_BLOCK
        qb = lax.dynamic_slice_in_dim(q, s0, Q_BLOCK, axis=1)
        qib = lax.dynamic_slice_in_dim(qi, s0, Q_BLOCK, axis=1).astype(jnp.float32)
        wib = lax.dynamic_slice_in_dim(wi, s0, Q_BLOCK, axis=1).astype(jnp.float32)
        cq = lax.dynamic_slice_in_dim(chunk_ids, s0, Q_BLOCK)
        admissible = chunk_ids[None, :] <= cq[:, None]
        idx_logits = jnp.einsum('bqhd,bsd->bqhs', qib, ki32)
        score = jnp.einsum('bqhs,bqh->bqs', jax.nn.relu(idx_logits), wib)
        score = jnp.where(admissible[None], score, -jnp.inf)
        _, sel = lax.top_k(score, topk)
        valid = chunk_ids[sel] <= cq[None, :, None]
        k_sel = jax.vmap(lambda kk, ii: kk[ii])(k, sel)
        v_sel = jax.vmap(lambda vv, ii: vv[ii])(v, sel)
        qg = qb.reshape(B, Q_BLOCK, G, R, d)
        logits = jnp.einsum('bqgrd,bqkgd->bqgrk', qg, k_sel).astype(jnp.float32) * scale
        logits = jnp.where(valid[:, :, None, None, :], logits, -jnp.inf)
        p = jax.nn.softmax(logits, axis=-1).astype(v.dtype)
        o = jnp.einsum('bqgrk,bqkgd->bqgrd', p, v_sel)
        return o.reshape(B, Q_BLOCK, H, d)

    o = lax.map(block, jnp.arange(nb))
    return o.transpose(1, 0, 2, 3, 4).reshape(B, T, H, d)

def hgrn2_chunkwise(q, k, v, log_f):
    B, T, H, dk = q.shape
    dv = v.shape[-1]
    n = T // CHUNK

    def to_chunks(a):
        return a.reshape(B, n, CHUNK, H, a.shape[-1]).transpose(1, 0, 2, 3, 4)

    causal = jnp.tril(jnp.ones((CHUNK, CHUNK), dtype=bool))[None, :, :, None, None]

    def step(S, inp):
        q_, k_, v_, g_ = inp
        b = jnp.cumsum(g_, axis=1)
        diff = b[:, :, None] - b[:, None, :]
        decay = jnp.exp(jnp.where(causal, diff, -jnp.inf))
        attn = jnp.einsum('bthd,bshd,btshd->bhts', q_, k_, decay)
        o_intra = jnp.einsum('bhts,bshv->bthv', attn, v_)
        o_inter = jnp.einsum('bthd,bhdv->bthv', q_ * jnp.exp(b), S)
        b_last = b[:, -1]
        k_dec = k_ * jnp.exp(b_last[:, None] - b)
        S_new = jnp.exp(b_last)[..., None] * S + jnp.einsum('bshd,bshv->bhdv', k_dec, v_)
        return S_new, o_intra + o_inter

    S0 = jnp.zeros((B, H, dk, dv), jnp.float32)
    _, o = lax.scan(step, S0, (to_chunks(q), to_chunks(k), to_chunks(v), to_chunks(log_f)))
    return o.transpose(1, 0, 2, 3, 4).reshape(B, T, H, dv)

def hybrid_layer(x, lb, norm_g, w_in, q_norm_g, k_norm_g, idx_k_norm_g, hgrn_out_norm_g,
                 w_branch, w_out, rope_a, rope_i, chunk_ids, topk):
    B, T, D = x.shape
    h = rms_norm(x, norm_g)
    proj = h @ w_in
    cuts = np.cumsum(SPLIT_SIZES)[:-1].tolist()
    (q_a, k_a, v_a, z_a, q_i, k_i, w_i,
     q_b, f_b, i_b, z_b, gates) = jnp.split(proj, cuts, axis=-1)

    q = apply_partial_rope(rms_norm(q_a.reshape(B, T, H_A, HD_A), q_norm_g), *rope_a)
    k = apply_partial_rope(rms_norm(k_a.reshape(B, T, KV_A, HD_A), k_norm_g), *rope_a)
    v = v_a.reshape(B, T, KV_A, HD_A)
    qi = apply_partial_rope(q_i.reshape(B, T, H_IDX, D_IDX), *rope_i)
    ki = apply_partial_rope(rms_norm(k_i, idx_k_norm_g)[:, :, None, :], *rope_i)[:, :, 0, :]
    wi = w_i * (H_IDX ** -0.5 * D_IDX ** -0.5)
    o_a = dsa_attention(q, k, v, qi, ki, wi, chunk_ids, topk)
    y_a = o_a.reshape(B, T, BRANCH_WIDTH) * jax.nn.silu(z_a)

    qb = jax.nn.silu(q_b.astype(jnp.float32)).reshape(B, T, H_B, DK_B)
    lbh = lb.reshape(H_B, DK_B)
    f = lbh + (1.0 - lbh) * jax.nn.sigmoid(f_b.astype(jnp.float32).reshape(B, T, H_B, DK_B))
    vb = i_b.astype(jnp.float32).reshape(B, T, H_B, DV_B)
    o_b = hgrn2_chunkwise(qb, 1.0 - f, vb, jnp.log(f)).astype(x.dtype)
    o_b = rms_norm(o_b, hgrn_out_norm_g)
    y_b = o_b.reshape(B, T, BRANCH_WIDTH) * jax.nn.silu(z_b)

    y = jnp.stack([y_a, y_b], axis=2)
    p = jnp.einsum('btnc,ncd->btnd', y, w_branch)
    g = jax.nn.sigmoid(gates.reshape(B, T, N_BRANCH, D))
    merged = jnp.sum(g * p, axis=2)
    return x + merged @ w_out

def second_inputs(seed: int = 0) -> dict:
    key = jax.random.key(seed)
    ks = jax.random.split(key, 12)
    f32 = jnp.float32
    D = D_MODEL
    return {
        "x": jax.random.normal(ks[0], (BATCH, SEQ, D), f32),
        "meta_tokens": jax.random.normal(ks[1], (N_META, D), f32),
        "hgrn_lb_logits": 0.1 * jax.random.normal(ks[2], (DEPTH + 1, H_B * DK_B), f32),
        "norm_g": 1.0 + 0.02 * jax.random.normal(ks[3], (DEPTH, D), f32),
        "w_in": jax.random.normal(ks[4], (DEPTH, D, N_IN), f32) * D ** -0.5,
        "q_norm_g": 1.0 + 0.02 * jax.random.normal(ks[5], (DEPTH, HD_A), f32),
        "k_norm_g": 1.0 + 0.02 * jax.random.normal(ks[6], (DEPTH, HD_A), f32),
        "idx_k_norm_g": 1.0 + 0.02 * jax.random.normal(ks[7], (DEPTH, D_IDX), f32),
        "hgrn_out_norm_g": 1.0 + 0.02 * jax.random.normal(ks[8], (DEPTH, DV_B), f32),
        "w_branch": jax.random.normal(ks[9], (DEPTH, N_BRANCH, BRANCH_WIDTH, D), f32) * BRANCH_WIDTH ** -0.5,
        "w_out": jax.random.normal(ks[10], (DEPTH, D, D), f32) * D ** -0.5,
    }

def second_block(x, meta_tokens, hgrn_lb_logits, norm_g, w_in, q_norm_g, k_norm_g, idx_k_norm_g,
              hgrn_out_norm_g, w_branch, w_out):
    B, S, D = x.shape
    T = S + N_META
    Tp = -(-T // Q_BLOCK) * Q_BLOCK
    meta = jnp.broadcast_to(meta_tokens.astype(x.dtype)[None], (B, N_META, D))
    h = jnp.concatenate([meta, x, jnp.zeros((B, Tp - T, D), x.dtype)], axis=1)

    pos = jnp.arange(Tp, dtype=jnp.int32)
    chunk_ids = jnp.where(pos < N_META, 0, 1 + (pos - N_META) // CHUNK).astype(jnp.int32)
    rope_a = rope_tables(pos, ROT_A)
    rope_i = rope_tables(pos, ROT_IDX)
    topk = min(TOPK_MAX, S // 4)

    lb_all = jnp.cumsum(jax.nn.softmax(hgrn_lb_logits.astype(jnp.float32), axis=0), axis=0)

    for l in range(DEPTH):
        h = hybrid_layer(h, lb_all[l], norm_g[l], w_in[l], q_norm_g[l], k_norm_g[l],
                         idx_k_norm_g[l], hgrn_out_norm_g[l], w_branch[l], w_out[l],
                         rope_a, rope_i, chunk_ids, topk)
    return h[:, N_META:N_META + S]


def setup_inputs(seed=0):
    out = dict(first_inputs(seed))
    for name, value in second_inputs(seed + 1).items():
        if name != "x":
            out[name + "_2"] = value
    return out


def reference(
    x, positions, pre_norm_g, w_in, q_a_norm_g, w_q_b, kv_a_norm_g, w_kv_b, conv_w, w_o_mla,
    w_o_conv, w_out, post_norm_g, meta_tokens_2, hgrn_lb_logits_2, norm_g_2, w_in_2, q_norm_g_2,
    k_norm_g_2, idx_k_norm_g_2, hgrn_out_norm_g_2, w_branch_2, w_out_2,
):
    x = first_block(
        x, positions, pre_norm_g, w_in, q_a_norm_g, w_q_b, kv_a_norm_g, w_kv_b, conv_w, w_o_mla,
        w_o_conv, w_out, post_norm_g,
    )
    return second_block(
        x, meta_tokens_2, hgrn_lb_logits_2, norm_g_2, w_in_2, q_norm_g_2, k_norm_g_2,
        idx_k_norm_g_2, hgrn_out_norm_g_2, w_branch_2, w_out_2,
    )


_drawn_inputs = setup_inputs


def setup_inputs(seed=0):
    import zlib

    import numpy as np

    out = dict(_drawn_inputs(seed))
    spreads = {}
    factors = {'q_a_norm_g': 8.0,
     'kv_a_norm_g': 8.0,
     'post_norm_g': 3.682,
     'hgrn_lb_logits_2': 8.0,
     'norm_g_2': 5.945,
     'q_norm_g_2': 8.0,
     'k_norm_g_2': 8.0,
     'idx_k_norm_g_2': 8.0,
     'hgrn_out_norm_g_2': 8.0}
    for name, (base, spread) in spreads.items():
        noise = np.random.default_rng([zlib.crc32(name.encode()), seed]).standard_normal(out[name].shape)
        drawn = base * np.exp(spread * noise) if base else spread * noise
        out[name] = __import__('jax').numpy.asarray(drawn.astype(out[name].dtype))
    for name, factor in factors.items():
        out[name] = (out[name] * factor).astype(out[name].dtype)
    return out
```

```python
from collections import deque
from contextlib import ExitStack

import numpy as np

import concourse.bass as bass
from concourse import mybir

F32 = mybir.dt.float32
F32R = mybir.dt.float32r
I32 = mybir.dt.int32
U8 = mybir.dt.uint8
ALU = mybir.AluOpType
ACT = mybir.ActivationFunctionType
AX = mybir.AxisListType.X

P = 128
D = 2048
KT = D // P
S = 256
NMETA = 16
T = S + NMETA
EPS = 1e-6
NEG = -1e30

H1, DN, RD, DV, LORA = 16, 128, 64, 128, 512
C_QA, C_KV, C_KR = 0, LORA, 2 * LORA
C_ZMLA = 2 * LORA + RD
C_CIN, C_B, C_C, C_ZCONV, C_GMLA, C_GCONV = (C_ZMLA + D * i for i in range(1, 7))
SCALE1 = 1.0 / float(np.sqrt(DN + RD))

BW = D // 2
HA, KVA, HI, DI, HB = 8, 4, 16, 64, 8
CHUNK, TOPK = 64, 64
C2_QA, C2_KA, C2_VA, C2_ZA, C2_QI = 0, 1024, 1536, 2048, 3072
C2_KI, C2_WI, C2_QB, C2_FB, C2_IB, C2_ZB, C2_G = 4096, 4160, 4176, 5200, 6224, 7248, 8272
SCALE2 = float(P) ** -0.5
W_SCALE = HI ** -0.5 * DI ** -0.5
MASKED, TAKEN = -3.0e38, -3.3e38

UNIT = 1024
N_RAW, N_SPLIT, LEAD = 4, 3, 2

CONSTS = {}


def _constants():
    p = np.arange(P)
    parts, at = [], 0

    def put(name, a):
        nonlocal at
        a = np.asarray(a, np.float32).reshape(P, -1)
        CONSTS[name] = (at, at + a.shape[1])
        parts.append(a)
        at += a.shape[1]

    def rotation(group, half, copies):
        r = np.zeros((P, P))
        for m in range(P):
            o = m % group
            base = m - o if copies == 1 else 0
            if o < half:
                r[base + o + half, m] = -1.0
            elif o < 2 * half:
                r[base + o - half, m] = 1.0
        return r

    put("ident", np.eye(P))
    put("ones", np.ones((P, P)))
    put("rot_q1", rotation(RD, RD // 2, 1))
    put("dup64", p[:, None] == p[None, :] % 64)
    put("rot_k1", rotation(RD, RD // 2, 2))
    causal = np.where(p[None, :] <= p[:, None], 0.0, NEG)
    put("mask1", np.concatenate([np.zeros((P, P)), causal], 1))
    inv = 10000.0 ** (-(np.arange(RD // 2) * 2) / RD)
    put("inv_freq", inv.astype(np.float32)[p % 32])
    put("neg_half", np.full((P, 1), -0.5))
    put("pad", np.zeros((P, 2)))
    CONSTS["resident"] = (0, at)

    put("rot_a", rotation(P, 16, 1))
    put("rot_i", rotation(DI, 8, 2))
    put("rot_i1", rotation(DI, 8, 1))
    pos = np.arange(T, dtype=np.float32)

    def rope(group, half):
        o = p % group
        iv = np.power(np.float64(500000.0), -(o % half) * 2.0 / (2 * half)).astype(np.float32)
        ang = (pos[None, :] * iv[:, None]).astype(np.float32).astype(np.float64)
        on = (o < 2 * half)[:, None]
        return np.where(on, np.cos(ang), 1.0), np.where(on, np.sin(ang), 0.0)

    for name, (c, s) in (("a", rope(P, 16)), ("i", rope(DI, 8))):
        put("cos_" + name, c)
        put("sin_" + name, s)
    CONSTS["late"] = (CONSTS["resident"][1], at)
    f = np.concatenate(parts, 1)

    s, t = p[:, None], p[None, :]
    lv = [((s // (2 * h) == t // (2 * h)) & (s % (2 * h) < h) & (t % (2 * h) >= h)) for h in LEVELS]
    return np.ascontiguousarray(f), np.ascontiguousarray(np.concatenate(lv, 1).astype(np.float32))


LEVELS = (1, 2, 4, 8, 16, 32, 64)
CONST_F, CONST_LVL = _constants()

ROWS = {}
_at = 0
for _name, _n in (("pre", 16), ("post", 16), ("norm2", 16), ("conv", 48), ("qa", 4), ("kva", 4),
                  ("lb", 16), ("qn", 1), ("kn", 1), ("on", 1), ("ikn", 1)):
    ROWS[_name] = _at
    _at += _n
N_ROWS = _at


class Queue:

    def __init__(self, eng, sem):
        self.eng, self.sem, self.count, self.seen = eng, sem, 0, {}

    def wait(self, marks):
        for m in marks:
            if m is not None:
                sem, value = m
                if self.seen.get(sem.name, 0) < value:
                    self.eng.wait_ge(sem, value)
                    self.seen[sem.name] = value

    def mark(self, inst):
        inst.then_inc(self.sem, 1)
        self.count += 1
        return (self.sem, self.count)


class Slot:

    def __init__(self, ap):
        self.ap, self.free = ap, []


class Ring:
    def __init__(self, aps):
        self.slots, self.i = [Slot(a) for a in aps], 0

    def next(self):
        s = self.slots[self.i % len(self.slots)]
        self.i += 1
        return s


class Phase:

    def __init__(self, weight, groups, ktiles, hi, lo, n, evac, ready=(), period=1):
        self.order = lambda w, n: [(w, lambda x: x)]
        self.weight, self.groups, self.ktiles = weight, groups, ktiles
        self.hi, self.lo, self.n = hi, lo, n
        self.evac, self.ready, self.period = evac, ready, period


class Unit:
    def __init__(self, phase, g, k0, nk):
        self.phase, self.g, self.k0, self.nk = phase, g, k0, nk
        self.last = k0 + nk == phase.ktiles


def build(nc, a, out, taps=None):
    ctx = ExitStack()
    with ctx:
        def sb(name, shape, dt=F32):
            return ctx.enter_context(nc.sbuf_tensor(name, shape, dt))

        def sem(name):
            return ctx.enter_context(nc.semaphore(name))

        PE = Queue(nc.tensor, sem("pe_done"))
        SC = Queue(nc.scalar, sem("act_done"))
        VE = Queue(nc.vector, sem("dve_done"))
        GP = Queue(nc.gpsimd, sem("pool_done"))
        SP = Queue(nc.sync, None)

        def act(waits, *args, **kw):
            SC.wait(waits)
            return SC.mark(nc.scalar.activation(*args, **kw))

        def dve(waits, op, *args, **kw):
            VE.wait(waits)
            return VE.mark(op(*args, **kw))

        def pool(waits, op, *args, **kw):
            GP.wait(waits)
            return GP.mark(op(*args, **kw))

        v, gp = nc.vector, nc.gpsimd

        def pe_t(waits, dst, src, ident):
            PE.wait(waits)
            return nc.tensor.transpose(dst, src, ident)

        def mm(dst, lhsT, rhs, start=True, stop=True):
            return nc.tensor.matmul(dst, lhsT, rhs, start=start, stop=stop, skip_group_check=True)

        loads = [0]

        def load(dst, src, waits=(), q=None):
            q = q or SP
            q.wait(waits)
            loads[0] += 1
            s = sem(f"load{loads[0]}")
            q.eng.dma_start(dst, src).then_inc(s, 16)
            return (s, 16)

        raw = sb("w_raw", [P, N_RAW, UNIT])
        whi = sb("w_hi", [P, N_SPLIT, UNIT], F32R)
        wlo = sb("w_lo", [P, N_SPLIT, UNIT], F32R)
        hb_hi = sb("hb_hi", [P, KT, S], F32R)
        hb_lo = sb("hb_lo", [P, KT, S], F32R)
        ob_hi = sb("ob_hi", [P, KT, T], F32R)
        ob_lo = sb("ob_lo", [P, KT, T], F32R)
        arena = sb("arena", [P, 72 * 256])
        con = sb("con", [P, CONSTS["resident"][1]])
        cols = sb("cols", [P, P])
        rope1 = sb("rope1", [P, 2, S])
        factor = sb("factor", [P, 3, T])
        small = sb("small", [P, 256])
        scratch = Ring([sb(f"scratch{i}", [P, T])[:, :] for i in range(5)])
        head_factors = Ring([sb(f"head_factor{i}", [P, T])[:, :] for i in range(2)])
        acc_a, acc_b = sb("acc_a", [P, S])[:, :], sb("acc_b", [P, S])[:, :]
        psum = [ctx.enter_context(nc.psum_tensor(f"bank{i}", [P, 512], F32)) for i in range(8)]
        proj_banks = Ring([b[:, :] for b in psum[:5]])
        side_banks = Ring([b[:, :] for b in psum[5:]])

        def region(kb0, kb, *shape):
            n = int(np.prod(shape))
            assert n <= 256 * kb
            at = int(kb0 * 256)
            ap = arena[:, at:at + n]
            if len(shape) == 1:
                return ap
            if len(shape) == 2:
                return ap.rearrange("p (a b) -> p a b", a=shape[0])
            return ap.rearrange("p (a b c) -> p a b c", a=shape[0], b=shape[1])

        def c(name):
            lo, hi = CONSTS[name]
            return con[:, lo:hi]

        def col(name, i=0):
            j = ROWS[name] + i
            return cols[:, j:j + 1]

        def tap(name, ap, waits):
            if taps is not None and name in taps:
                d = nc.dram_tensor("tap_" + name, [ap.shape[0], int(np.prod(ap.shape[1:]))], F32, kind="ExternalOutput").ap()
                allm = [(q.sem, q.count) for q in (PE, SC, VE, GP) if q.count]
                t = load(d, ap.rearrange("p a b -> p (a b)") if len(ap.shape) == 3 else ap, allm)
                for q in (SP, PE, SC, VE, GP):
                    q.wait([t])

        units = []
        raw_sem = [sem(f"raw{i}") for i in range(N_RAW)]
        raw_free = [None] * N_RAW
        split_free = [None] * N_SPLIT
        split_done = {}
        landed = {}
        issued = [0, 0]

        def plan(phase):
            phase.first = len(units)
            for g, (c0, nc_, tiles) in enumerate(phase.groups):
                step = min(UNIT // nc_, phase.ktiles)
                for k0 in range(0, phase.ktiles, step):
                    units.append(Unit(phase, g, k0, step))
            phase.end = len(units)
            return phase

        def size(u):
            c0, n, _ = u.phase.groups[u.g]
            return c0, n, u.nk * n

        def issue_load():
            i = issued[0]
            if i >= len(units):
                return
            issued[0] += 1
            u, s = units[i], i % N_RAW
            c0, n, sz = size(u)
            SP.wait([raw_free[s]])
            src = u.phase.weight.rearrange("(k p) n -> p k n", p=P)[:, u.k0:u.k0 + u.nk, c0:c0 + n]
            dst = raw[:, s, 0:sz].rearrange("p (k n) -> p k n", k=u.nk)
            nc.sync.dma_start(dst, src).then_inc(raw_sem[s], 16)
            landed[i] = (raw_sem[s], 16 * (i // N_RAW + 1))

        def issue_split():
            i = issued[1]
            if i >= len(units):
                return
            issued[1] += 1
            s, r = i % N_SPLIT, i % N_RAW
            _, _, sz = size(units[i])
            for src, dst in units[i].phase.order(raw[:, r, 0:sz], sz):
                hi = act([landed[i], split_free[s]], dst(whi[:, s, 0:sz]), src, ACT.Copy)
                lo = dve([hi, split_free[s]], v.tensor_tensor, dst(wlo[:, s, 0:sz]), src,
                         dst(whi[:, s, 0:sz]).bitcast(F32), ALU.subtract)
            raw_free[r] = lo
            split_done[i] = [hi, lo]
            issue_load()

        pending, active = deque(), []
        seq = {"width": 3}

        def pump():
            for job in list(active):
                if next(job, "end") == "end":
                    active.remove(job)
            if pending and len(active) < seq["width"]:
                job = pending.popleft()
                active.append(job)
                if next(job, "end") == "end":
                    active.remove(job)

        def drain_jobs():
            while pending or active:
                pump()

        def run(phase):
            banks = {}
            for i in range(phase.first, phase.end):
                while issued[1] <= min(i + LEAD, len(units) - 1):
                    issue_split()
                u, s = units[i], i % N_SPLIT
                c0, n, sz = size(u)
                tiles = phase.groups[u.g][2]
                hi_w = whi[:, s, 0:sz].rearrange("p (k n) -> p k n", k=u.nk)
                lo_w = wlo[:, s, 0:sz].rearrange("p (k n) -> p k n", k=u.nk)
                PE.wait(split_done.pop(i))
                for m, tile in enumerate(tiles):
                    if u.k0 == 0:
                        banks[m] = proj_banks.next()
                        PE.wait(banks[m].free)
                    dst = banks[m].ap[:, 0:phase.n]
                    for k in range(u.nk):
                        kt = u.k0 + k
                        PE.wait(phase.ready(kt) if callable(phase.ready) else phase.ready)
                        x_hi, x_lo = phase.hi(kt), phase.lo(kt)
                        first, last = kt == 0, kt == phase.ktiles - 1
                        mm(dst, tile(hi_w[:, k, :]), x_hi, first, False)
                        mm(dst, tile(hi_w[:, k, :]), x_lo, False, False)
                        inst = mm(dst, tile(lo_w[:, k, :]), x_hi, False, last)
                    if u.last or m == len(tiles) - 1:
                        done = PE.mark(inst)
                    if u.last:
                        banks[m].free = phase.evac(u.g, m, dst, done)
                split_free[s] = done
                if (i - phase.first) % phase.period == phase.period - 1:
                    pump()

        def plain(c0, groups, cols_=512):
            tiles = [(lambda w, m=m: w[:, m * P:(m + 1) * P]) for m in range(cols_ // P)]
            return [(c0 + g * cols_, cols_, tiles) for g in range(groups)]

        def factor_of(slot, span, acc, acc_done, n, slot_free):
            lo, hi = span
            b = side_banks.next()
            PE.wait(b.free + [acc_done])
            t = PE.mark(mm(b.ap[:, 0:hi - lo], c("ones"), acc))
            dst = factor[:, slot, lo:hi]
            t = dve([t] + slot_free, v.tensor_scalar, dst, b.ap[:, 0:hi - lo], 1.0 / n, EPS, ALU.mult, ALU.add)
            b.free = [t]
            return pool([t], gp.tensor_tensor, dst, dst, c("neg_half").to_broadcast([P, hi - lo]), ALU.pow)

        def head_factor(x, x_done, n, width, rows=P):
            sq, f = scratch.next(), head_factors.next()
            t = pool(sq.free + [x_done], gp.tensor_tensor, sq.ap[0:rows, 0:width], x, x, ALU.mult)
            b = side_banks.next()
            PE.wait(b.free + [t])
            t = PE.mark(mm(b.ap[:, 0:width], c("ones")[0:rows, :], sq.ap[0:rows, 0:width]))
            sq.free = [t]
            t = dve([t] + f.free, v.tensor_scalar, f.ap[:, 0:width], b.ap[:, 0:width], 1.0 / n, EPS, ALU.mult, ALU.add)
            b.free = [t]
            t = pool([t], gp.tensor_tensor, f.ap[:, 0:width], f.ap[:, 0:width],
                     c("neg_half").to_broadcast([P, width]), ALU.pow)
            return f, t

        def split_to(dst_hi, dst_lo, src, src_done, free, gain=None):
            if gain is None:
                hi = act(free + [src_done], dst_hi, src, ACT.Copy)
                lo = dve([hi, src_done], v.tensor_tensor, dst_lo, src, dst_hi.bitcast(F32), ALU.subtract)
            else:
                hi = act(free + [src_done], dst_hi, src, ACT.Copy, scale=gain)
                lo = dve([hi, src_done], v.scalar_tensor_tensor, dst_lo, src, gain, dst_hi.bitcast(F32),
                         ALU.mult, ALU.subtract)
            return [hi, lo]

        def sum_squares(acc, tiles, marks, waits=()):
            t = pool([marks[0], *waits], gp.tensor_tensor, acc, tiles[0], tiles[0], ALU.mult)
            for x, m in list(zip(tiles, marks))[1:]:
                sq = scratch.next()
                w = acc.shape[1]
                t1 = pool(sq.free + [m], gp.tensor_tensor, sq.ap[:, 0:w], x, x, ALU.mult)
                t = pool([t1, t], gp.tensor_tensor, acc, acc, sq.ap[:, 0:w], ALU.add)
                sq.free = [t]
            return t

        Q1, QR, K1, V1, G1 = (region(0, 16, H1, S), region(16, 8, H1 // 2, S), region(24, 16, H1, S),
                              region(40, 16, 2, D), region(56, 16, KT, S))
        OUT1 = region(40, 16, KT, S)
        GM = K1
        x_in = region(0, 16, 2, D)
        x_meta = region(16, 8, D)
        xT = G1
        XR = region(24, 16, KT, S)
        kr1 = sb("kr1", [P, S])
        prob = Ring([sb(f"prob{i}", [P, 416])[:, :] for i in range(2)])
        probT = Ring([sb(f"probT{i}", [P, 640])[:, :] for i in range(2)])

        hb = (lambda k: hb_hi[:, k, :], lambda k: hb_lo[:, k, :])
        ob = (lambda k: ob_hi[:, k, 0:S], lambda k: ob_lo[:, k, 0:S])
        ob_kv = (lambda k: ob_hi[:, k + 4, 0:S], lambda k: ob_lo[:, k + 4, 0:S])
        ob_main = (lambda k: ob_hi[:, k, NMETA:T], lambda k: ob_lo[:, k, NMETA:T])
        ob_all = (lambda k: ob_hi[:, k, :], lambda k: ob_lo[:, k, :])
        hb_b = (lambda k: hb_hi[:, k + 8, :], lambda k: hb_lo[:, k + 8, :])
        w1, w2 = a["w_in"], a["w_in_2"][0]
        HD = DN + RD

        def pair_order(w, n):
            view = w.rearrange("p (k h x) -> p k h x", h=2, x=HD)
            out_ = []
            for lo, hi, at in ((0, DN, 0), (DN, HD, 2 * DN)):
                out_.append((view[:, :, :, lo:hi],
                             lambda x, lo=lo, hi=hi, at=at: x.rearrange("p (k y) -> p k y", y=2 * HD)
                             [:, :, at:at + 2 * (hi - lo)].rearrange("p k (h x) -> p k h x", h=2)))
            return out_

        pair = plain(0, 1, 384)[0][2]
        one = [lambda w: w[:, 0:P]]

        evac = {}

        def ph(name, *args, **kw):
            p_ = Phase(*args, evac=lambda *e: evac[name](*e), **kw)
            return plan(p_)

        p_qa = ph("qa", w1, plain(C_QA, 1), KT, *hb, S)
        p_kv = ph("kva", w1, plain(C_KV, 1), KT, *hb, S)
        p_kr = ph("kr", w1, [(C_KR, P, one)], KT, *hb, S)
        p_q = ph("q", a["w_q_b"], [(g * 384, 384, pair) for g in range(8)], 4, *ob, S)
        p_q.order = pair_order
        p_k = ph("kv", a["w_kv_b"], plain(0, 8), 4, *ob_kv, S)
        p_conv = []
        for j in range(4):
            for name, c0 in (("cin", C_CIN), ("cgate", C_C), ("bgate", C_B), ("zconv", C_ZCONV)):
                p_conv.append((j, ph(f"{name}{j}", w1, plain(c0 + 512 * j, 1), KT, *hb, S, period=2)))
        p_gc = ph("gconv", w1, plain(C_GCONV, 4), KT, *hb, S)
        p_oc = ph("oconv", a["w_o_conv"], plain(0, 4), KT, *ob, S)
        p_zm = ph("zmla", w1, plain(C_ZMLA, 4), KT, *hb, S)
        p_gm = ph("gmla", w1, plain(C_GMLA, 4), KT, *hb, S)
        p_om = ph("omla", a["w_o_mla"], plain(0, 4), KT, *ob, S)
        p_w = ph("wout", a["w_out"], plain(0, 4), KT, *hb, S)
        p2_ki = ph("ki", w2, [(C2_KI, P, one)], KT, *ob_all, T)
        p2_qi = ph("qi", w2, plain(C2_QI, 2), KT, *ob_main, S)
        p2_ka = ph("ka", w2, plain(C2_KA, 1), KT, *ob_all, T)
        p2_va = ph("va", w2, plain(C2_VA, 1), KT, *ob_all, T)
        p2_qa = ph("qa2", w2, plain(C2_QA, 2), KT, *ob_main, S)
        p2_fb = ph("fb", w2, plain(C2_FB, 2), KT, *ob_all, T, period=2)
        p2_ib = ph("ib", w2, plain(C2_IB, 2), KT, *ob_all, T, period=2)
        p2_qb = ph("qb", w2, plain(C2_QB, 2), KT, *ob_main, S, period=2)
        p2_ga = ph("ga", w2, plain(C2_G, 4), KT, *ob_main, S)
        p2_za = ph("za", w2, plain(C2_ZA, 2), KT, *ob_main, S)
        p2_ba = ph("ba", a["w_branch_2"][0, 0], plain(0, 4), 8, *hb, S)
        p2_zb = ph("zb", w2, plain(C2_ZB, 2), KT, *ob_main, S)
        p2_gb = ph("gb", w2, plain(C2_G + D, 4), KT, *ob_main, S)
        p2_bb = ph("bb", a["w_branch_2"][0, 1], plain(0, 4), 8, *hb_b, S)
        p2_w = ph("wout2", a["w_out_2"][0], plain(0, 4), KT, *ob, S)

        x_load = [load(x_in[:, b, :], a["x"][0, b * P:(b + 1) * P, :], q=SC) for b in range(2)]
        con_load = load(con[:, :], a["const_f"][:, 0:CONSTS["resident"][1]])
        rows_in = region(24, 1, P)
        row_loads = []

        def rows_of(name, src, n):
            r = ROWS[name]
            row_loads.append(load(rows_in[r:r + n, 0:src.shape[1]], src, [rows_zero]))

        rows_zero = dve([], v.memset, rows_in, 0.0)
        r128 = lambda ap: ap.rearrange("(k p) -> k p", p=P)
        rows_of("pre", r128(a["pre_norm_g"]), 16)
        for _ in range(N_RAW):
            issue_load()
        rows_of("post", r128(a["post_norm_g"]), 16)
        rows_of("norm2", r128(a["norm_g_2"][0]), 16)
        rows_of("conv", a["conv_w"].rearrange("c (k p) -> (c k) p", p=P), 48)
        rows_of("qa", r128(a["q_a_norm_g"]), 4)
        rows_of("kva", r128(a["kv_a_norm_g"]), 4)
        rows_of("lb", a["hgrn_lb_logits_2"].rearrange("l (k p) -> (l k) p", p=P), 16)
        rows_of("qn", a["q_norm_g_2"], 1)
        rows_of("kn", a["k_norm_g_2"], 1)
        rows_of("on", a["hgrn_out_norm_g_2"], 1)
        rows_of("ikn", a["idx_k_norm_g_2"], 1)
        pos_i = region(25, 1, S)[0:1, :].bitcast(I32)
        pos_load = load(pos_i, a["positions"])
        meta_load = load(x_meta[0:NMETA, :], a["meta_tokens_2"])

        b = side_banks.next()
        PE.wait([con_load, rows_zero, *row_loads])
        t = PE.mark(nc.tensor.transpose(b.ap[:, 0:P], rows_in, c("ident")))
        cols_done = dve([t], v.tensor_copy, cols[:, :], b.ap[:, 0:P])
        b.free = [cols_done]

        x_marks, h_marks = [], []
        for k in range(KT):
            b = proj_banks.next()
            PE.wait([con_load, *x_load, *b.free])
            for blk in range(2):
                t = nc.tensor.transpose(b.ap[:, blk * P:(blk + 1) * P], x_in[:, blk, k * P:(k + 1) * P], c("ident"))
            t = PE.mark(t)
            x_marks.append(act([t], xT[:, k, :], b.ap[:, 0:S], ACT.Copy))
            b.free = [x_marks[-1]]
            h_marks.append(split_to(hb_hi[:, k, :], hb_lo[:, k, :], xT[:, k, :], x_marks[-1], [cols_done],
                                    gain=col("pre", k)))
        x_in_free = t
        x_sq = t = sum_squares(acc_b, [xT[:, k, :] for k in range(KT)], x_marks)
        h_ready = lambda kt: h_marks[kt]

        pos_f = small[0:1, 0:S]
        tp = dve([pos_load], v.tensor_copy, pos_f, pos_i)
        bp = side_banks.next()
        PE.wait([tp, con_load, *bp.free])
        tp = PE.mark(mm(bp.ap[:, 0:S], c("ones")[0:1, :], pos_f))
        ang, turns = scratch.next(), scratch.next()
        ta = dve([tp] + ang.free, v.tensor_scalar, ang.ap[:, 0:S], bp.ap[:, 0:S], c("inv_freq"), None, ALU.mult)
        bp.free = [ta]
        MAGIC = 1.5 * 2.0 ** 23
        rope_done = []
        for which, shift in ((1, 0.0), (0, 0.25)):
            dst = rope1[:, which, :]
            k_ = turns.ap[:, 0:S]
            tk = dve([ta] + rope_done + turns.free, v.tensor_scalar, k_, ang.ap[:, 0:S], 1.0 / (2 * np.pi), shift, ALU.mult, ALU.add)
            tk = dve([tk], v.tensor_scalar, k_, k_, MAGIC, MAGIC, ALU.add, ALU.subtract)
            tk = dve([tk], v.scalar_tensor_tensor, dst, k_, -6.28125, ang.ap[:, 0:S], ALU.mult, ALU.add)
            tk = dve([tk], v.scalar_tensor_tensor, dst, k_, -0.0019350051879882812, dst, ALU.mult, ALU.add)
            tk = dve([tk], v.scalar_tensor_tensor, dst, k_, -3.0199159819e-07, dst, ALU.mult, ALU.add)
            if shift:
                tk = dve([tk], v.tensor_scalar, dst, dst, np.pi / 2, None, ALU.add)
            tk = dve([tk], v.tensor_scalar, dst, dst, 3.14159250, -3.14159250, ALU.min, ALU.max)
            rope_done = [act([tk], dst, dst, ACT.Sin)]
        ang.free = turns.free = rope_done
        cos1, sin1 = rope1[:, 0, :], rope1[:, 1, :]
        tap("rope1", rope1[:, :, :], rope_done)

        small2, small3 = sb("small2", [P, 64]), sb("small3", [P, 2 * HI])
        lbx, lb, oml = small2[:, 16:32], small2[:, 0:8], small2[:, 8:16]
        l0, l1 = cols[:, ROWS["lb"]:ROWS["lb"] + 8], cols[:, ROWS["lb"] + 8:ROWS["lb"] + 16]
        mx = small2[:, 32:40]
        tl = dve([cols_done], v.tensor_tensor, mx, l0, l1, ALU.max)
        tl = dve([tl], v.tensor_tensor, lbx[:, 0:8], l0, mx, ALU.subtract)
        tl = dve([tl], v.tensor_tensor, lbx[:, 8:16], l1, mx, ALU.subtract)
        tl = act([tl], lbx, lbx, ACT.Exp)
        tl = dve([tl], v.tensor_tensor, mx, lbx[:, 0:8], lbx[:, 8:16], ALU.add)
        tl = dve([tl], v.reciprocal, mx, mx)
        tl1 = dve([tl], v.tensor_tensor, lb, lbx[:, 0:8], mx, ALU.mult)
        lb_done = dve([tl1], v.tensor_tensor, oml, lbx[:, 8:16], mx, ALU.mult)

        R_, RR, RQ = factor[:, 0, 0:S], factor[:, 1, 0:S], factor[:, 2, 0:S]
        r1_done = factor_of(0, (0, S), acc_b, t, D, [])
        RKV = RR

        lat_marks = {}
        lat_sq = {}
        rq_done, rkv_done = [], []

        def latent(which, base, gname, done_list, dst_factor):
            def f(g, m, ps, done):
                s = scratch.next()
                t = dve([done, r1_done] + s.free, v.tensor_tensor, s.ap[:, 0:S], ps, R_, ALU.mult)
                s2 = split_to(ob_hi[:, base + m, 0:S], ob_lo[:, base + m, 0:S], s.ap[:, 0:S], t, [], gain=col(gname, m))
                lat_marks[which, m] = s2
                if m == 0:
                    acc = lat_sq[which] = acc_a if which == "q" else acc_b
                    tq = pool([t], gp.tensor_tensor, acc, s.ap[:, 0:S], s.ap[:, 0:S], ALU.mult)
                else:
                    acc, prev = lat_sq[which], lat_sq[which + "t"]
                    q = scratch.next()
                    tq = pool([t] + q.free, gp.tensor_tensor, q.ap[:, 0:S], s.ap[:, 0:S], s.ap[:, 0:S], ALU.mult)
                    tq = pool([tq], gp.tensor_tensor, acc, acc, q.ap[:, 0:S], ALU.add)
                    q.free = [tq]
                lat_sq[which + "t"] = tq
                s.free = [*s2, tq]
                if m == 3:
                    done_list.append((dst_factor, acc, tq))
                return [t]
            return f

        evac["qa"] = latent("q", 0, "qa", rq_done, 2)
        evac["kva"] = latent("kv", 4, "kva", rkv_done, None)

        def square_factor(dst, acc, acc_done, n):
            b = side_banks.next()
            PE.wait(b.free + [acc_done])
            t = PE.mark(mm(b.ap[:, 0:S], c("ones"), acc))
            t = dve([t], v.tensor_scalar, dst, b.ap[:, 0:S], 1.0 / n, EPS, ALU.mult, ALU.add)
            b.free = [t]
            return pool([t], gp.tensor_tensor, dst, dst, c("neg_half").to_broadcast([P, S]), ALU.pow)

        kr_done = []

        def rope_tile(x, x_done, rot, cos, sin, rope_ready, width, dup=None, rows=P):
            b = side_banks.next()
            PE.wait(b.free + [x_done] + rope_ready)
            t = PE.mark(mm(b.ap[:, 0:width], rot[0:rows, :], x[0:rows, :]))
            s = scratch.next()
            t1 = dve([t] + s.free + rope_ready, v.tensor_tensor, s.ap[:, 0:width], b.ap[:, 0:width], sin, ALU.mult)
            b.free = [t1]
            if dup is not None:
                b = side_banks.next()
                PE.wait(b.free)
                t = PE.mark(mm(b.ap[:, 0:width], dup[0:rows, :], x[0:rows, :]))
                t2 = dve([t], v.tensor_tensor, x, b.ap[:, 0:width], cos, ALU.mult)
                b.free = [t2]
            else:
                t2 = pool([x_done, t] + rope_ready, gp.tensor_tensor, x, x, cos, ALU.mult)
            t = pool([t1, t2], gp.tensor_tensor, x, x, s.ap[:, 0:width], ALU.add)
            s.free = [t]
            return t

        def evac_kr(g, m, ps, done):
            t = dve([done], v.tensor_tensor, kr1[:, :], ps, R_, ALU.mult)

            def job():
                yield
                kr_done.append(rope_tile(kr1[:, :], t, c("rot_k1"), cos1, sin1, rope_done, S, dup=c("dup64")))
                tap("kr1", kr1[:, :], kr_done)
            pending.append(job())
            return [t]

        evac["kr"] = evac_kr
        q_done, qr_done, k_done, v_done, v_read = {}, {}, {}, {}, {}

        def evac_q(g, m, ps, done):
            if m < 2:
                h = 2 * g + m
                t = q_done[h] = dve([done, x_in_free, *rq_done], v.tensor_tensor, Q1[:, h, :], ps, RQ, ALU.mult)
                return [t]
            t = dve([done, meta_free], v.tensor_tensor, QR[:, g, :], ps, RQ, ALU.mult)

            def job():
                yield
                qr_done[g] = rope_tile(QR[:, g, :], t, c("rot_q1"), cos1, sin1, rope_done, S)
                yield
            pending.append(job())
            return [t]

        evac["q"] = evac_q

        def evac_kvb(g, m, ps, done):
            h = 2 * g + m // 2
            if m % 2 == 0:
                t = k_done[h] = dve([done, *rkv_done, cols_done], v.tensor_tensor, K1[:, h, :], ps, RKV, ALU.mult)
                return [t]
            s = scratch.next()
            t = v_read[h] = dve([done, *rkv_done] + s.free, v.tensor_tensor, s.ap[:, 0:S], ps, RKV, ALU.mult)
            b = side_banks.next()

            def job():
                PE.wait(b.free + [t])
                for blk in range(2):
                    i = nc.tensor.transpose(b.ap[:, blk * P:(blk + 1) * P], s.ap[:, blk * P:(blk + 1) * P], c("ident"))
                t2 = PE.mark(i)
                s.free = [t2]
                v_done[h] = act([t2], V1[:, :, h * P:(h + 1) * P],
                                b.ap[:, 0:S].rearrange("p (b n) -> p b n", b=2), ACT.Copy)
                b.free = [v_done[h]]
            job()
            return [t]

        evac["kv"] = evac_kvb

        attn_done = {}
        stats = Ring([sb(f"stats{i}", [P, 8])[:, :] for i in range(4)])

        def attention1(h):
            half = 64 * (h % 2)
            kr, qr = kr1[half:half + 64, :], QR[half:half + 64, h // 2, :]
            b = side_banks.next()
            PE.wait(b.free + [q_done[h], qr_done[h // 2], k_done[h], *kr_done])
            mm(b.ap[:, 0:P], Q1[:, h, 0:P], K1[:, h, 0:P], True, False)
            mm(b.ap[:, 0:P], qr[:, 0:P], kr[:, 0:P], False, True)
            mm(b.ap[:, P:3 * P], Q1[:, h, P:S], K1[:, h, :], True, False)
            t = PE.mark(mm(b.ap[:, P:3 * P], qr[:, P:S], kr, False, True))
            p, st = prob.next(), stats.next()
            dve([t] + p.free, v.scalar_tensor_tensor, p.ap[:, 0:P], b.ap[:, 0:P], SCALE1, c("mask1")[:, P:S],
                ALU.mult, ALU.add)
            t = dve([], v.scalar_tensor_tensor, p.ap[:, P:384], b.ap[:, P:384], SCALE1, c("mask1"),
                    ALU.mult, ALU.add)
            b.free = [t]
            parts = ((0, P), (P, 3 * P))
            done = softmax(p, st, parts, t)
            yield
            pt = probT.next()
            b = side_banks.next()
            PE.wait(b.free + done)
            for j in range(3):
                i = nc.tensor.transpose(b.ap[:, j * P:(j + 1) * P], p.ap[:, j * P:(j + 1) * P], c("ident"))
            t = PE.mark(i)
            p.free = [t]
            t = act([t] + pt.free, pt.ap[:, 0:384], b.ap[:, 0:384], ACT.Copy)
            b.free = [t]
            yield
            b = side_banks.next()
            PE.wait(b.free + [t, v_done[h]])
            mm(b.ap[:, 0:S], V1[:, 0, h * P:(h + 1) * P], pt.ap[:, 0:S], True, False)
            t = PE.mark(mm(b.ap[:, P:S], V1[:, 1, h * P:(h + 1) * P], pt.ap[:, S:384], False, True))
            pt.free = [t]
            attn_done[h] = act([t], Q1[:, h, :], b.ap[:, 0:S], ACT.Copy)
            b.free = [attn_done[h]]

        def softmax(p, st, parts, t):
            n = len(parts)
            tm = [dve([t] + st.free, v.tensor_reduce, st.ap[:, i:i + 1], p.ap[:, lo:hi], AX, ALU.max, negate=True)
                  for i, (lo, hi) in enumerate(parts)]
            te = [act([tm[i]], p.ap[:, lo:hi], p.ap[:, lo:hi], ACT.Exp, bias=st.ap[:, i:i + 1],
                      accum_out=st.ap[:, 2 + i:3 + i]) for i, (lo, hi) in enumerate(parts)]
            tr = dve(te, v.reciprocal, st.ap[:, 4:4 + n], st.ap[:, 2:2 + n])
            done = [dve([tr], v.tensor_scalar, p.ap[:, lo:hi], p.ap[:, lo:hi], st.ap[:, 4 + i:5 + i], None, ALU.mult)
                    for i, (lo, hi) in enumerate(parts)]
            st.free = done
            return done

        metaT = small
        b = side_banks.next()
        PE.wait([meta_load, con_load, *b.free])
        for k in range(KT):
            i = nc.tensor.transpose(b.ap[:, k * NMETA:(k + 1) * NMETA], x_meta[0:NMETA, k * P:(k + 1) * P],
                                    c("ident")[0:NMETA, 0:NMETA])
        t = PE.mark(i)
        meta_free = t
        meta_done = act([t, tp], metaT[:, :], b.ap[:, 0:KT * NMETA], ACT.Copy)
        b.free = [meta_done]

        conv_t, cin_t = {}, {}
        u_t, gate_t = region(56, 4, 4, S), region(60, 4, 4, S)
        oc_marks = {}

        def conv_evacs(j):
            def cin(g, m, ps, done):
                cin_t[m] = dve([done, rr_done, *conv_free[m]], v.tensor_tensor, gate_t[:, m, :], ps, RR, ALU.mult)
                return [cin_t[m]]

            def cgate(g, m, ps, done):
                k = 4 * j + m
                s = scratch.next()
                u, y = s.ap[:, 0:S], u_t[:, m, :]
                t = dve([done, cin_t[m]] + s.free, v.tensor_tensor, u, ps, gate_t[:, m, :], ALU.mult)
                tu = t
                t = act([t, *conv_free[m]], y, u, ACT.Copy, scale=col("conv", 32 + k))
                t = dve([t, tu], v.scalar_tensor_tensor, y[:, 1:S], u[:, 0:S - 1], col("conv", 16 + k), y[:, 1:S],
                        ALU.mult, ALU.add)
                t = dve([t], v.scalar_tensor_tensor, y[:, 2:S], u[:, 0:S - 2], col("conv", k), y[:, 2:S],
                        ALU.mult, ALU.add)
                s.free = [t]
                conv_t[m] = t
                return [tu]

            def bgate(g, m, ps, done):
                y = u_t[:, m, :]
                t = dve([done, conv_t[m]], v.tensor_tensor, y, ps, y, ALU.mult)
                conv_t[m] = pool([t], gp.tensor_tensor, y, y, R_, ALU.mult)
                return [t]

            def zconv(g, m, ps, done):
                k = 4 * j + m
                y = u_t[:, m, :]
                s, s2 = scratch.next(), scratch.next()
                z, sg = s.ap[:, 0:S], s2.ap[:, 0:S]
                tz = dve([done] + s.free, v.tensor_tensor, z, ps, R_, ALU.mult)
                t = act([tz] + s2.free, sg, z, ACT.Sigmoid)
                t = pool([t, tz], gp.tensor_tensor, z, z, sg, ALU.mult)
                s2.free = [t]
                t = pool([t, conv_t[m]], gp.tensor_tensor, z, z, y, ALU.mult)
                conv_free[m] = [t]
                oc_marks[k] = split_to(ob_hi[:, k, 0:S], ob_lo[:, k, 0:S], z, t, lat_read)
                s.free = oc_marks[k]
                return [tz]
            return cin, cgate, bgate, zconv

        conv_free = {m: [x_sq, *h_marks[KT - 1]] for m in range(4)}

        for ph_ in (p_qa, p_kv, p_kr, *[x for _, x in p_conv], p_gc, p_zm, p_gm):
            ph_.ready = h_ready
        run(p_qa)
        _, acc_, ta_ = rq_done.pop()
        rq_done.append(square_factor(RQ, acc_, ta_, LORA))
        run(p_kv)
        _, acc_, ta_ = rkv_done.pop()
        run(p_kr)
        rkv_done.append(square_factor(RKV, acc_, ta_, LORA))
        p_q.ready = lambda kt: lat_marks["q", kt]
        p_k.ready = lambda kt: lat_marks["kv", kt]
        run(p_q)
        tap("Q1", Q1, [q_done[15]])
        run(p_k)
        rr_done = pool([r1_done, k_done[15], v_read[15]], gp.tensor_tensor, RR, R_, R_, ALU.mult)
        lat_read = [(PE.sem, PE.count)]
        drain_jobs()
        tap("QR", QR, [qr_done[7]])
        tap("K1", K1, [k_done[15]])
        tap("V1", V1, [v_done[15]])
        pending.extend(attention1(h) for h in range(H1))
        for j, p_ in p_conv:
            for name, f in zip(("cin", "cgate", "bgate", "zconv"), conv_evacs(j)):
                evac[f"{name}{j}"] = f
            run(p_)
        if pending or active:
            drain_jobs()
        tap("attn1", Q1, [attn_done[15]])

        def sigmoid_to(dst, factor_, fdone, marks, key, free=()):
            def f(g, m, ps, done):
                k = 4 * g + m
                s = scratch.next()
                tz = dve([done, fdone] + s.free, v.tensor_tensor, s.ap[:, 0:S], ps, factor_, ALU.mult)
                marks[key, k] = act([tz, *free], dst[:, k, :], s.ap[:, 0:S], ACT.Sigmoid)
                s.free = [marks[key, k]]
                return [tz]
            return f

        gate = {}
        evac["gconv"] = sigmoid_to(G1, R_, r1_done, gate, "gc", sum(conv_free.values(), []))
        run(p_gc)

        def evac_oc(g, m, ps, done):
            k = 4 * g + m
            gate["yc", k] = dve([done, gate["gc", k]], v.tensor_tensor, G1[:, k, :], ps, G1[:, k, :], ALU.mult)
            return [gate["yc", k]]

        evac["oconv"] = evac_oc
        p_oc.ready = lambda kt: oc_marks[kt]
        run(p_oc)
        oc_read = [(PE.sem, PE.count)]
        tap("yconv", G1, [gate["yc", 15]])
        zm, zm_pool = {}, {}

        def silu_times(y, y_marks, factor_, fdone, dst_hi, dst_lo, free, marks):
            def f(g, m, ps, done):
                k = 4 * g + m
                s, s2 = scratch.next(), scratch.next()
                z, sg = s.ap[:, 0:S], s2.ap[:, 0:S]
                tz = dve([done, fdone] + s.free, v.tensor_tensor, z, ps, factor_, ALU.mult)
                t = act([tz] + s2.free, sg, z, ACT.Sigmoid)
                t = pool([t, tz], gp.tensor_tensor, z, z, sg, ALU.mult)
                s2.free = [t]
                t = zm_pool[k] = pool([t, y_marks[k]], gp.tensor_tensor, z, z, y[:, k, :], ALU.mult)
                marks[k] = split_to(dst_hi(k), dst_lo(k), z, t, free)
                s.free = marks[k]
                return [tz]
            return f

        evac["zmla"] = silu_times(Q1, attn_done, R_, r1_done, *ob, oc_read, zm)
        run(p_zm)
        evac["gmla"] = sigmoid_to(GM, R_, r1_done, gate, "gm", list(attn_done.values()))
        run(p_gm)
        hb_read = [(PE.sem, PE.count)]
        mg, gm_read = {}, []

        def evac_om(g, m, ps, done):
            k = 4 * g + m
            s = scratch.next()
            z = s.ap[:, 0:S]
            tz = dve([done, gate["gm", k]] + s.free, v.tensor_tensor, z, ps, GM[:, k, :], ALU.mult)
            t = pool([tz, gate["yc", k]], gp.tensor_tensor, z, z, G1[:, k, :], ALU.add)
            gm_read[:] = [tz]
            mg[k] = split_to(hb_hi[:, k, :], hb_lo[:, k, :], z, t, hb_read)
            s.free = mg[k]
            return [tz]

        evac["omla"] = evac_om
        p_om.ready = lambda kt: zm[kt]
        run(p_om)
        ob_read = [(PE.sem, PE.count)]
        out_t, sq_t = {}, [None]
        acc1 = acc_a

        def evac_w(g, m, ps, done):
            k = 4 * g + m
            t = out_t[k] = act([done, *attn_done.values()], OUT1[:, k, :], ps, ACT.Copy)
            if k == 0:
                sq_t[0] = pool([t], gp.tensor_tensor, acc1, OUT1[:, k, :], OUT1[:, k, :], ALU.mult)
            else:
                s = scratch.next()
                t1 = pool([t] + s.free, gp.tensor_tensor, s.ap[:, 0:S], OUT1[:, k, :], OUT1[:, k, :], ALU.mult)
                sq_t[0] = pool([t1, sq_t[0]], gp.tensor_tensor, acc1, acc1, s.ap[:, 0:S], ALU.add)
                s.free = [sq_t[0]]
            return [t]

        evac["wout"] = evac_w
        p_w.ready = lambda kt: mg[kt]
        metaf = metaT[:, :].rearrange("p (k n) -> p k n", k=KT)
        meta_marks, acc_m = [], small2[:, 40:56]
        for k in range(KT):
            meta_marks.append(split_to(ob_hi[:, k, 0:NMETA], ob_lo[:, k, 0:NMETA], metaf[:, k, :], meta_done,
                                       ob_read, gain=col("norm2", k)))
        tm = sum_squares(acc_m, [metaf[:, k, :] for k in range(KT)], [meta_done] * KT)
        x_again = [load(x_in[:, b_, :], a["x"][0, b_ * P:(b_ + 1) * P, :], list(zm_pool.values()) + gm_read)
                   for b_ in range(2)]

        def residual():
            yield
            yield
            for k in range(KT):
                b = side_banks.next()
                PE.wait(b.free + x_again)
                for blk in range(2):
                    i = nc.tensor.transpose(b.ap[:, blk * P:(blk + 1) * P], x_in[:, blk, k * P:(k + 1) * P], c("ident"))
                t = PE.mark(i)
                xr_done[k] = act([t, *gm_read], XR[:, k, :], b.ap[:, 0:S], ACT.Copy)
                b.free = [xr_done[k]]
                if k % 2:
                    yield

        xr_done = {}
        pending.append(residual())
        run(p_w)
        drain_jobs()
        hb2_read = [(PE.sem, PE.count)]
        tap("out1", OUT1, [out_t[15]])

        F2 = factor[:, 1, :]
        m_done = factor_of(1, (0, NMETA), acc_m, tm, D, [])
        rp_done = square_factor(RQ, acc1, sq_t[0], D)
        x1_marks, h2_marks, sq2 = [], [], None
        acc2 = acc_b
        for k in range(KT):
            o, x = OUT1[:, k, :], XR[:, k, :]
            t = dve([rp_done, out_t[k]], v.tensor_tensor, o, o, RQ, ALU.mult)
            t = dve([t, xr_done[k]], v.scalar_tensor_tensor, x, o, col("post", k), x, ALU.mult, ALU.add)
            x1_marks.append(t)
            h2_marks.append(split_to(ob_hi[:, k, NMETA:T], ob_lo[:, k, NMETA:T], x, t, ob_read, gain=col("norm2", k))
                            + meta_marks[k])
            if k == 0:
                sq2 = pool([t], gp.tensor_tensor, acc2, x, x, ALU.mult)
            else:
                s = scratch.next()
                t1 = pool([t] + s.free, gp.tensor_tensor, s.ap[:, 0:S], x, x, ALU.mult)
                sq2 = pool([t1, sq2], gp.tensor_tensor, acc2, acc2, s.ap[:, 0:S], ALU.add)
                s.free = [sq2]
        x1_dram = nc.dram_tensor("x1_kept", [P, KT * S], F32, kind="Internal").ap()
        x1_kept = load(x1_dram, XR.rearrange("p k n -> p (k n)"), x1_marks)
        tap("x1", XR, x1_marks)
        arena_free = [x1_marks[-1], sq2, x1_kept, h2_marks[-1][0], h2_marks[-1][1]]

        QI, KI = region(0, 8, 8, S), region(8, 2, T)
        KA, QA, VA = region(9.25, 4.25, KVA, T), region(13.5, 8, HA, S), region(21.5, 6, 3, 512)
        FB, IB, QB = region(27.5, 8.5, HB, T), region(36, 12, 3, 1024), region(48, 8, HB, S)
        GA = region(56, 16, KT, S)
        L0 = CONSTS["late"][0]
        late = region(58, 6, CONSTS["late"][1] - L0)
        bias2, score2 = region(65, 2, 416), region(67, 2, 416)
        late_load = load(late, a["const_f"][:, L0:CONSTS["late"][1]], arena_free)

        def lc(name):
            lo, hi = CONSTS[name]
            return late[:, lo - L0:hi - L0]

        for p_ in (p2_ki, p2_qi, p2_ka, p2_va, p2_qa, p2_fb, p2_ib, p2_qb, p2_ga, p2_za, p2_zb, p2_gb):
            p_.ready = lambda kt: h2_marks[kt]

        wiT = small3[:, :]
        ki_done, wi_done, qi_done = [], [], {}
        F2M = F2[:, NMETA:T]
        f2 = []

        def evac_ki(g, m, ps, done):
            f2.append(factor_of(1, (NMETA, T), acc2, sq2, D, []))
            t = dve([done, *f2, m_done, *arena_free], v.tensor_tensor, KI, ps, F2, ALU.mult)

            def job():
                yield
                b = side_banks.next()
                PE.wait(b.free + [t])
                for blk in range(2):
                    i = nc.tensor.transpose(b.ap[:, blk * P:(blk + 1) * P],
                                            KI[:, NMETA + blk * P:NMETA + (blk + 1) * P], c("ident"))
                t1 = PE.mark(i)
                wi_done.append(dve([t1], v.tensor_scalar, wiT.rearrange("p (b h) -> p b h", b=2),
                                   b.ap[:, 0:S].rearrange("p (b n) -> p b n", b=2)[:, :, DI:DI + HI],
                                   W_SCALE, None, ALU.mult))
                b.free = wi_done
                f, tf = head_factor(KI[0:DI, :], t, DI, T, rows=DI)
                yield
                t2 = dve([tf, t1], v.tensor_tensor, KI[0:DI, :], KI[0:DI, :], f.ap[0:DI, :], ALU.mult)
                f.free = [t2]
                t2 = act([t2], KI[0:DI, :], KI[0:DI, :], ACT.Copy, scale=col("ikn")[0:DI, :])
                yield
                ki_done.append(rope_tile(KI, t2, lc("rot_i"), lc("cos_i"), lc("sin_i"), [late_load], T,
                                         dup=c("dup64"), rows=DI))
            pending.append(job())
            return [t]

        evac["ki"] = evac_ki

        def evac_qi(g, m, ps, done):
            k = 4 * g + m
            t = dve([done, *f2, *arena_free], v.tensor_tensor, QI[:, k, :], ps, F2M, ALU.mult)

            def job():
                yield
                qi_done[k] = rope_tile(QI[:, k, :], t, lc("rot_i1"), lc("cos_i")[:, NMETA:T],
                                       lc("sin_i")[:, NMETA:T], [late_load], S)
            pending.append(job())
            return [t]

        evac["qi"] = evac_qi

        def rms_rope_head(dst, ps, done, fac, width, lo, gname, marks, k):
            t = dve([done, *f2, *arena_free], v.tensor_tensor, dst, ps, fac, ALU.mult)

            def job():
                yield
                f, tf = head_factor(dst, t, P, width)
                yield
                t2 = dve([tf], v.scalar_tensor_tensor, dst, dst, col(gname), f.ap[:, 0:width], ALU.mult, ALU.mult)
                f.free = [t2]
                marks[k] = rope_tile(dst, t2, lc("rot_a"), lc("cos_a")[:, lo:T], lc("sin_a")[:, lo:T],
                                     [late_load], width)
            pending.append(job())
            return [t]

        ka_done, qa_done, va_done = {}, {}, {}
        evac["ka"] = lambda g, m, ps, done: rms_rope_head(KA[:, m, :], ps, done, F2, T, 0, "kn", ka_done, m)
        evac["qa2"] = lambda g, m, ps, done: rms_rope_head(QA[:, 4 * g + m, :], ps, done, F2M, S, NMETA, "qn",
                                                           qa_done, 4 * g + m)

        def token_major(dst, marks):
            def f(g, m, ps, done):
                k = 4 * g + m
                s = scratch.next()
                t = t_out = dve([done, *f2, *arena_free] + s.free, v.tensor_tensor, s.ap, ps, F2, ALU.mult)
                b = side_banks.next()
                PE.wait(b.free + [t])
                for blk in range(2):
                    nc.tensor.transpose(b.ap[:, blk * P:(blk + 1) * P],
                                        s.ap[:, NMETA + blk * P:NMETA + (blk + 1) * P], c("ident"))
                i = nc.tensor.transpose(b.ap[0:NMETA, S:S + P], s.ap[:, 0:NMETA], c("ident"))
                t = PE.mark(i)
                s.free = [t]
                w = slice(k * P, (k + 1) * P)
                act([t], dst[:, 1:3, w], b.ap[:, 0:S].rearrange("p (b n) -> p b n", b=2), ACT.Copy)
                marks[k] = act([], dst[0:NMETA, 0, w], b.ap[0:NMETA, S:S + P], ACT.Copy)
                b.free = [marks[k]]
                return [t_out]
            return f

        evac["va"] = token_major(VA, va_done)
        ib_done = {}
        evac["ib"] = token_major(IB, ib_done)

        KEYS = (NMETA + P, T)
        PART = ((0, KEYS[0]), (KEYS[0], KEYS[0] + KEYS[1]))
        chain = {"score": None, "bias": None}

        def index_head(h):
            half = 64 * (h % 2)
            b = side_banks.next()
            PE.wait(b.free + [qi_done[h // 2], *ki_done])
            for blk, (lo, hi) in enumerate(PART):
                i = mm(b.ap[:, lo:hi], QI[half:half + 64, h // 2, blk * P:(blk + 1) * P],
                       KI[half:half + 64, 0:KEYS[blk]])
            t = PE.mark(i)
            p = prob.next()
            t = act([t] + p.free, p.ap, b.ap[:, 0:416], ACT.Relu)
            b.free = [t]
            yield
            for blk, (lo, hi) in enumerate(PART):
                w = wiT[:, blk * HI + h:blk * HI + h + 1]
                if h == 0:
                    ts = dve([t, *wi_done, *arena_free], v.tensor_scalar, score2[:, lo:hi], p.ap[:, lo:hi], w, None, ALU.mult)
                else:
                    ts = dve([t, chain["score"]], v.scalar_tensor_tensor, score2[:, lo:hi], p.ap[:, lo:hi], w,
                             score2[:, lo:hi], ALU.mult, ALU.add)
            p.free = [ts]
            chain["score"] = ts

        best = sb("best", [P, 16])

        def select():
            t = chain["score"]
            for blk, (lo, hi) in enumerate(PART):
                t = dve([t], v.memset, score2[0:CHUNK, hi - CHUNK:hi], MASKED)
            for r in range(TOPK // 8):
                yield
                for blk, (lo, hi) in enumerate(PART):
                    m8 = best[:, 8 * blk:8 * blk + 8]
                    t8 = dve([t], v.max, m8, score2[:, lo:hi])
                    t = dve([t8], v.match_replace, score2[:, lo:hi], m8, score2[:, lo:hi], TAKEN)
            chain["bias"] = dve([t], v.tensor_scalar, bias2, score2, (MASKED + TAKEN) / 2, NEG, ALU.is_gt, ALU.mult)

        ya_done = {}

        def attention2(h):
            g = h // 2
            b = side_banks.next()
            PE.wait(b.free + [qa_done[h], ka_done[g]])
            for blk, (lo, hi) in enumerate(PART):
                i = mm(b.ap[:, lo:hi], QA[:, h, blk * P:(blk + 1) * P], KA[:, g, 0:KEYS[blk]])
            t = PE.mark(i)
            p, st = prob.next(), stats.next()
            t = dve([t, chain["bias"]] + p.free, v.scalar_tensor_tensor, p.ap, b.ap[:, 0:416], SCALE2, bias2,
                    ALU.mult, ALU.add)
            b.free = [t]
            done = softmax(p, st, PART, t)
            yield
            pt = probT.next()
            b, b2 = side_banks.next(), side_banks.next()
            PE.wait(b.free + b2.free + done)
            lo0, lo1 = PART[0][0] + NMETA, PART[1][0] + NMETA
            for j, lo in enumerate((lo0, lo1, lo1 + P)):
                nc.tensor.transpose(b.ap[:, j * P:(j + 1) * P], p.ap[:, lo:lo + P], c("ident"))
            for blk in range(2):
                lo = PART[blk][0]
                i = nc.tensor.transpose(b2.ap[0:NMETA, blk * P:(blk + 1) * P], p.ap[:, lo:lo + NMETA], c("ident"))
            t = PE.mark(i)
            p.free = [t]
            t1 = act([t] + pt.free, pt.ap[:, 0:384], b.ap[:, 0:384], ACT.Copy)
            b.free = [t1]
            t = act([], pt.ap[0:NMETA, 384:640], b2.ap[0:NMETA, 0:S], ACT.Copy)
            b2.free = [t]
            yield
            b = side_banks.next()
            w = slice(g * P, (g + 1) * P)
            PE.wait(b.free + [t, va_done[g]])
            mm(b.ap[:, 0:S], VA[:, 1, w], pt.ap[:, 0:S], True, False)
            mm(b.ap[:, P:S], VA[:, 2, w], pt.ap[:, S:384], False, False)
            t = PE.mark(mm(b.ap[:, 0:S], VA[0:NMETA, 0, w], pt.ap[0:NMETA, 384:640], False, True))
            pt.free = [t]
            ya_done[h] = act([t], QA[:, h, :], b.ap[:, 0:S], ACT.Copy)
            b.free = [ya_done[h]]

        fb_done, qb_done = {}, {}

        def evac_fb(g, m, ps, done):
            k = 4 * g + m
            s = scratch.next()
            t = dve([done, *f2] + s.free, v.tensor_tensor, s.ap, ps, F2, ALU.mult)
            t1 = act([t], s.ap, s.ap, ACT.Sigmoid)
            fb_done[k] = dve([t1, lb_done, *arena_free], v.tensor_scalar, FB[:, k, :], s.ap, oml[:, k:k + 1], lb[:, k:k + 1],
                             ALU.mult, ALU.add)
            s.free = [fb_done[k]]
            return [t]

        evac["fb"] = evac_fb

        def evac_qb(g, m, ps, done):
            k = 4 * g + m
            s = scratch.next()
            t = dve([done, *f2, *arena_free], v.tensor_tensor, QB[:, k, :], ps, F2M, ALU.mult)
            t1 = act([t] + s.free, s.ap[:, 0:S], QB[:, k, :], ACT.Sigmoid)
            qb_done[k] = pool([t1], gp.tensor_tensor, QB[:, k, :], QB[:, k, :], s.ap[:, 0:S], ALU.mult)
            s.free = [qb_done[k]]
            return [t]

        evac["qb"] = evac_qb

        W2 = 2 * S

        def doubled(Cp, Rp, n, h, free):
            cv = Cp.rearrange("p (b x) -> p b x", x=2 * h)
            rv = Rp.rearrange("p (b x) -> p b x", x=2 * h)
            nb = n // (2 * h)
            t = dve(free, v.tensor_tensor, rv[:, :, 0:h], rv[:, :, 0:h],
                    cv[:, :, 2 * h - 1:2 * h].to_broadcast([P, nb, h]), ALU.mult)
            t = dve([t], v.tensor_tensor, cv[:, :, h:2 * h], cv[:, :, h:2 * h],
                    cv[:, :, h - 1:h].to_broadcast([P, nb, h]), ALU.mult)
            return t

        o_done = {}
        hg = {}

        def meta_state():
            C0, R0, kd = hg["C"], hg["R"], hg["kL"]
            n = HB * NMETA
            fm = FB[:, :, 0:NMETA]
            cv = C0[:, 0:n]
            t = dve([*fb_done.values(), *arena_free, *hg["free"]], v.tensor_copy, cv.rearrange("p (h x) -> p h x", h=HB), fm)
            t1 = dve([], v.memset, R0[:, 0:n], 1.0)
            t = dve([], v.tensor_scalar, kd[:, 0:n].rearrange("p (h x) -> p h x", h=HB), fm, -1.0, 1.0, ALU.mult, ALU.add)
            for h in (1, 2, 4, 8):
                t = doubled(cv, R0[:, 0:n], n, h, [t, t1])
            yield
            t = dve([t], v.tensor_tensor, kd[:, 0:n], kd[:, 0:n], R0[:, 0:n], ALU.mult)
            for half in range(2):
                b = side_banks.next()
                PE.wait(b.free + [t])
                for j in range(4):
                    h = 4 * half + j
                    i = nc.tensor.transpose(b.ap[0:NMETA, j * P:(j + 1) * P], kd[:, h * NMETA:(h + 1) * NMETA], c("ident"))
                t2 = PE.mark(i)
                t2 = act([t2], hg["kM"][0:NMETA, half * 512:(half + 1) * 512], b.ap[0:NMETA, :], ACT.Copy)
                b.free = [t2]
            hg["kM_done"] = t2
            hg["free"] = [(PE.sem, PE.count), (VE.sem, VE.count)]

        def recurrence(pr):
            Cb, Rb, kL, qL, A, kK = hg["C"], hg["R"], hg["kL"], hg["qL"], hg["A"], hg["kK"]
            F = FB[:, 2 * pr:2 * pr + 2, NMETA:T]
            q = QB[:, 2 * pr:2 * pr + 2, :].rearrange("p h x -> p (h x)")
            h2 = lambda x: x.rearrange("p (h x) -> p h x", h=2)
            t = dve(hg["free"] + [qb_done[2 * pr], qb_done[2 * pr + 1]], v.tensor_copy, h2(Cb), F)
            t1 = dve([], v.memset, Rb, 1.0)
            tk = dve([], v.tensor_scalar, h2(kK), F, -1.0, 1.0, ALU.mult, ALU.add)
            b = side_banks.next()
            PE.wait(b.free + [tk])
            for j in range(4):
                w = slice(j * P, (j + 1) * P)
                i = mm(b.ap[:, w], kK[:, w], q[:, w])
            tp = PE.mark(i)
            four = lambda x: x.rearrange("p (a b) -> p a b", a=4)
            tA = dve([tp], v.tensor_tensor, four(A), four(b.ap), c("ident").unsqueeze(1).to_broadcast([P, 4, P]), ALU.mult)
            b.free = [tA]
            tprev = None
            for li, h in enumerate(LEVELS):
                yield
                right = lambda x: x.rearrange("p (b x) -> p b x", x=2 * h)[:, :, h:2 * h]
                left = lambda x: x.rearrange("p (b x) -> p b x", x=2 * h)[:, :, 0:h]
                ws = [t, t1, tk, tprev, *hg["init"]]
                ta_ = dve(ws, v.tensor_tensor, right(qL), right(q), right(Cb), ALU.mult)
                tb_ = pool(ws, gp.tensor_tensor, left(kL), left(kK), left(Rb), ALU.mult)
                b = side_banks.next()
                PE.wait(b.free + [ta_, tb_])
                for j in range(4):
                    w = slice(j * P, (j + 1) * P)
                    i = mm(b.ap[:, w], kL[:, w], qL[:, w])
                tprev = PE.mark(i)
                t = doubled(Cb, Rb, W2, h, [t, t1, tb_])
                tA = dve([tprev, lvl_done, tA], v.copy_predicated, four(A),
                         lvl[:, li * P:(li + 1) * P].unsqueeze(1).to_broadcast([P, 4, P]), four(b.ap))
                b.free = [tA]
            yield
            tk2 = pool([t, tprev], gp.tensor_tensor, h2(kL)[:, :, 0:P], h2(kK)[:, :, 0:P], h2(Rb)[:, :, 0:P], ALU.mult)
            tq2 = dve([t, tprev], v.tensor_tensor, qL, q, Cb, ALU.mult)
            b = side_banks.next()
            PE.wait(b.free + [tk2])
            for j in range(2):
                i = nc.tensor.transpose(b.ap[:, j * P:(j + 1) * P], kL[:, j * S:j * S + P], c("ident"))
            t3 = PE.mark(i)
            kd = hg["kd"]
            t3 = act([t3] + hg["kd_free"], kd, b.ap[:, 0:S], ACT.Copy)
            b.free = [t3]
            b = side_banks.next()
            PE.wait(b.free + [hg["kM_done"], t3, *ib_done.values()])
            for j in range(2):
                h = 2 * pr + j
                w = slice(h * P, (h + 1) * P)
                mm(b.ap[:, j * P:(j + 1) * P], hg["kM"][0:NMETA, w], IB[0:NMETA, 0, w])
                i = mm(b.ap[:, S + j * P:S + (j + 1) * P], kd[:, j * P:(j + 1) * P], IB[:, 1, w])
            t4 = PE.mark(i)
            St = hg["S"]
            t5 = act([t4] + hg["S_free"], St[:, 0:S], b.ap[:, 0:S], ACT.Copy)
            for j in range(2):
                t6 = dve([t5, t], v.scalar_tensor_tensor, St[:, S + j * P:S + (j + 1) * P], St[:, j * P:(j + 1) * P],
                         Cb[:, j * S + P - 1:j * S + P], b.ap[:, S + j * P:S + (j + 1) * P], ALU.mult, ALU.add)
            b.free = [t6]
            hg["kd_free"] = [t4]
            yield
            b = side_banks.next()
            PE.wait(b.free + [t6, tq2, tA])
            for j in range(2):
                w = slice((2 * pr + j) * P, (2 * pr + j + 1) * P)
                for blk in range(2):
                    x = slice(j * S + blk * P, j * S + (blk + 1) * P)
                    mm(b.ap[:, x], IB[:, 1 + blk, w], A[:, x], True, False)
                    i = mm(b.ap[:, x], St[:, blk * S + j * P:blk * S + (j + 1) * P], qL[:, x], False, True)
            t7 = PE.mark(i)
            hg["S_free"] = [t7]
            hg["free"] = [t7, t6]
            t8 = act([t7], QB[:, 2 * pr:2 * pr + 2, :].rearrange("p h x -> p (h x)"), b.ap, ACT.Copy)
            b.free = [t8]
            yield
            for j in range(2):
                h = 2 * pr + j
                f, tf = head_factor(QB[:, h, :], t8, P, S)
                o_done[h] = dve([tf], v.scalar_tensor_tensor, QB[:, h, :], QB[:, h, :], col("on"), f.ap[:, 0:S],
                                ALU.mult, ALU.mult)
                f.free = [o_done[h]]

        run(p2_ki)
        run(p2_qi)
        run(p2_ka)
        drain_jobs()
        tap("KI", KI, ki_done)
        tap("QI", QI, [qi_done[7]])
        index_jobs = [index_head(h) for h in range(HI)]
        pending.extend(index_jobs)
        run(p2_va)
        run(p2_qa)
        drain_jobs()
        tap("score2", score2, [chain["score"]])
        tap("KA", KA, list(ka_done.values()))
        tap("QA", QA, list(qa_done.values()))
        pending.append(select())
        run(p2_fb)
        drain_jobs()
        tap("bias2", bias2, [chain["bias"]])
        pending.extend(attention2(h) for h in range(HA))
        run(p2_ib)
        run(p2_qb)
        drain_jobs()
        tap("ya", QA, list(ya_done.values()))
        attn2_over = list(ya_done.values()) + [chain["bias"]]
        hg.update(C=region(0, 2, W2), R=region(2, 2, W2), kL=region(4, 2, W2), qL=region(6, 2, W2),
                  A=region(8, 2, W2), kK=region(10, 2, W2), kd=region(12, 1, S), S=region(21.5, 2, W2),
                  kM=region(23.5, 4, 1024), free=[(PE.sem, PE.count), (SC.sem, SC.count), (VE.sem, VE.count),
                                                (GP.sem, GP.count)], kd_free=[], S_free=[])
        lvl = small[:, 0:224].bitcast(U8)
        lvl_f = region(0, 3.5, len(LEVELS) * P)
        lvl_done = dve([load(lvl_f, a["const_lvl"], hg["free"])], v.tensor_copy, lvl, lvl_f)
        hg["free"].append(lvl_done)
        hg["init"] = [dve(attn2_over + hg["free"], v.memset, hg["qL"], 0.0), dve([], v.memset, hg["kL"], 0.0)]
        hg["free"] += hg["init"]
        SC.wait(hg["free"])
        pending.append(meta_state())
        pending.extend(recurrence(pr) for pr in range(HB // 2))
        g2 = {}
        evac["ga"] = sigmoid_to(GA, F2M, f2[0], g2, "ga", attn2_over + [late_load] + list(qa_done.values()))
        seq["width"] = 1
        run(p2_ga)
        ya, yb = {}, {}
        evac["za"] = silu_times(QA, ya_done, F2M, f2[0], *hb, hb2_read, ya)
        run(p2_za)

        def evac_ba(g, m, ps, done):
            k = 4 * g + m
            g2["pa", k] = dve([done, g2["ga", k]], v.tensor_tensor, GA[:, k, :], ps, GA[:, k, :], ALU.mult)
            return [g2["pa", k]]

        evac["ba"] = evac_ba
        p2_ba.ready = lambda kt: ya[kt]
        run(p2_ba)
        while pending or active:
            pump()
        seq["width"] = 3
        tap("ob", QB, list(o_done.values()))
        evac["zb"] = silu_times(QB, o_done, F2M, f2[0], *hb_b, hb2_read, yb)
        run(p2_zb)
        GB = region(29, 16, KT, S)
        zb_read = zm_pool[7]
        rec_over = list(o_done.values()) + [(PE.sem, PE.count), (SC.sem, SC.count)]
        evac["gb"] = sigmoid_to(GB, F2M, f2[0], g2, "gb", rec_over)
        run(p2_gb)
        h2_read = [(PE.sem, PE.count)]
        mg2, gb_read = {}, []

        def evac_bb(g, m, ps, done):
            k = 4 * g + m
            s = scratch.next()
            z = s.ap[:, 0:S]
            tz = dve([done, g2["gb", k]] + s.free, v.tensor_tensor, z, ps, GB[:, k, :], ALU.mult)
            t = pool([tz, g2["pa", k]], gp.tensor_tensor, z, z, GA[:, k, :], ALU.add)
            gb_read[:] = [tz]
            mg2[k] = split_to(ob_hi[:, k, 0:S], ob_lo[:, k, 0:S], z, t, h2_read)
            s.free = mg2[k]
            return [tz]

        evac["bb"] = evac_bb
        p2_bb.ready = lambda kt: yb[kt]
        run(p2_bb)

        stores = []
        xT2 = region(29, 16, KT, S)
        x1_back = load(xT2.rearrange("p k n -> p (k n)"), x1_dram, [x1_kept, gb_read[0]])
        OT = region(0, 16, 2, D)
        bb_over = rec_over + [zb_read]

        def evac_w2(g, m, ps, done):
            k = 4 * g + m
            t = dve([done, x1_back], v.tensor_tensor, xT2[:, k, :], ps, xT2[:, k, :], ALU.add)
            final[k] = t
            if m == 3:
                def job():
                    for j in range(4):
                        kk = 4 * g + j
                        b = side_banks.next()
                        PE.wait(b.free + [final[kk]])
                        for blk in range(2):
                            i = nc.tensor.transpose(b.ap[:, blk * P:(blk + 1) * P], xT2[:, kk, blk * P:(blk + 1) * P],
                                                    c("ident"))
                        t1 = PE.mark(i)
                        t2 = act([t1, *bb_over], OT[:, :, kk * P:(kk + 1) * P],
                                 b.ap[:, 0:S].rearrange("p (b n) -> p b n", b=2), ACT.Copy)
                        b.free = [t2]
                    for blk in range(2):
                        stores.append(load(out[0, blk * P:(blk + 1) * P, g * 512:(g + 1) * 512],
                                           OT[:, blk, g * 512:(g + 1) * 512], [t2]))
                    yield
                pending.append(job())
            return [t]

        final = {}
        evac["wout2"] = evac_w2
        p2_w.ready = lambda kt: mg2[kt]
        run(p2_w)
        drain_jobs()
        SP.wait(stores)


_INS = ["x", "positions", "pre_norm_g", "w_in", "q_a_norm_g", "w_q_b", "kv_a_norm_g", "w_kv_b", "conv_w",
        "w_o_mla", "w_o_conv", "w_out", "post_norm_g", "meta_tokens_2", "hgrn_lb_logits_2", "norm_g_2",
        "w_in_2", "q_norm_g_2", "k_norm_g_2", "idx_k_norm_g_2", "hgrn_out_norm_g_2", "w_branch_2", "w_out_2"]
TAPS = None


def kernel(**inputs):
    import concourse.bacc as _bacc
    from concourse.bass_utils import run_bass_kernel_spmd as _run

    nc = _bacc.Bacc("TRN2", target_bir_lowering=False, num_devices=1)
    arrays, aps = {}, {}
    given = {name: np.ascontiguousarray(inputs[name]) for name in _INS}
    given["const_f"], given["const_lvl"] = CONST_F, CONST_LVL
    for name, arr in given.items():
        arrays[f"in_{name}"] = arr
        aps[name] = nc.dram_tensor(f"in_{name}", arr.shape, mybir.dt.from_np(arr.dtype), kind="ExternalInput").ap()
    out = nc.dram_tensor("out_0", (1, S, D), F32, kind="ExternalOutput").ap()
    build(nc, aps, out, TAPS)
    r = _run(nc, [arrays], core_ids=[0])
    return r.results[0]["out_0"]
```

```python
from collections import deque
from contextlib import ExitStack

import numpy as np

import concourse.bass as bass
from concourse import mybir

F32 = mybir.dt.float32
F32R = mybir.dt.float32r
I32 = mybir.dt.int32
U8 = mybir.dt.uint8
ALU = mybir.AluOpType
ACT = mybir.ActivationFunctionType
AX = mybir.AxisListType.X

P = 128
D = 2048
KT = D // P
S = 256
NMETA = 16
T = S + NMETA
EPS = 1e-6
NEG = -1e30

H1, DN, RD, DV, LORA = 16, 128, 64, 128, 512
C_QA, C_KV, C_KR = 0, LORA, 2 * LORA
C_ZMLA = 2 * LORA + RD
C_CIN, C_B, C_C, C_ZCONV, C_GMLA, C_GCONV = (C_ZMLA + D * i for i in range(1, 7))
SCALE1 = 1.0 / float(np.sqrt(DN + RD))

BW = D // 2
HA, KVA, HI, DI, HB = 8, 4, 16, 64, 8
CHUNK, TOPK = 64, 64
C2_QA, C2_KA, C2_VA, C2_ZA, C2_QI = 0, 1024, 1536, 2048, 3072
C2_KI, C2_WI, C2_QB, C2_FB, C2_IB, C2_ZB, C2_G = 4096, 4160, 4176, 5200, 6224, 7248, 8272
SCALE2 = float(P) ** -0.5
W_SCALE = HI ** -0.5 * DI ** -0.5
MASKED, TAKEN = -3.0e38, -3.3e38

UNIT = 1024
N_RAW, N_SPLIT, LEAD = 4, 3, 2

CONSTS = {}


def _constants():
    p = np.arange(P)
    parts, at = [], 0

    def put(name, a):
        nonlocal at
        a = np.asarray(a, np.float32).reshape(P, -1)
        CONSTS[name] = (at, at + a.shape[1])
        parts.append(a)
        at += a.shape[1]

    def rotation(group, half, copies):
        r = np.zeros((P, P))
        for m in range(P):
            o = m % group
            base = m - o if copies == 1 else 0
            if o < half:
                r[base + o + half, m] = -1.0
            elif o < 2 * half:
                r[base + o - half, m] = 1.0
        return r

    put("ident", np.eye(P))
    put("ones", np.ones((P, P)))
    put("rot_q1", rotation(RD, RD // 2, 1))
    put("dup64", p[:, None] == p[None, :] % 64)
    put("rot_k1", rotation(RD, RD // 2, 2))
    causal = np.where(p[None, :] <= p[:, None], 0.0, NEG)
    put("mask1", np.concatenate([np.zeros((P, P)), causal], 1))
    inv = 10000.0 ** (-(np.arange(RD // 2) * 2) / RD)
    put("inv_freq", inv.astype(np.float32)[p % 32])
    put("neg_half", np.full((P, 1), -0.5))
    put("pad", np.zeros((P, 2)))
    CONSTS["resident"] = (0, at)

    put("rot_a", rotation(P, 16, 1))
    put("rot_i", rotation(DI, 8, 2))
    put("rot_i1", rotation(DI, 8, 1))
    pos = np.arange(T, dtype=np.float32)

    def rope(group, half):
        o = p % group
        iv = np.power(np.float64(500000.0), -(o % half) * 2.0 / (2 * half)).astype(np.float32)
        ang = (pos[None, :] * iv[:, None]).astype(np.float32).astype(np.float64)
        on = (o < 2 * half)[:, None]
        return np.where(on, np.cos(ang), 1.0), np.where(on, np.sin(ang), 0.0)

    for name, (c, s) in (("a", rope(P, 16)), ("i", rope(DI, 8))):
        put("cos_" + name, c)
        put("sin_" + name, s)
    CONSTS["late"] = (CONSTS["resident"][1], at)
    f = np.concatenate(parts, 1)

    s, t = p[:, None], p[None, :]
    lv = [((s // (2 * h) == t // (2 * h)) & (s % (2 * h) < h) & (t % (2 * h) >= h)) for h in LEVELS]
    return np.ascontiguousarray(f), np.ascontiguousarray(np.concatenate(lv, 1).astype(np.float32))


LEVELS = (1, 2, 4, 8, 16, 32, 64)
CONST_F, CONST_LVL = _constants()

ROWS = {}
_at = 0
for _name, _n in (("pre", 16), ("post", 16), ("norm2", 16), ("conv", 48), ("qa", 4), ("kva", 4),
                  ("lb", 16), ("qn", 1), ("kn", 1), ("on", 1), ("ikn", 1)):
    ROWS[_name] = _at
    _at += _n
N_ROWS = _at


class Queue:

    def __init__(self, eng, sem):
        self.eng, self.sem, self.count, self.seen = eng, sem, 0, {}

    def wait(self, marks):
        for m in marks:
            if m is not None:
                sem, value = m
                if self.seen.get(sem.name, 0) < value:
                    self.eng.wait_ge(sem, value)
                    self.seen[sem.name] = value

    def mark(self, inst):
        inst.then_inc(self.sem, 1)
        self.count += 1
        return (self.sem, self.count)


class Slot:

    def __init__(self, ap):
        self.ap, self.marks, self.held = ap, [], False

    @property
    def free(self):
        return self.marks

    @free.setter
    def free(self, marks):
        self.marks, self.held = marks, False


class Ring:
    def __init__(self, aps):
        self.slots, self.i = [Slot(a) for a in aps], 0

    def next(self):
        s = self.slots[self.i % len(self.slots)]
        self.i += 1
        assert not s.held
        s.held = True
        return s


class Phase:

    def __init__(self, weight, groups, ktiles, hi, lo, n, evac, ready=(), period=1):
        self.order = lambda w, n: [(w, lambda x: x)]
        self.weight, self.groups, self.ktiles = weight, groups, ktiles
        self.hi, self.lo, self.n = hi, lo, n
        self.evac, self.ready, self.period = evac, ready, period


class Unit:
    def __init__(self, phase, g, k0, nk):
        self.phase, self.g, self.k0, self.nk = phase, g, k0, nk
        self.last = k0 + nk == phase.ktiles


def build(nc, a, out, taps=None):
    ctx = ExitStack()
    with ctx:
        def sb(name, shape, dt=F32):
            return ctx.enter_context(nc.sbuf_tensor(name, shape, dt))

        def sem(name):
            return ctx.enter_context(nc.semaphore(name))

        PE = Queue(nc.tensor, sem("pe_done"))
        SC = Queue(nc.scalar, sem("act_done"))
        VE = Queue(nc.vector, sem("dve_done"))
        GP = Queue(nc.gpsimd, sem("pool_done"))
        SP = Queue(nc.sync, None)

        def act(waits, *args, **kw):
            SC.wait(waits)
            return SC.mark(nc.scalar.activation(*args, **kw))

        def dve(waits, op, *args, **kw):
            VE.wait(waits)
            return VE.mark(op(*args, **kw))

        def pool(waits, op, *args, **kw):
            GP.wait(waits)
            return GP.mark(op(*args, **kw))

        v, gp = nc.vector, nc.gpsimd

        def pe_t(waits, dst, src, ident):
            PE.wait(waits)
            return nc.tensor.transpose(dst, src, ident)

        def mm(dst, lhsT, rhs, start=True, stop=True):
            return nc.tensor.matmul(dst, lhsT, rhs, start=start, stop=stop, skip_group_check=True)

        loads = [0]

        def load(dst, src, waits=(), q=None):
            q = q or SP
            q.wait(waits)
            loads[0] += 1
            s = sem(f"load{loads[0]}")
            q.eng.dma_start(dst, src).then_inc(s, 16)
            return (s, 16)

        raw = sb("w_raw", [P, N_RAW, UNIT])
        whi = sb("w_hi", [P, N_SPLIT, UNIT], F32R)
        wlo = sb("w_lo", [P, N_SPLIT, UNIT], F32R)
        hb_hi = sb("hb_hi", [P, KT, S], F32R)
        hb_lo = sb("hb_lo", [P, KT, S], F32R)
        ob_hi = sb("ob_hi", [P, KT, T], F32R)
        ob_lo = sb("ob_lo", [P, KT, T], F32R)
        arena = sb("arena", [P, 72 * 256])
        con = sb("con", [P, CONSTS["resident"][1]])
        cols = sb("cols", [P, P])
        rope1 = sb("rope1", [P, 2, S])
        factor = sb("factor", [P, 3, T])
        small = sb("small", [P, 256])
        scratch = Ring([sb(f"scratch{i}", [P, T])[:, :] for i in range(5)])
        head_factors = Ring([sb(f"head_factor{i}", [P, T])[:, :] for i in range(3)])
        acc_a, acc_b = sb("acc_a", [P, S])[:, :], sb("acc_b", [P, S])[:, :]
        psum = [ctx.enter_context(nc.psum_tensor(f"bank{i}", [P, 512], F32)) for i in range(8)]
        stats = Ring([sb(f"stats{i}", [P, 8])[:, :] for i in range(6)])
        proj_banks = Ring([b[:, :] for b in psum[:5]])
        side_banks = Ring([b[:, :] for b in psum[5:]])

        def region(kb0, kb, *shape):
            n = int(np.prod(shape))
            assert n <= 256 * kb
            at = int(kb0 * 256)
            ap = arena[:, at:at + n]
            if len(shape) == 1:
                return ap
            if len(shape) == 2:
                return ap.rearrange("p (a b) -> p a b", a=shape[0])
            return ap.rearrange("p (a b c) -> p a b c", a=shape[0], b=shape[1])

        def c(name):
            lo, hi = CONSTS[name]
            return con[:, lo:hi]

        def col(name, i=0):
            j = ROWS[name] + i
            return cols[:, j:j + 1]

        def tap(name, ap, waits):
            if taps is not None and name in taps:
                d = nc.dram_tensor("tap_" + name, [ap.shape[0], int(np.prod(ap.shape[1:]))], F32, kind="ExternalOutput").ap()
                allm = [(q.sem, q.count) for q in (PE, SC, VE, GP) if q.count]
                t = load(d, ap.rearrange("p a b -> p (a b)") if len(ap.shape) == 3 else ap, allm)
                for q in (SP, PE, SC, VE, GP):
                    q.wait([t])

        units = []
        raw_sem = [sem(f"raw{i}") for i in range(N_RAW)]
        raw_free = [None] * N_RAW
        split_free = [None] * N_SPLIT
        split_done = {}
        landed = {}
        issued = [0, 0]

        def plan(phase):
            phase.first = len(units)
            for g, (c0, nc_, tiles) in enumerate(phase.groups):
                step = min(UNIT // nc_, phase.ktiles)
                for k0 in range(0, phase.ktiles, step):
                    units.append(Unit(phase, g, k0, step))
            phase.end = len(units)
            return phase

        def size(u):
            c0, n, _ = u.phase.groups[u.g]
            return c0, n, u.nk * n

        def issue_load():
            i = issued[0]
            if i >= len(units):
                return
            issued[0] += 1
            u, s = units[i], i % N_RAW
            c0, n, sz = size(u)
            SP.wait([raw_free[s]])
            src = u.phase.weight.rearrange("(k p) n -> p k n", p=P)[:, u.k0:u.k0 + u.nk, c0:c0 + n]
            dst = raw[:, s, 0:sz].rearrange("p (k n) -> p k n", k=u.nk)
            nc.sync.dma_start(dst, src).then_inc(raw_sem[s], 16)
            landed[i] = (raw_sem[s], 16 * (i // N_RAW + 1))

        def issue_split():
            i = issued[1]
            if i >= len(units):
                return
            issued[1] += 1
            s, r = i % N_SPLIT, i % N_RAW
            _, _, sz = size(units[i])
            for src, dst in units[i].phase.order(raw[:, r, 0:sz], sz):
                hi = act([landed[i], split_free[s]], dst(whi[:, s, 0:sz]), src, ACT.Copy)
                lo = dve([hi, split_free[s]], v.tensor_tensor, dst(wlo[:, s, 0:sz]), src,
                         dst(whi[:, s, 0:sz]).bitcast(F32), ALU.subtract)
            raw_free[r] = lo
            split_done[i] = [hi, lo]
            issue_load()

        pending, active = deque(), []
        deferred = deque()
        seq = {"width": 3}

        def pump():
            for job in list(active):
                if next(job, "end") == "end":
                    active.remove(job)
            if pending and len(active) < seq["width"]:
                job = pending.popleft()
                active.append(job)
                if next(job, "end") == "end":
                    active.remove(job)

        def drain_jobs():
            flush()
            while pending or active:
                pump()

        def run(phase):
            banks = {}
            for i in range(phase.first, phase.end):
                while issued[1] <= min(i + LEAD, len(units) - 1):
                    issue_split()
                u, s = units[i], i % N_SPLIT
                c0, n, sz = size(u)
                tiles = phase.groups[u.g][2]
                hi_w = whi[:, s, 0:sz].rearrange("p (k n) -> p k n", k=u.nk)
                lo_w = wlo[:, s, 0:sz].rearrange("p (k n) -> p k n", k=u.nk)
                PE.wait(split_done.pop(i))
                for m, tile in enumerate(tiles):
                    if u.k0 == 0:
                        banks[m] = proj_banks.next()
                        PE.wait(banks[m].free)
                    dst = banks[m].ap[:, 0:phase.n]
                    for k in range(u.nk):
                        kt = u.k0 + k
                        PE.wait(phase.ready(kt) if callable(phase.ready) else phase.ready)
                        x_hi, x_lo = phase.hi(kt), phase.lo(kt)
                        first, last = kt == 0, kt == phase.ktiles - 1
                        mm(dst, tile(hi_w[:, k, :]), x_hi, first, False)
                        mm(dst, tile(hi_w[:, k, :]), x_lo, False, False)
                        inst = mm(dst, tile(lo_w[:, k, :]), x_hi, False, last)
                    if u.last or m == len(tiles) - 1:
                        done = PE.mark(inst)
                    for d in deferred:
                        d[0] -= 1
                    due = [d for d in deferred if d[0] <= 0]
                    for d in due:
                        deferred.remove(d)
                        d[1]()
                    if u.last:
                        banks[m].free = phase.evac(u.g, m, dst, done)
                split_free[s] = done
                if (i - phase.first) % phase.period == phase.period - 1:
                    pump()

        def later(step, tiles=4):
            deferred.append([tiles, step])

        def flush():
            while deferred:
                deferred.popleft()[1]()

        def plain(c0, groups, cols_=512):
            tiles = [(lambda w, m=m: w[:, m * P:(m + 1) * P]) for m in range(cols_ // P)]
            return [(c0 + g * cols_, cols_, tiles) for g in range(groups)]

        def row_factor(squares, done, n, width, rows=P):
            starts = [0] if width < P else list(range(0, width - P + 1, P))
            if width > P and width % P:
                starts.append(width - P)
            m = min(width, P)
            st, b = stats.next(), side_banks.next()
            PE.wait(b.free + [done])
            for j, lo in enumerate(starts):
                t = mm(b.ap[0:m, j:j + 1], squares[0:rows, lo:lo + m], c("ones")[0:rows, 0:1])
            t = PE.mark(t)
            f = st.ap[0:m, 0:len(starts)]
            t = dve([t] + st.free, v.tensor_scalar, f, b.ap[0:m, 0:len(starts)], 1.0 / n, EPS, ALU.mult, ALU.add)
            b.free = [t]
            t = pool([t], gp.tensor_tensor, f, f, c("neg_half")[0:m, :].to_broadcast([m, len(starts)]), ALU.pow)
            at = 0
            for j, lo in enumerate(starts):
                new = lo + m - at
                t1 = dve([t], v.tensor_scalar, squares[0:m, at:at + new], c("ident")[0:m, m - new:m],
                         st.ap[0:m, j:j + 1], None, ALU.mult)
                at += new
            st.free = [t1]
            yield
            b = side_banks.next()
            PE.wait(b.free + [t1])
            at = 0
            for lo in starts:
                new = lo + m - at
                t = mm(b.ap[:, at:at + new], c("ones")[0:m, :], squares[0:m, at:at + new])
                at += new
            return b, PE.mark(t)

        def factor_job(dst, squares, done, n, width, marks, free=(), delay=0):
            for _ in range(delay):
                yield
            b, t = yield from row_factor(squares, done, n, width)
            marks.append(dve([t, *free], v.tensor_copy, dst, b.ap[:, 0:width]))
            b.free = [marks[-1]]

        def add_square(acc, x, x_done, prev, w=S):
            if prev is None:
                return act([x_done], acc, x, ACT.Square)
            sq = scratch.next()
            t = act([x_done] + sq.free, sq.ap[:, 0:w], x, ACT.Square)
            t = pool([t, prev], gp.tensor_tensor, acc, acc, sq.ap[:, 0:w], ALU.add)
            sq.free = [t]
            return t

        def split_to(dst_hi, dst_lo, src, src_done, free, gain=None):
            if gain is None:
                hi = act(free + [src_done], dst_hi, src, ACT.Copy)
                lo = dve([hi, src_done], v.tensor_tensor, dst_lo, src, dst_hi.bitcast(F32), ALU.subtract)
            else:
                hi = act(free + [src_done], dst_hi, src, ACT.Copy, scale=gain)
                lo = dve([hi, src_done], v.scalar_tensor_tensor, dst_lo, src, gain, dst_hi.bitcast(F32),
                         ALU.mult, ALU.subtract)
            return [hi, lo]

        Q1, QR, K1, V1, G1 = (region(0, 16, H1, S), region(16, 8, H1 // 2, S), region(24, 16, H1, S),
                              region(40, 16, 2, D), region(56, 16, KT, S))
        LAT = V1[:, 0, :].rearrange("p (k n) -> p k n", k=8)
        OUT1 = region(40, 16, KT, S)
        GM = K1
        x_in = region(0, 16, 2, D)
        x_meta = region(16, 8, D)
        xT = G1
        XR = region(24, 16, KT, S)
        kr1 = sb("kr1", [P, S])
        prob = Ring([sb(f"prob{i}", [P, 416])[:, :] for i in range(2)])
        probT = Ring([sb(f"probT{i}", [P, 384])[:, :] for i in range(2)])

        hb = (lambda k: hb_hi[:, k, :], lambda k: hb_lo[:, k, :])
        ob = (lambda k: ob_hi[:, k, 0:S], lambda k: ob_lo[:, k, 0:S])
        ob_kv = (lambda k: ob_hi[:, k + 4, 0:S], lambda k: ob_lo[:, k + 4, 0:S])
        ob_main = (lambda k: ob_hi[:, k, NMETA:T], lambda k: ob_lo[:, k, NMETA:T])
        ob_all = (lambda k: ob_hi[:, k, :], lambda k: ob_lo[:, k, :])
        hb_b = (lambda k: hb_hi[:, k + 8, :], lambda k: hb_lo[:, k + 8, :])
        w1, w2 = a["w_in"], a["w_in_2"][0]
        HD = DN + RD

        def pair_order(w, n):
            view = w.rearrange("p (k h x) -> p k h x", h=2, x=HD)
            out_ = []
            for lo, hi, at in ((0, DN, 0), (DN, HD, 2 * DN)):
                out_.append((view[:, :, :, lo:hi],
                             lambda x, lo=lo, hi=hi, at=at: x.rearrange("p (k y) -> p k y", y=2 * HD)
                             [:, :, at:at + 2 * (hi - lo)].rearrange("p k (h x) -> p k h x", h=2)))
            return out_

        pair = plain(0, 1, 384)[0][2]
        one = [lambda w: w[:, 0:P]]

        evac = {}

        def ph(name, *args, **kw):
            p_ = Phase(*args, evac=lambda *e: evac[name](*e), **kw)
            return plan(p_)

        p_qa = ph("qa", w1, plain(C_QA, 1), KT, *hb, S)
        p_kv = ph("kva", w1, plain(C_KV, 1), KT, *hb, S)
        p_kr = ph("kr", w1, [(C_KR, P, one)], KT, *hb, S)
        p_q = ph("q", a["w_q_b"], [(g * 384, 384, pair) for g in range(8)], 4, *ob, S)
        p_q.order = pair_order
        p_k = ph("kv", a["w_kv_b"], plain(0, 8), 4, *ob_kv, S)
        p_conv = []
        for j in range(4):
            for name, c0 in (("cin", C_CIN), ("cgate", C_C), ("bgate", C_B), ("zconv", C_ZCONV)):
                p_conv.append((j, ph(f"{name}{j}", w1, plain(c0 + 512 * j, 1), KT, *hb, S, period=3)))
        p_gc = ph("gconv", w1, plain(C_GCONV, 4), KT, *hb, S)
        p_oc = ph("oconv", a["w_o_conv"], plain(0, 4), KT, *ob, S)
        p_zm = ph("zmla", w1, plain(C_ZMLA, 4), KT, *hb, S)
        p_gm = ph("gmla", w1, plain(C_GMLA, 4), KT, *hb, S)
        p_om = ph("omla", a["w_o_mla"], plain(0, 4), KT, *ob, S)
        p_w = ph("wout", a["w_out"], plain(0, 4), KT, *hb, S)
        p2_qi = ph("qi", w2, plain(C2_QI, 2), KT, *ob_main, S)
        p2_ki = ph("ki", w2, [(C2_KI, P, one)], KT, *ob_all, T)
        p2_ka = ph("ka", w2, plain(C2_KA, 1), KT, *ob_all, T)
        p2_va = ph("va", w2, plain(C2_VA, 1), KT, *ob_all, T)
        p2_qa = ph("qa2", w2, plain(C2_QA, 2), KT, *ob_main, S)
        p2_fb = ph("fb", w2, plain(C2_FB, 2), KT, *ob_all, T)
        p2_ib = ph("ib", w2, plain(C2_IB, 2), KT, *ob_all, T)
        p2_qb = ph("qb", w2, plain(C2_QB, 2), KT, *ob_main, S)
        p2_ga = ph("ga", w2, plain(C2_G, 4), KT, *ob_main, S)
        p2_za = ph("za", w2, plain(C2_ZA, 2), KT, *ob_main, S)
        p2_ba = ph("ba", a["w_branch_2"][0, 0], plain(0, 4), 8, *hb, S)
        p2_zb = ph("zb", w2, plain(C2_ZB, 2), KT, *ob_main, S)
        p2_gb = ph("gb", w2, plain(C2_G + D, 4), KT, *ob_main, S)
        p2_bb = ph("bb", a["w_branch_2"][0, 1], plain(0, 4), 8, *hb_b, S)
        p2_w = ph("wout2", a["w_out_2"][0], plain(0, 4), KT, *ob, S)

        x_load = [load(x_in[:, b, :], a["x"][0, b * P:(b + 1) * P, :], q=SC) for b in range(2)]
        con_load = load(con[:, :], a["const_f"][:, 0:CONSTS["resident"][1]])
        rows_in = region(24, 1, P)
        row_loads = []

        def rows_of(name, src, n):
            r = ROWS[name]
            row_loads.append(load(rows_in[r:r + n, 0:src.shape[1]], src, [rows_zero]))

        rows_zero = dve([], v.memset, rows_in, 0.0)
        r128 = lambda ap: ap.rearrange("(k p) -> k p", p=P)
        rows_of("pre", r128(a["pre_norm_g"]), 16)
        for _ in range(N_RAW):
            issue_load()
        rows_of("post", r128(a["post_norm_g"]), 16)
        rows_of("norm2", r128(a["norm_g_2"][0]), 16)
        rows_of("conv", a["conv_w"].rearrange("c (k p) -> (c k) p", p=P), 48)
        rows_of("qa", r128(a["q_a_norm_g"]), 4)
        rows_of("kva", r128(a["kv_a_norm_g"]), 4)
        rows_of("lb", a["hgrn_lb_logits_2"].rearrange("l (k p) -> (l k) p", p=P), 16)
        rows_of("qn", a["q_norm_g_2"], 1)
        rows_of("kn", a["k_norm_g_2"], 1)
        rows_of("on", a["hgrn_out_norm_g_2"], 1)
        rows_of("ikn", a["idx_k_norm_g_2"], 1)
        pos_i = region(25, 1, S)[0:1, :].bitcast(I32)
        pos_load = load(pos_i, a["positions"])
        meta_load = load(x_meta[0:NMETA, :], a["meta_tokens_2"])

        b = side_banks.next()
        PE.wait([con_load, rows_zero, *row_loads])
        t = PE.mark(nc.tensor.transpose(b.ap[:, 0:P], rows_in, c("ident")))
        cols_done = dve([t], v.tensor_copy, cols[:, :], b.ap[:, 0:P])
        b.free = [cols_done]

        x_marks, h_marks = [], []
        for k in range(KT):
            b = proj_banks.next()
            PE.wait([con_load, *x_load, *b.free])
            for blk in range(2):
                t = nc.tensor.transpose(b.ap[:, blk * P:(blk + 1) * P], x_in[:, blk, k * P:(k + 1) * P], c("ident"))
            t = PE.mark(t)
            x_marks.append(dve([t], v.tensor_copy, xT[:, k, :], b.ap[:, 0:S]))
            b.free = [x_marks[-1]]
            h_marks.append(split_to(hb_hi[:, k, :], hb_lo[:, k, :], xT[:, k, :], x_marks[-1], [cols_done],
                                    gain=col("pre", k)))
            x_sq = add_square(acc_b, xT[:, k, :], x_marks[-1], x_sq if k else None)
        x_in_free = t
        r1_marks = []
        pending.append(factor_job(factor[:, 0, 0:S], acc_b, x_sq, D, S, r1_marks, delay=4))
        h_ready = lambda kt: h_marks[kt]

        pos_f = small[0:1, 0:S]
        tp = dve([pos_load], v.tensor_copy, pos_f, pos_i)
        bp = side_banks.next()
        PE.wait([tp, con_load, *bp.free])
        tp = PE.mark(mm(bp.ap[:, 0:S], c("ones")[0:1, :], pos_f))
        ang, turns = scratch.next(), scratch.next()
        ta = dve([tp] + ang.free, v.tensor_scalar, ang.ap[:, 0:S], bp.ap[:, 0:S], c("inv_freq"), None, ALU.mult)
        bp.free = [ta]
        MAGIC = 1.5 * 2.0 ** 23
        rope_done = []
        for which, shift in ((1, 0.0), (0, 0.25)):
            dst = rope1[:, which, :]
            k_ = turns.ap[:, 0:S]
            tk = dve([ta] + rope_done + turns.free, v.tensor_scalar, k_, ang.ap[:, 0:S], 1.0 / (2 * np.pi), shift, ALU.mult, ALU.add)
            tk = dve([tk], v.tensor_scalar, k_, k_, MAGIC, MAGIC, ALU.add, ALU.subtract)
            tk = dve([tk], v.scalar_tensor_tensor, dst, k_, -6.28125, ang.ap[:, 0:S], ALU.mult, ALU.add)
            tk = dve([tk], v.scalar_tensor_tensor, dst, k_, -0.0019350051879882812, dst, ALU.mult, ALU.add)
            tk = dve([tk], v.scalar_tensor_tensor, dst, k_, -3.0199159819e-07, dst, ALU.mult, ALU.add)
            if shift:
                tk = dve([tk], v.tensor_scalar, dst, dst, np.pi / 2, None, ALU.add)
            tk = dve([tk], v.tensor_scalar, dst, dst, 3.14159250, -3.14159250, ALU.min, ALU.max)
            rope_done = [act([tk], dst, dst, ACT.Sin)]
        ang.free = turns.free = rope_done
        cos1, sin1 = rope1[:, 0, :], rope1[:, 1, :]
        tap("rope1", rope1[:, :, :], rope_done)

        small2, small3 = sb("small2", [P, 64]), sb("small3", [P, 2 * HI])
        lbx, lb, oml = small2[:, 16:32], small2[:, 0:8], small2[:, 8:16]
        l0, l1 = cols[:, ROWS["lb"]:ROWS["lb"] + 8], cols[:, ROWS["lb"] + 8:ROWS["lb"] + 16]
        mx = small2[:, 32:40]
        tl = dve([cols_done], v.tensor_tensor, mx, l0, l1, ALU.max)
        tl = dve([tl], v.tensor_tensor, lbx[:, 0:8], l0, mx, ALU.subtract)
        tl = dve([tl], v.tensor_tensor, lbx[:, 8:16], l1, mx, ALU.subtract)
        tl = act([tl], lbx, lbx, ACT.Exp)
        tl = dve([tl], v.tensor_tensor, mx, lbx[:, 0:8], lbx[:, 8:16], ALU.add)
        tl = dve([tl], v.reciprocal, mx, mx)
        tl1 = dve([tl], v.tensor_tensor, lb, lbx[:, 0:8], mx, ALU.mult)
        lb_done = dve([tl1], v.tensor_tensor, oml, lbx[:, 8:16], mx, ALU.mult)

        R_, RR, RQ = factor[:, 0, 0:S], factor[:, 1, 0:S], factor[:, 2, 0:S]
        RKV = RR

        lat_marks = {}
        lat_sq = {}
        rq_done, rkv_done = [], []

        def latent(which, base, gname, done_list, dst_factor):
            def f(g, m, ps, done):
                x = LAT[:, base + m, :]
                t = dve([done, r1_marks[0]], v.tensor_tensor, x, ps, R_, ALU.mult)
                acc = acc_a if which == "q" else acc_b
                tq = lat_sq[which] = add_square(acc, x, t, lat_sq.get(which))

                def split():
                    lat_marks[which, m] = split_to(ob_hi[:, base + m, 0:S], ob_lo[:, base + m, 0:S], x, t, [],
                                                   gain=col(gname, m))
                later(split)
                if m == 3:
                    pending.append(factor_job(dst_factor, acc, tq, LORA, S, done_list))
                return [t]
            return f

        evac["qa"] = latent("q", 0, "qa", rq_done, RQ)
        evac["kva"] = latent("kv", 4, "kva", rkv_done, RKV)

        kr_done = []

        def rope_tile(x, x_done, rot, cos, sin, rope_ready, width, dup=None, rows=P):
            b = side_banks.next()
            PE.wait(b.free + [x_done] + rope_ready)
            t = PE.mark(mm(b.ap[:, 0:width], rot[0:rows, :], x[0:rows, :]))
            s = scratch.next()
            t1 = dve([t] + s.free + rope_ready, v.tensor_tensor, s.ap[:, 0:width], b.ap[:, 0:width], sin, ALU.mult)
            b.free = [t1]
            if dup is not None:
                b = side_banks.next()
                PE.wait(b.free)
                t = PE.mark(mm(b.ap[:, 0:width], dup[0:rows, :], x[0:rows, :]))
                t2 = dve([t], v.tensor_tensor, x, b.ap[:, 0:width], cos, ALU.mult)
                b.free = [t2]
            else:
                t2 = pool([x_done, t] + rope_ready, gp.tensor_tensor, x, x, cos, ALU.mult)
            t = pool([t1, t2], gp.tensor_tensor, x, x, s.ap[:, 0:width], ALU.add)
            s.free = [t]
            return t

        def evac_kr(g, m, ps, done):
            t = dve([done], v.tensor_tensor, kr1[:, :], ps, R_, ALU.mult)

            def job():
                yield
                kr_done.append(rope_tile(kr1[:, :], t, c("rot_k1"), cos1, sin1, rope_done, S, dup=c("dup64")))
                tap("kr1", kr1[:, :], kr_done)
            pending.append(job())
            return [t]

        evac["kr"] = evac_kr
        q_done, qr_done, k_done, v_done, v_read = {}, {}, {}, {}, {}

        def evac_q(g, m, ps, done):
            if m < 2:
                h = 2 * g + m
                t = q_done[h] = dve([done, x_in_free, *rq_done], v.tensor_tensor, Q1[:, h, :], ps, RQ, ALU.mult)
                return [t]
            t = dve([done, meta_free], v.tensor_tensor, QR[:, g, :], ps, RQ, ALU.mult)

            def job():
                yield
                qr_done[g] = rope_tile(QR[:, g, :], t, c("rot_q1"), cos1, sin1, rope_done, S)
                yield
            pending.append(job())
            return [t]

        evac["q"] = evac_q

        def evac_kvb(g, m, ps, done):
            h = 2 * g + m // 2
            if m % 2 == 0:
                t = k_done[h] = dve([done, *rkv_done, cols_done], v.tensor_tensor, K1[:, h, :], ps, RKV, ALU.mult)
                return [t]
            s = scratch.next()
            t = v_read[h] = dve([done, *rkv_done] + s.free, v.tensor_tensor, s.ap[:, 0:S], ps, RKV, ALU.mult)

            def job():
                b = side_banks.next()
                PE.wait(b.free + [t])
                for blk in range(2):
                    i = nc.tensor.transpose(b.ap[:, blk * P:(blk + 1) * P], s.ap[:, blk * P:(blk + 1) * P], c("ident"))
                t2 = PE.mark(i)
                s.free = [t2]
                v_done[h] = act([t2, lat_free], V1[:, :, h * P:(h + 1) * P],
                                b.ap[:, 0:S].rearrange("p (b n) -> p b n", b=2), ACT.Copy)
                b.free = [v_done[h]]
            later(job, 2)
            return [t]

        evac["kv"] = evac_kvb

        attn_done = {}

        def attention1(h):
            half = 64 * (h % 2)
            kr, qr = kr1[half:half + 64, :], QR[half:half + 64, h // 2, :]
            b = side_banks.next()
            PE.wait(b.free + [q_done[h], qr_done[h // 2], k_done[h], *kr_done])
            mm(b.ap[:, 0:P], Q1[:, h, 0:P], K1[:, h, 0:P], True, False)
            mm(b.ap[:, 0:P], qr[:, 0:P], kr[:, 0:P], False, True)
            mm(b.ap[:, P:3 * P], Q1[:, h, P:S], K1[:, h, :], True, False)
            t = PE.mark(mm(b.ap[:, P:3 * P], qr[:, P:S], kr, False, True))
            p, st = prob.next(), stats.next()
            dve([t] + p.free, v.scalar_tensor_tensor, p.ap[:, 0:P], b.ap[:, 0:P], SCALE1, c("mask1")[:, P:S],
                ALU.mult, ALU.add)
            t = dve([], v.scalar_tensor_tensor, p.ap[:, P:384], b.ap[:, P:384], SCALE1, c("mask1"),
                    ALU.mult, ALU.add)
            b.free = [t]
            parts = ((0, P), (P, 3 * P))
            done = softmax(p, st, parts, t)
            yield
            pt = probT.next()
            b = side_banks.next()
            PE.wait(b.free + done)
            for j in range(3):
                i = nc.tensor.transpose(b.ap[:, j * P:(j + 1) * P], p.ap[:, j * P:(j + 1) * P], c("ident"))
            t = PE.mark(i)
            p.free = [t]
            t = act([t] + pt.free, pt.ap[:, 0:384], b.ap[:, 0:384], ACT.Copy)
            b.free = [t]
            yield
            b = side_banks.next()
            PE.wait(b.free + [t, v_done[h]])
            mm(b.ap[:, 0:S], V1[:, 0, h * P:(h + 1) * P], pt.ap[:, 0:S], True, False)
            t = PE.mark(mm(b.ap[:, P:S], V1[:, 1, h * P:(h + 1) * P], pt.ap[:, S:384], False, True))
            pt.free = [t]
            attn_done[h] = act([t], Q1[:, h, :], b.ap[:, 0:S], ACT.Copy)
            b.free = [attn_done[h]]

        def softmax(p, st, parts, t):
            n = len(parts)
            tm = [dve([t] + st.free, v.tensor_reduce, st.ap[:, i:i + 1], p.ap[:, lo:hi], AX, ALU.max, negate=True)
                  for i, (lo, hi) in enumerate(parts)]
            te = [act([tm[i]], p.ap[:, lo:hi], p.ap[:, lo:hi], ACT.Exp, bias=st.ap[:, i:i + 1],
                      accum_out=st.ap[:, 2 + i:3 + i]) for i, (lo, hi) in enumerate(parts)]
            tr = dve(te, v.reciprocal, st.ap[:, 4:4 + n], st.ap[:, 2:2 + n])
            done = [dve([tr], v.tensor_scalar, p.ap[:, lo:hi], p.ap[:, lo:hi], st.ap[:, 4 + i:5 + i], None, ALU.mult)
                    for i, (lo, hi) in enumerate(parts)]
            st.free = done
            return done

        metaT = small
        b = side_banks.next()
        PE.wait([meta_load, con_load, *b.free])
        for k in range(KT):
            i = nc.tensor.transpose(b.ap[:, k * NMETA:(k + 1) * NMETA], x_meta[0:NMETA, k * P:(k + 1) * P],
                                    c("ident")[0:NMETA, 0:NMETA])
        t = PE.mark(i)
        meta_free = t
        meta_done = act([t, tp], metaT[:, :], b.ap[:, 0:KT * NMETA], ACT.Copy)
        b.free = [meta_done]

        conv_t, cin_t = {}, {}
        u_t, gate_t = region(56, 4, 4, S), region(60, 4, 4, S)
        oc_marks = {}

        def conv_evacs(j):
            def cin(g, m, ps, done):
                cin_t[m] = dve([done, rr_done, *conv_free[m]], v.tensor_tensor, gate_t[:, m, :], ps, RR, ALU.mult)
                return [cin_t[m]]

            def cgate(g, m, ps, done):
                k = 4 * j + m
                s = scratch.next()
                u, y = s.ap[:, 0:S], u_t[:, m, :]
                tu = dve([done, cin_t[m]] + s.free, v.tensor_tensor, u, ps, gate_t[:, m, :], ALU.mult)
                t1 = act([tu, *conv_free[m]], y, u, ACT.Copy, scale=col("conv", 32 + k))

                def taps():
                    t = dve([t1, tu], v.scalar_tensor_tensor, y[:, 1:S], u[:, 0:S - 1], col("conv", 16 + k),
                            y[:, 1:S], ALU.mult, ALU.add)
                    t = dve([t], v.scalar_tensor_tensor, y[:, 2:S], u[:, 0:S - 2], col("conv", k), y[:, 2:S],
                            ALU.mult, ALU.add)
                    s.free = [t]
                    conv_t[m] = t
                later(taps, 1)
                return [tu]

            def bgate(g, m, ps, done):
                y = u_t[:, m, :]
                t = dve([done, conv_t[m]], v.tensor_tensor, y, ps, y, ALU.mult)
                conv_t[m] = pool([t], gp.tensor_tensor, y, y, R_, ALU.mult)
                return [t]

            def zconv(g, m, ps, done):
                k = 4 * j + m
                y = u_t[:, m, :]
                s, s2 = scratch.next(), scratch.next()
                z, sg = s.ap[:, 0:S], s2.ap[:, 0:S]
                tz = dve([done] + s.free, v.tensor_tensor, z, ps, R_, ALU.mult)
                t = act([tz] + s2.free, sg, z, ACT.Sigmoid)
                t = pool([t, tz], gp.tensor_tensor, z, z, sg, ALU.mult)
                s2.free = [t]
                t = pool([t, conv_t[m]], gp.tensor_tensor, y, z, y, ALU.mult)
                s.free = [t]

                def split():
                    conv_free[m] = oc_marks[k] = split_to(ob_hi[:, k, 0:S], ob_lo[:, k, 0:S], y, t, lat_read)
                later(split)
                return [tz]
            return cin, cgate, bgate, zconv

        conv_free = {m: [x_sq, *h_marks[KT - 1]] for m in range(4)}

        for ph_ in (p_qa, p_kv, p_kr, *[x for _, x in p_conv], p_gc, p_zm, p_gm):
            ph_.ready = h_ready
        run(p_qa)
        run(p_kv)
        run(p_kr)
        flush()
        p_q.ready = lambda kt: lat_marks["q", kt]
        p_k.ready = lambda kt: lat_marks["kv", kt]
        run(p_q)
        tap("Q1", Q1, [q_done[15]])
        lat_free = lat_marks["kv", 3][1]
        run(p_k)
        flush()
        rr_done = pool([r1_marks[0], k_done[15], v_read[15]], gp.tensor_tensor, RR, R_, R_, ALU.mult)
        lat_read = [(PE.sem, PE.count)]
        tap("QR", QR, [qr_done[7]])
        tap("K1", K1, [k_done[15]])
        tap("V1", V1, [v_done[15]])
        pending.extend(attention1(h) for h in range(H1))
        for j, p_ in p_conv:
            for name, f in zip(("cin", "cgate", "bgate", "zconv"), conv_evacs(j)):
                evac[f"{name}{j}"] = f
            run(p_)
        if pending or active:
            drain_jobs()
        tap("attn1", Q1, [attn_done[15]])

        def sigmoid_to(dst, factor_, fdone, marks, key, free=()):
            def f(g, m, ps, done):
                k = 4 * g + m
                s = scratch.next()
                tz = dve([done, fdone] + s.free, v.tensor_tensor, s.ap[:, 0:S], ps, factor_, ALU.mult)
                marks[key, k] = act([tz, *free], dst[:, k, :], s.ap[:, 0:S], ACT.Sigmoid)
                s.free = [marks[key, k]]
                return [tz]
            return f

        gate = {}
        evac["gconv"] = sigmoid_to(G1, R_, r1_marks[0], gate, "gc", sum(conv_free.values(), []))
        run(p_gc)

        def evac_oc(g, m, ps, done):
            k = 4 * g + m
            gate["yc", k] = dve([done, gate["gc", k]], v.tensor_tensor, G1[:, k, :], ps, G1[:, k, :], ALU.mult)
            return [gate["yc", k]]

        evac["oconv"] = evac_oc
        flush()
        p_oc.ready = lambda kt: oc_marks[kt]
        run(p_oc)
        oc_read = [(PE.sem, PE.count)]
        tap("yconv", G1, [gate["yc", 15]])
        zm, zm_pool, zm_read = {}, {}, []

        def silu_times(y, y_marks, factor_, fdone, dst_hi, dst_lo, free, marks):
            def f(g, m, ps, done):
                k = 4 * g + m
                s, s2 = scratch.next(), scratch.next()
                z, sg = s.ap[:, 0:S], s2.ap[:, 0:S]
                tz = dve([done, fdone] + s.free, v.tensor_tensor, z, ps, factor_, ALU.mult)
                t = act([tz] + s2.free, sg, z, ACT.Sigmoid)
                t = pool([t, tz], gp.tensor_tensor, z, z, sg, ALU.mult)
                s2.free = [t]
                t = zm_pool[k] = pool([t, y_marks[k]], gp.tensor_tensor, y[:, k, :], z, y[:, k, :], ALU.mult)
                s.free = [t]

                def split():
                    marks[k] = split_to(dst_hi(k), dst_lo(k), y[:, k, :], t, free)
                    zm_read[:] = marks[k]
                later(split)
                return [tz]
            return f

        evac["zmla"] = silu_times(Q1, attn_done, R_, r1_marks[0], *ob, oc_read, zm)
        run(p_zm)
        evac["gmla"] = sigmoid_to(GM, R_, r1_marks[0], gate, "gm", list(attn_done.values()))
        run(p_gm)
        hb_read = [(PE.sem, PE.count)]
        mg, gm_read = {}, []

        def evac_om(g, m, ps, done):
            k = 4 * g + m
            s = scratch.next()
            z, y = s.ap[:, 0:S], G1[:, k, :]
            tz = dve([done, gate["gm", k]] + s.free, v.tensor_tensor, z, ps, GM[:, k, :], ALU.mult)
            t = pool([tz, gate["yc", k]], gp.tensor_tensor, y, z, y, ALU.add)
            gm_read[:] = [tz]
            s.free = [t]

            def split():
                mg[k] = split_to(hb_hi[:, k, :], hb_lo[:, k, :], y, t, hb_read)
            later(split)
            return [tz]

        evac["omla"] = evac_om
        p_om.ready = lambda kt: zm[kt]
        run(p_om)
        ob_read = [(PE.sem, PE.count)]
        out_t, sq_t = {}, [None]

        def evac_w(g, m, ps, done):
            k = 4 * g + m
            t = out_t[k] = act([done, *attn_done.values()], OUT1[:, k, :], ps, ACT.Copy)
            sq_t[0] = add_square(acc_a, OUT1[:, k, :], t, sq_t[0])
            return [t]

        evac["wout"] = evac_w
        p_w.ready = lambda kt: mg[kt]
        metaf = metaT[:, :].rearrange("p (k n) -> p k n", k=KT)
        meta_marks, acc_m = [], small2[:, 40:56]
        for k in range(KT):
            meta_marks.append(split_to(ob_hi[:, k, 0:NMETA], ob_lo[:, k, 0:NMETA], metaf[:, k, :], meta_done,
                                       ob_read, gain=col("norm2", k)))
        for k in range(KT):
            tm = add_square(acc_m, metaf[:, k, :], meta_done, tm if k else None, NMETA)
        F2 = factor[:, 1, :]
        m_marks, rp = [], []
        pending.append(factor_job(F2[:, 0:NMETA], acc_m, tm, D, NMETA, m_marks, delay=5))
        x_again = [load(x_in[:, b_, :], a["x"][0, b_ * P:(b_ + 1) * P, :], zm_read + gm_read)
                   for b_ in range(2)]

        def residual():
            yield
            yield
            for k in range(KT):
                b = side_banks.next()
                PE.wait(b.free + x_again)
                for blk in range(2):
                    i = nc.tensor.transpose(b.ap[:, blk * P:(blk + 1) * P], x_in[:, blk, k * P:(k + 1) * P], c("ident"))
                t = PE.mark(i)
                xr_done[k] = act([t, *gm_read], XR[:, k, :], b.ap[:, 0:S], ACT.Copy)
                b.free = [xr_done[k]]
                if k % 2:
                    yield

        xr_done = {}
        pending.append(residual())
        run(p_w)
        drain_jobs()
        hb2_read = [(PE.sem, PE.count)]
        tap("out1", OUT1, [out_t[15]])

        for _ in factor_job(RQ, acc_a, sq_t[0], D, S, rp):
            pass
        rp_done = rp[0]
        x1_marks, h2_marks, sq2 = [], [], None

        def lo_of(k):
            h2_marks[k].append(dve([h2_marks[k][0], x1_marks[k]], v.scalar_tensor_tensor, ob_lo[:, k, NMETA:T],
                                   XR[:, k, :], col("norm2", k), ob_hi[:, k, NMETA:T].bitcast(F32),
                                   ALU.mult, ALU.subtract))

        for k in range(KT):
            o, x = OUT1[:, k, :], XR[:, k, :]
            t = dve([rp_done, out_t[k]], v.tensor_tensor, o, o, RQ, ALU.mult)
            t = dve([t, xr_done[k]], v.scalar_tensor_tensor, x, o, col("post", k), x, ALU.mult, ALU.add)
            x1_marks.append(t)
            hi = act([t], ob_hi[:, k, NMETA:T], x, ACT.Copy, scale=col("norm2", k))
            h2_marks.append([hi, *meta_marks[k]])
            sq2 = add_square(acc_b, x, t, sq2)
            if k:
                lo_of(k - 1)
        lo_of(KT - 1)
        x1_dram = nc.dram_tensor("x1_kept", [P, KT * S], F32, kind="Internal").ap()
        x1_kept = load(x1_dram, XR.rearrange("p k n -> p (k n)"), x1_marks)
        tap("x1", XR, x1_marks)
        arena_free = [x1_marks[-1], sq2, x1_kept, h2_marks[-1][0], h2_marks[-1][-1]]

        QI, KI = region(0, 8, 8, S), region(8, 2, T)
        KA, QA, VA = region(9.25, 4.25, KVA, T), region(13.5, 8, HA, S), region(21.5, 6, 3, 512)
        FB, IB, QB = region(27.5, 8.5, HB, T), region(36, 12, 3, 1024), region(48, 8, HB, S)
        GA = region(56, 16, KT, S)
        L0 = CONSTS["late"][0]
        late = region(58, 6, CONSTS["late"][1] - L0)
        bias2, score2 = region(65, 2, 416), region(67, 2, 416)
        late_load = load(late, a["const_f"][:, L0:CONSTS["late"][1]], arena_free)

        def lc(name):
            lo, hi = CONSTS[name]
            return late[:, lo - L0:hi - L0]

        for p_ in (p2_ki, p2_qi, p2_ka, p2_va, p2_qa, p2_fb, p2_ib, p2_qb, p2_ga, p2_za, p2_zb, p2_gb):
            p_.ready = lambda kt: h2_marks[kt]

        wiT = small3[:, :]
        ki_done, wi_done, qi_done = [], [], {}
        F2M = F2[:, NMETA:T]
        f2 = []

        pending.append(factor_job(F2M, acc_b, sq2, D, S, f2, delay=4))

        def evac_ki(g, m, ps, done):
            t = dve([done, *f2, *m_marks, *arena_free], v.tensor_tensor, KI, ps, F2, ALU.mult)

            def job():
                yield
                b = side_banks.next()
                PE.wait(b.free + [t])
                for blk in range(2):
                    i = nc.tensor.transpose(b.ap[:, blk * P:(blk + 1) * P],
                                            KI[:, NMETA + blk * P:NMETA + (blk + 1) * P], c("ident"))
                t1 = PE.mark(i)
                wi_done.append(dve([t1], v.tensor_scalar, wiT.rearrange("p (b h) -> p b h", b=2),
                                   b.ap[:, 0:S].rearrange("p (b n) -> p b n", b=2)[:, :, DI:DI + HI],
                                   W_SCALE, None, ALU.mult))
                b.free = wi_done
                f = head_factors.next()
                tf = pool(f.free + [t], gp.tensor_tensor, f.ap[0:DI, :], KI[0:DI, :], KI[0:DI, :], ALU.mult)
                yield
                b, tf = yield from row_factor(f.ap, tf, DI, T, rows=DI)
                t2 = dve([tf, t1], v.tensor_tensor, KI[0:DI, :], KI[0:DI, :], b.ap[0:DI, 0:T], ALU.mult)
                b.free = f.free = [t2]
                t2 = act([t2], KI[0:DI, :], KI[0:DI, :], ACT.Copy, scale=col("ikn")[0:DI, :])
                yield
                ki_done.append(rope_tile(KI, t2, lc("rot_i"), lc("cos_i"), lc("sin_i"), [late_load], T,
                                         dup=c("dup64"), rows=DI))
                pending.extend(index_head(h) for h in range(HI))
            pending.append(job())
            return [t]

        evac["ki"] = evac_ki

        def evac_qi(g, m, ps, done):
            k = 4 * g + m
            t = dve([done, *f2, *arena_free], v.tensor_tensor, QI[:, k, :], ps, F2M, ALU.mult)

            def job():
                yield
                qi_done[k] = rope_tile(QI[:, k, :], t, lc("rot_i1"), lc("cos_i")[:, NMETA:T],
                                       lc("sin_i")[:, NMETA:T], [late_load], S)
            pending.append(job())
            return [t]

        evac["qi"] = evac_qi

        def rms_rope_head(dst, ps, done, fac, width, lo, gname, marks, k):
            t = dve([done, *f2, *arena_free], v.tensor_tensor, dst, ps, fac, ALU.mult)

            def job():
                f = head_factors.next()
                tf = pool(f.free + [t], gp.tensor_tensor, f.ap[:, 0:width], dst, dst, ALU.mult)
                yield
                b, tf = yield from row_factor(f.ap, tf, P, width)
                t2 = dve([tf], v.scalar_tensor_tensor, dst, dst, col(gname), b.ap[:, 0:width], ALU.mult, ALU.mult)
                b.free = f.free = [t2]
                yield
                marks[k] = rope_tile(dst, t2, lc("rot_a"), lc("cos_a")[:, lo:T], lc("sin_a")[:, lo:T],
                                     [late_load], width)
            pending.append(job())
            return [t]

        ka_done, qa_done, va_done = {}, {}, {}
        evac["ka"] = lambda g, m, ps, done: rms_rope_head(KA[:, m, :], ps, done, F2, T, 0, "kn", ka_done, m)
        evac["qa2"] = lambda g, m, ps, done: rms_rope_head(QA[:, 4 * g + m, :], ps, done, F2M, S, NMETA, "qn",
                                                           qa_done, 4 * g + m)

        def token_major(dst, marks):
            def f(g, m, ps, done):
                k = 4 * g + m
                s = scratch.next()
                t_out = dve([done, *f2, *arena_free] + s.free, v.tensor_tensor, s.ap, ps, F2, ALU.mult)

                def job():
                    b = side_banks.next()
                    PE.wait(b.free + [t_out])
                    for blk in range(2):
                        nc.tensor.transpose(b.ap[:, blk * P:(blk + 1) * P],
                                            s.ap[:, NMETA + blk * P:NMETA + (blk + 1) * P], c("ident"))
                    i = nc.tensor.transpose(b.ap[0:NMETA, S:S + P], s.ap[:, 0:NMETA], c("ident"))
                    t = PE.mark(i)
                    s.free = [t]
                    w = slice(k * P, (k + 1) * P)
                    act([t], dst[:, 1:3, w], b.ap[:, 0:S].rearrange("p (b n) -> p b n", b=2), ACT.Copy)
                    marks[k] = act([], dst[0:NMETA, 0, w], b.ap[0:NMETA, S:S + P], ACT.Copy)
                    b.free = [marks[k]]
                later(job, 2)
                return [t_out]
            return f

        evac["va"] = token_major(VA, va_done)
        ib_done = {}
        evac["ib"] = token_major(IB, ib_done)

        KEYS = (NMETA + P, T)
        PART = ((0, KEYS[0]), (KEYS[0], KEYS[0] + KEYS[1]))
        chain = {"score": None, "bias": None}

        def index_head(h):
            half = 64 * (h % 2)
            b = side_banks.next()
            PE.wait(b.free + [qi_done[h // 2], *ki_done])
            for blk, (lo, hi) in enumerate(PART):
                i = mm(b.ap[:, lo:hi], QI[half:half + 64, h // 2, blk * P:(blk + 1) * P],
                       KI[half:half + 64, 0:KEYS[blk]])
            t = PE.mark(i)
            p = prob.next()
            t = act([t] + p.free, p.ap, b.ap[:, 0:416], ACT.Relu)
            b.free = [t]
            yield
            for blk, (lo, hi) in enumerate(PART):
                w = wiT[:, blk * HI + h:blk * HI + h + 1]
                if h == 0:
                    ts = dve([t, *wi_done, *arena_free], v.tensor_scalar, score2[:, lo:hi], p.ap[:, lo:hi], w, None, ALU.mult)
                else:
                    ts = dve([t, chain["score"]], v.scalar_tensor_tensor, score2[:, lo:hi], p.ap[:, lo:hi], w,
                             score2[:, lo:hi], ALU.mult, ALU.add)
            p.free = [ts]
            chain["score"] = ts
            if h == HI - 1:
                pending.append(select())

        best = sb("best", [P, 16])

        def select():
            t = chain["score"]
            for blk, (lo, hi) in enumerate(PART):
                t = dve([t], v.memset, score2[0:CHUNK, hi - CHUNK:hi], MASKED)
            for r in range(TOPK // 8):
                yield
                for blk, (lo, hi) in enumerate(PART):
                    m8 = best[:, 8 * blk:8 * blk + 8]
                    t8 = dve([t], v.max, m8, score2[:, lo:hi])
                    t = dve([t8], v.match_replace, score2[:, lo:hi], m8, score2[:, lo:hi], TAKEN)
            chain["bias"] = dve([t], v.tensor_scalar, bias2, score2, (MASKED + TAKEN) / 2, NEG, ALU.is_gt, ALU.mult)
            pending.extend(attention2(h) for h in range(HA))

        ya_done = {}

        prob_meta = Ring([rope1[0:NMETA, i, :] for i in range(2)])

        def attention2(h):
            g = h // 2
            b = side_banks.next()
            PE.wait(b.free + [qa_done[h], ka_done[g]])
            for blk, (lo, hi) in enumerate(PART):
                i = mm(b.ap[:, lo:hi], QA[:, h, blk * P:(blk + 1) * P], KA[:, g, 0:KEYS[blk]])
            t = PE.mark(i)
            p, st = prob.next(), stats.next()
            t = dve([t, chain["bias"]] + p.free, v.scalar_tensor_tensor, p.ap, b.ap[:, 0:416], SCALE2, bias2,
                    ALU.mult, ALU.add)
            b.free = [t]
            done = softmax(p, st, PART, t)
            yield
            pt = probT.next()
            b, b2 = side_banks.next(), side_banks.next()
            PE.wait(b.free + b2.free + done)
            lo0, lo1 = PART[0][0] + NMETA, PART[1][0] + NMETA
            for j, lo in enumerate((lo0, lo1, lo1 + P)):
                nc.tensor.transpose(b.ap[:, j * P:(j + 1) * P], p.ap[:, lo:lo + P], c("ident"))
            for blk in range(2):
                lo = PART[blk][0]
                i = nc.tensor.transpose(b2.ap[0:NMETA, blk * P:(blk + 1) * P], p.ap[:, lo:lo + NMETA], c("ident"))
            t = PE.mark(i)
            p.free = [t]
            t1 = act([t] + pt.free, pt.ap[:, 0:384], b.ap[:, 0:384], ACT.Copy)
            b.free = [t1]
            ptm = prob_meta.next()
            t = act(ptm.free, ptm.ap, b2.ap[0:NMETA, 0:S], ACT.Copy)
            b2.free = [t]
            yield
            b = side_banks.next()
            w = slice(g * P, (g + 1) * P)
            PE.wait(b.free + [t, va_done[g]])
            mm(b.ap[:, 0:S], VA[:, 1, w], pt.ap[:, 0:S], True, False)
            mm(b.ap[:, P:S], VA[:, 2, w], pt.ap[:, S:384], False, False)
            t = PE.mark(mm(b.ap[:, 0:S], VA[0:NMETA, 0, w], ptm.ap, False, True))
            pt.free = ptm.free = [t]
            ya_done[h] = act([t], QA[:, h, :], b.ap[:, 0:S], ACT.Copy)
            b.free = [ya_done[h]]

        fb_done, qb_done = {}, {}

        def evac_fb(g, m, ps, done):
            k = 4 * g + m
            s = scratch.next()
            t = dve([done, *f2] + s.free, v.tensor_tensor, s.ap, ps, F2, ALU.mult)
            t1 = act([t, *arena_free], FB[:, k, :], s.ap, ACT.Sigmoid)
            s.free = [t1]

            def forget():
                fb_done[k] = dve([t1, lb_done], v.tensor_scalar, FB[:, k, :], FB[:, k, :], oml[:, k:k + 1],
                                 lb[:, k:k + 1], ALU.mult, ALU.add)
            later(forget, 2)
            return [t]

        evac["fb"] = evac_fb

        def evac_qb(g, m, ps, done):
            k = 4 * g + m
            s = scratch.next()
            t = dve([done, *f2, *arena_free], v.tensor_tensor, QB[:, k, :], ps, F2M, ALU.mult)
            t1 = act([t] + s.free, s.ap[:, 0:S], QB[:, k, :], ACT.Sigmoid)
            qb_done[k] = pool([t1], gp.tensor_tensor, QB[:, k, :], QB[:, k, :], s.ap[:, 0:S], ALU.mult)
            s.free = [qb_done[k]]
            return [t]

        evac["qb"] = evac_qb

        W2 = 2 * S

        def doubled(Cp, Rp, n, h, free):
            cv = Cp.rearrange("p (b x) -> p b x", x=2 * h)
            rv = Rp.rearrange("p (b x) -> p b x", x=2 * h)
            nb = n // (2 * h)
            t = dve(free, v.tensor_tensor, rv[:, :, 0:h], rv[:, :, 0:h],
                    cv[:, :, 2 * h - 1:2 * h].to_broadcast([P, nb, h]), ALU.mult)
            t = dve([t], v.tensor_tensor, cv[:, :, h:2 * h], cv[:, :, h:2 * h],
                    cv[:, :, h - 1:h].to_broadcast([P, nb, h]), ALU.mult)
            return t

        o_done = {}
        hg = {}

        def meta_state():
            C0, R0, kd = hg["C"], hg["R"], hg["kL"]
            n = HB * NMETA
            fm = FB[:, :, 0:NMETA]
            cv = C0[:, 0:n]
            t = dve([*fb_done.values(), *arena_free, *hg["free"]], v.tensor_copy, cv.rearrange("p (h x) -> p h x", h=HB), fm)
            t1 = dve([], v.memset, R0[:, 0:n], 1.0)
            t = dve([], v.tensor_scalar, kd[:, 0:n].rearrange("p (h x) -> p h x", h=HB), fm, -1.0, 1.0, ALU.mult, ALU.add)
            for h in (1, 2, 4, 8):
                t = doubled(cv, R0[:, 0:n], n, h, [t, t1])
            yield
            t = dve([t], v.tensor_tensor, kd[:, 0:n], kd[:, 0:n], R0[:, 0:n], ALU.mult)
            for half in range(2):
                b = side_banks.next()
                PE.wait(b.free + [t])
                for j in range(4):
                    h = 4 * half + j
                    i = nc.tensor.transpose(b.ap[0:NMETA, j * P:(j + 1) * P], kd[:, h * NMETA:(h + 1) * NMETA], c("ident"))
                t2 = PE.mark(i)
                t2 = act([t2], hg["kM"][0:NMETA, half * 512:(half + 1) * 512], b.ap[0:NMETA, :], ACT.Copy)
                b.free = [t2]
            hg["kM_done"] = t2
            hg["free"] = [(PE.sem, PE.count), (VE.sem, VE.count)]

        def recurrence(pr):
            Cb, Rb, kL, qL, A, kK = hg["C"], hg["R"], hg["kL"], hg["qL"], hg["A"], hg["kK"]
            F = FB[:, 2 * pr:2 * pr + 2, NMETA:T]
            q = QB[:, 2 * pr:2 * pr + 2, :].rearrange("p h x -> p (h x)")
            h2 = lambda x: x.rearrange("p (h x) -> p h x", h=2)
            t = dve(hg["free"] + [qb_done[2 * pr], qb_done[2 * pr + 1]], v.tensor_copy, h2(Cb), F)
            t1 = dve([], v.memset, Rb, 1.0)
            tk = dve([], v.tensor_scalar, h2(kK), F, -1.0, 1.0, ALU.mult, ALU.add)
            b = side_banks.next()
            PE.wait(b.free + [tk])
            for j in range(4):
                w = slice(j * P, (j + 1) * P)
                i = mm(b.ap[:, w], kK[:, w], q[:, w])
            tp = PE.mark(i)
            four = lambda x: x.rearrange("p (a b) -> p a b", a=4)
            tA = dve([tp], v.tensor_tensor, four(A), four(b.ap), c("ident").unsqueeze(1).to_broadcast([P, 4, P]), ALU.mult)
            b.free = [tA]
            tprev = None
            for li, h in enumerate(LEVELS):
                yield
                right = lambda x: x.rearrange("p (b x) -> p b x", x=2 * h)[:, :, h:2 * h]
                left = lambda x: x.rearrange("p (b x) -> p b x", x=2 * h)[:, :, 0:h]
                ws = [t, t1, tk, tprev, *hg["init"]]
                ta_ = dve(ws, v.tensor_tensor, right(qL), right(q), right(Cb), ALU.mult)
                tb_ = pool(ws, gp.tensor_tensor, left(kL), left(kK), left(Rb), ALU.mult)
                b = side_banks.next()
                PE.wait(b.free + [ta_, tb_])
                for j in range(4):
                    w = slice(j * P, (j + 1) * P)
                    i = mm(b.ap[:, w], kL[:, w], qL[:, w])
                tprev = PE.mark(i)
                t = doubled(Cb, Rb, W2, h, [t, t1, tb_])
                tA = dve([tprev, lvl_done, tA], v.copy_predicated, four(A),
                         lvl[:, li * P:(li + 1) * P].unsqueeze(1).to_broadcast([P, 4, P]), four(b.ap))
                b.free = [tA]
            yield
            tk2 = pool([t, tprev], gp.tensor_tensor, h2(kL)[:, :, 0:P], h2(kK)[:, :, 0:P], h2(Rb)[:, :, 0:P], ALU.mult)
            tq2 = dve([t, tprev], v.tensor_tensor, qL, q, Cb, ALU.mult)
            b = side_banks.next()
            PE.wait(b.free + [tk2])
            for j in range(2):
                i = nc.tensor.transpose(b.ap[:, j * P:(j + 1) * P], kL[:, j * S:j * S + P], c("ident"))
            t3 = PE.mark(i)
            kd = hg["kd"]
            t3 = act([t3] + hg["kd_free"], kd, b.ap[:, 0:S], ACT.Copy)
            b.free = [t3]
            b = side_banks.next()
            PE.wait(b.free + [hg["kM_done"], t3, *ib_done.values()])
            for j in range(2):
                h = 2 * pr + j
                w = slice(h * P, (h + 1) * P)
                mm(b.ap[:, j * P:(j + 1) * P], hg["kM"][0:NMETA, w], IB[0:NMETA, 0, w])
                i = mm(b.ap[:, S + j * P:S + (j + 1) * P], kd[:, j * P:(j + 1) * P], IB[:, 1, w])
            t4 = PE.mark(i)
            St = hg["S"]
            t5 = act([t4] + hg["S_free"], St[:, 0:S], b.ap[:, 0:S], ACT.Copy)
            for j in range(2):
                t6 = dve([t5, t], v.scalar_tensor_tensor, St[:, S + j * P:S + (j + 1) * P], St[:, j * P:(j + 1) * P],
                         Cb[:, j * S + P - 1:j * S + P], b.ap[:, S + j * P:S + (j + 1) * P], ALU.mult, ALU.add)
            b.free = [t6]
            hg["kd_free"] = [t4]
            yield
            b = side_banks.next()
            PE.wait(b.free + [t6, tq2, tA])
            for j in range(2):
                w = slice((2 * pr + j) * P, (2 * pr + j + 1) * P)
                for blk in range(2):
                    x = slice(j * S + blk * P, j * S + (blk + 1) * P)
                    mm(b.ap[:, x], IB[:, 1 + blk, w], A[:, x], True, False)
                    i = mm(b.ap[:, x], St[:, blk * S + j * P:blk * S + (j + 1) * P], qL[:, x], False, True)
            t7 = PE.mark(i)
            hg["S_free"] = [t7]
            hg["free"] = [t7, t6]
            t8 = act([t7], QB[:, 2 * pr:2 * pr + 2, :].rearrange("p h x -> p (h x)"), b.ap, ACT.Copy)
            b.free = [t8]
            for j in range(2):
                pending.append(out_norm(2 * pr + j, t8))

        def out_norm(h, o):
            f = head_factors.next()
            t = pool(f.free + [o], gp.tensor_tensor, f.ap[:, 0:S], QB[:, h, :], QB[:, h, :], ALU.mult)
            yield
            b, t = yield from row_factor(f.ap, t, P, S)
            o_done[h] = dve([t], v.scalar_tensor_tensor, QB[:, h, :], QB[:, h, :], col("on"), b.ap[:, 0:S],
                            ALU.mult, ALU.mult)
            b.free = f.free = [o_done[h]]

        run(p2_qi)
        run(p2_ki)
        run(p2_ka)
        tap("KI", KI, ki_done)
        tap("QI", QI, [qi_done[7]])
        run(p2_va)
        run(p2_qa)
        run(p2_fb)
        tap("score2", score2, [chain["score"]])
        tap("KA", KA, list(ka_done.values()))
        run(p2_ib)
        tap("bias2", bias2, [chain["bias"]])
        run(p2_qb)
        drain_jobs()
        tap("ya", QA, list(ya_done.values()))
        attn2_over = list(ya_done.values()) + [chain["bias"]]
        hg.update(C=region(0, 2, W2), R=region(2, 2, W2), kL=region(4, 2, W2), qL=region(6, 2, W2),
                  A=region(8, 2, W2), kK=region(10, 2, W2), kd=region(12, 1, S), S=region(21.5, 2, W2),
                  kM=region(23.5, 4, 1024), free=[(PE.sem, PE.count), (SC.sem, SC.count), (VE.sem, VE.count),
                                                (GP.sem, GP.count)], kd_free=[], S_free=[])
        lvl = small[:, 0:224].bitcast(U8)
        lvl_f = region(0, 3.5, len(LEVELS) * P)
        lvl_done = dve([load(lvl_f, a["const_lvl"], hg["free"])], v.tensor_copy, lvl, lvl_f)
        hg["free"].append(lvl_done)
        hg["init"] = [dve(attn2_over + hg["free"], v.memset, hg["qL"], 0.0), dve([], v.memset, hg["kL"], 0.0)]
        hg["free"] += hg["init"]
        SC.wait(hg["free"])

        def recurrences():
            yield from meta_state()
            for pr in range(HB // 2):
                yield from recurrence(pr)

        pending.append(recurrences())
        g2 = {}
        evac["ga"] = sigmoid_to(GA, F2M, f2[0], g2, "ga", attn2_over + [late_load] + list(qa_done.values()))
        run(p2_ga)
        ya, yb = {}, {}
        evac["za"] = silu_times(QA, ya_done, F2M, f2[0], *hb, hb2_read, ya)
        run(p2_za)

        def evac_ba(g, m, ps, done):
            k = 4 * g + m
            g2["pa", k] = dve([done, g2["ga", k]], v.tensor_tensor, GA[:, k, :], ps, GA[:, k, :], ALU.mult)
            return [g2["pa", k]]

        evac["ba"] = evac_ba
        p2_ba.ready = lambda kt: ya[kt]
        run(p2_ba)
        drain_jobs()
        tap("ob", QB, list(o_done.values()))
        evac["zb"] = silu_times(QB, o_done, F2M, f2[0], *hb_b, hb2_read, yb)
        run(p2_zb)
        GB = region(29, 16, KT, S)
        zb_read = [*zm_read]
        rec_over = list(o_done.values()) + [(PE.sem, PE.count), (SC.sem, SC.count)]
        evac["gb"] = sigmoid_to(GB, F2M, f2[0], g2, "gb", rec_over)
        run(p2_gb)
        h2_read = [(PE.sem, PE.count)]
        mg2, gb_read = {}, []

        def evac_bb(g, m, ps, done):
            k = 4 * g + m
            s = scratch.next()
            z, y = s.ap[:, 0:S], GA[:, k, :]
            tz = dve([done, g2["gb", k]] + s.free, v.tensor_tensor, z, ps, GB[:, k, :], ALU.mult)
            t = pool([tz, g2["pa", k]], gp.tensor_tensor, y, z, y, ALU.add)
            gb_read[:] = [tz]
            s.free = [t]

            def split():
                mg2[k] = split_to(ob_hi[:, k, 0:S], ob_lo[:, k, 0:S], y, t, h2_read)
            later(split)
            return [tz]

        evac["bb"] = evac_bb
        p2_bb.ready = lambda kt: yb[kt]
        run(p2_bb)

        stores = []
        xT2 = region(29, 16, KT, S)
        x1_back = load(xT2.rearrange("p k n -> p (k n)"), x1_dram, [x1_kept, gb_read[0]])
        OT = region(0, 16, 2, D)
        bb_over = rec_over + zb_read

        def evac_w2(g, m, ps, done):
            k = 4 * g + m
            t = dve([done, x1_back], v.tensor_tensor, xT2[:, k, :], ps, xT2[:, k, :], ALU.add)
            final[k] = t
            if m == 3:
                def job():
                    for j in range(4):
                        kk = 4 * g + j
                        b = side_banks.next()
                        PE.wait(b.free + [final[kk]])
                        for blk in range(2):
                            i = nc.tensor.transpose(b.ap[:, blk * P:(blk + 1) * P], xT2[:, kk, blk * P:(blk + 1) * P],
                                                    c("ident"))
                        t1 = PE.mark(i)
                        t2 = act([t1, *bb_over], OT[:, :, kk * P:(kk + 1) * P],
                                 b.ap[:, 0:S].rearrange("p (b n) -> p b n", b=2), ACT.Copy)
                        b.free = [t2]
                    for blk in range(2):
                        stores.append(load(out[0, blk * P:(blk + 1) * P, g * 512:(g + 1) * 512],
                                           OT[:, blk, g * 512:(g + 1) * 512], [t2]))
                    yield
                pending.append(job())
            return [t]

        final = {}
        evac["wout2"] = evac_w2
        p2_w.ready = lambda kt: mg2[kt]
        run(p2_w)
        drain_jobs()
        SP.wait(stores)


_INS = ["x", "positions", "pre_norm_g", "w_in", "q_a_norm_g", "w_q_b", "kv_a_norm_g", "w_kv_b", "conv_w",
        "w_o_mla", "w_o_conv", "w_out", "post_norm_g", "meta_tokens_2", "hgrn_lb_logits_2", "norm_g_2",
        "w_in_2", "q_norm_g_2", "k_norm_g_2", "idx_k_norm_g_2", "hgrn_out_norm_g_2", "w_branch_2", "w_out_2"]
TAPS = None


def kernel(**inputs):
    import concourse.bacc as _bacc
    from concourse.bass_utils import run_bass_kernel_spmd as _run

    nc = _bacc.Bacc("TRN2", target_bir_lowering=False, num_devices=1)
    arrays, aps = {}, {}
    given = {name: np.ascontiguousarray(inputs[name]) for name in _INS}
    given["const_f"], given["const_lvl"] = CONST_F, CONST_LVL
    for name, arr in given.items():
        arrays[f"in_{name}"] = arr
        aps[name] = nc.dram_tensor(f"in_{name}", arr.shape, mybir.dt.from_np(arr.dtype), kind="ExternalInput").ap()
    out = nc.dram_tensor("out_0", (1, S, D), F32, kind="ExternalOutput").ap()
    build(nc, aps, out, TAPS)
    r = _run(nc, [arrays], core_ids=[0])
    return r.results[0]["out_0"]
```

```python
from collections import deque
from contextlib import ExitStack

import numpy as np

import concourse.bass as bass
from concourse import mybir

F32 = mybir.dt.float32
F32R = mybir.dt.float32r
I32 = mybir.dt.int32
U8 = mybir.dt.uint8
ALU = mybir.AluOpType
ACT = mybir.ActivationFunctionType
AX = mybir.AxisListType.X

P = 128
D = 2048
KT = D // P
S = 256
NMETA = 16
T = S + NMETA
EPS = 1e-6
NEG = -1e30

H1, DN, RD, DV, LORA = 16, 128, 64, 128, 512
C_QA, C_KV, C_KR = 0, LORA, 2 * LORA
C_ZMLA = 2 * LORA + RD
C_CIN, C_B, C_C, C_ZCONV, C_GMLA, C_GCONV = (C_ZMLA + D * i for i in range(1, 7))
SCALE1 = 1.0 / float(np.sqrt(DN + RD))

BW = D // 2
HA, KVA, HI, DI, HB = 8, 4, 16, 64, 8
CHUNK, TOPK = 64, 64
C2_QA, C2_KA, C2_VA, C2_ZA, C2_QI = 0, 1024, 1536, 2048, 3072
C2_KI, C2_WI, C2_QB, C2_FB, C2_IB, C2_ZB, C2_G = 4096, 4160, 4176, 5200, 6224, 7248, 8272
SCALE2 = float(P) ** -0.5
W_SCALE = HI ** -0.5 * DI ** -0.5
MASKED, TAKEN = -3.0e38, -3.3e38

UNIT = 1024
N_RAW, N_SPLIT, LEAD = 4, 3, 2

CONSTS = {}


def _constants():
    p = np.arange(P)
    parts, at = [], 0

    def put(name, a):
        nonlocal at
        a = np.asarray(a, np.float32).reshape(P, -1)
        CONSTS[name] = (at, at + a.shape[1])
        parts.append(a)
        at += a.shape[1]

    def rotation(group, half, copies):
        r = np.zeros((P, P))
        for m in range(P):
            o = m % group
            base = m - o if copies == 1 else 0
            if o < half:
                r[base + o + half, m] = -1.0
            elif o < 2 * half:
                r[base + o - half, m] = 1.0
        return r

    put("ident", np.eye(P))
    put("ones", np.ones((P, P)))
    put("rot_q1", rotation(RD, RD // 2, 1))
    put("dup64", p[:, None] == p[None, :] % 64)
    put("rot_k1", rotation(RD, RD // 2, 2))
    causal = np.where(p[None, :] <= p[:, None], 0.0, NEG)
    put("mask1", np.concatenate([np.zeros((P, P)), causal], 1))
    inv = 10000.0 ** (-(np.arange(RD // 2) * 2) / RD)
    put("inv_freq", inv.astype(np.float32)[p % 32])
    put("neg_half", np.full((P, 1), -0.5))
    CONSTS["resident"] = (0, at)

    put("rot_a", rotation(P, 16, 1))
    put("rot_i", rotation(DI, 8, 2))
    put("rot_i1", rotation(DI, 8, 1))
    pos = np.arange(T, dtype=np.float32)

    def rope(group, half):
        o = p % group
        iv = np.power(np.float64(500000.0), -(o % half) * 2.0 / (2 * half)).astype(np.float32)
        ang = (pos[None, :] * iv[:, None]).astype(np.float32).astype(np.float64)
        on = (o < 2 * half)[:, None]
        return np.where(on, np.cos(ang), 1.0), np.where(on, np.sin(ang), 0.0)

    for name, (c, s) in (("a", rope(P, 16)), ("i", rope(DI, 8))):
        put("cos_" + name, c)
        put("sin_" + name, s)
    CONSTS["late"] = (CONSTS["resident"][1], at)
    f = np.concatenate(parts, 1)

    s, lv = p[:, None], []
    for h in LEVELS:
        t = p[p % (2 * h) >= h][None, :]
        lv.append((s // (2 * h) == t // (2 * h)) & (s % (2 * h) < h))
    return np.ascontiguousarray(f), np.ascontiguousarray(np.concatenate(lv, 1).astype(np.float32))


LEVELS = (1, 2, 4, 8, 16, 32, 64)
CONST_F, CONST_LVL = _constants()

ROWS = {}
_at = 0
for _name, _n in (("pre", 16), ("post", 16), ("norm2", 16), ("conv", 48), ("qa", 4), ("kva", 4),
                  ("lb", 16), ("qn", 1), ("kn", 1), ("on", 1), ("ikn", 1)):
    ROWS[_name] = _at
    _at += _n
N_ROWS = _at


class Queue:

    def __init__(self, eng, sem):
        self.eng, self.sem, self.count, self.seen = eng, sem, 0, {}

    def wait(self, marks):
        for m in marks:
            if m is not None:
                sem, value = m
                if self.seen.get(sem.name, 0) < value:
                    self.eng.wait_ge(sem, value)
                    self.seen[sem.name] = value

    def mark(self, inst):
        inst.then_inc(self.sem, 1)
        self.count += 1
        return (self.sem, self.count)


class Slot:

    def __init__(self, ap):
        self.ap, self.marks, self.held = ap, [], False

    @property
    def free(self):
        return self.marks

    @free.setter
    def free(self, marks):
        self.marks, self.held = marks, False


class Ring:
    def __init__(self, aps):
        self.slots, self.i = [Slot(a) for a in aps], 0

    def next(self):
        s = self.slots[self.i % len(self.slots)]
        self.i += 1
        assert not s.held
        s.held = True
        return s


class Phase:

    def __init__(self, weight, groups, ktiles, hi, lo, n, evac, ready=(), period=1):
        self.order = lambda w, n: [(w, lambda x: x)]
        self.hold = False
        self.weight, self.groups, self.ktiles = weight, groups, ktiles
        self.hi, self.lo, self.n = hi, lo, n
        self.evac, self.ready, self.period = evac, ready, period


class TokenTile:

    def __init__(self, block, columns, n):
        self.block, self.columns, self.n = block, columns, n


class Unit:
    def __init__(self, phase, g, k0, nk):
        self.phase, self.g, self.k0, self.nk = phase, g, k0, nk
        self.last = k0 + nk == phase.ktiles


def build(nc, a, out):
    ctx = ExitStack()
    with ctx:
        def sb(name, shape, dt=F32):
            return ctx.enter_context(nc.sbuf_tensor(name, shape, dt))

        def sem(name):
            return ctx.enter_context(nc.semaphore(name))

        PE = Queue(nc.tensor, sem("pe_done"))
        SC = Queue(nc.scalar, sem("act_done"))
        VE = Queue(nc.vector, sem("dve_done"))
        GP = Queue(nc.gpsimd, sem("pool_done"))
        SP = Queue(nc.sync, None)

        def act(waits, *args, **kw):
            SC.wait(waits)
            return SC.mark(nc.scalar.activation(*args, **kw))

        def dve(waits, op, *args, **kw):
            VE.wait(waits)
            return VE.mark(op(*args, **kw))

        def pool(waits, op, *args, **kw):
            GP.wait(waits)
            return GP.mark(op(*args, **kw))

        v, gp = nc.vector, nc.gpsimd

        def pe_t(waits, dst, src, ident):
            PE.wait(waits)
            return nc.tensor.transpose(dst, src, ident)

        def mm(dst, lhsT, rhs, start=True, stop=True):
            return nc.tensor.matmul(dst, lhsT, rhs, start=start, stop=stop, skip_group_check=True)

        loads = [0]

        def load(dst, src, waits=(), q=None):
            q = q or SP
            q.wait(waits)
            loads[0] += 1
            s = sem(f"load{loads[0]}")
            q.eng.dma_start(dst, src).then_inc(s, 16)
            return (s, 16)

        raw = sb("w_raw", [P, N_RAW, UNIT])
        whi = sb("w_hi", [P, N_SPLIT, UNIT], F32R)
        wlo = sb("w_lo", [P, N_SPLIT, UNIT], F32R)
        hb_hi = sb("hb_hi", [P, KT, S], F32R)
        hb_lo = sb("hb_lo", [P, KT, S], F32R)
        ob_hi = sb("ob_hi", [P, KT, T], F32R)
        ob_lo = sb("ob_lo", [P, KT, T], F32R)
        arena = sb("arena", [P, 72 * 256])
        con = sb("con", [P, CONSTS["resident"][1]])
        cols = sb("cols", [P, P])
        rope1 = sb("rope1", [P, 2, S])
        factor = sb("factor", [P, 3, T])
        small = sb("small", [P, 256])
        scratch = Ring([sb(f"scratch{i}", [P, T])[:, :] for i in range(5)])
        head_factors = Ring([sb(f"head_factor{i}", [P, T])[:, :] for i in range(3)])
        acc_a, acc_b = sb("acc_a", [P, S])[:, :], sb("acc_b", [P, S])[:, :]
        psum = [ctx.enter_context(nc.psum_tensor(f"bank{i}", [P, 512], F32)) for i in range(8)]
        stats = Ring([sb(f"stats{i}", [P, 8])[:, :] for i in range(6)])
        proj_banks = Ring([b[:, :] for b in psum[:5]])
        side_banks = Ring([b[:, :] for b in psum[5:]])

        def region(kb0, kb, *shape):
            n = int(np.prod(shape))
            assert n <= 256 * kb
            at = int(kb0 * 256)
            ap = arena[:, at:at + n]
            if len(shape) == 1:
                return ap
            if len(shape) == 2:
                return ap.rearrange("p (a b) -> p a b", a=shape[0])
            return ap.rearrange("p (a b c) -> p a b c", a=shape[0], b=shape[1])

        def c(name):
            lo, hi = CONSTS[name]
            return con[:, lo:hi]

        def col(name, i=0):
            j = ROWS[name] + i
            return cols[:, j:j + 1]

        units = []
        raw_sem = [sem(f"raw{i}") for i in range(N_RAW)]
        raw_free = [None] * N_RAW
        split_free = [None] * N_SPLIT
        split_done = {}
        landed = {}
        issued = [0, 0]

        def plan(phase):
            phase.first = len(units)
            for g, (c0, nc_, tiles) in enumerate(phase.groups):
                step = min(UNIT // nc_, phase.ktiles)
                for k0 in range(0, phase.ktiles, step):
                    units.append(Unit(phase, g, k0, step))
            phase.end = len(units)
            return phase

        def size(u):
            c0, n, _ = u.phase.groups[u.g]
            return c0, n, u.nk * n

        def issue_load():
            i = issued[0]
            if i >= len(units):
                return
            issued[0] += 1
            u, s = units[i], i % N_RAW
            c0, n, sz = size(u)
            SP.wait([raw_free[s]])
            src = u.phase.weight.rearrange("(k p) n -> p k n", p=P)[:, u.k0:u.k0 + u.nk, c0:c0 + n]
            dst = raw[:, s, 0:sz].rearrange("p (k n) -> p k n", k=u.nk)
            nc.sync.dma_start(dst, src).then_inc(raw_sem[s], 16)
            landed[i] = (raw_sem[s], 16 * (i // N_RAW + 1))

        def issue_split():
            i = issued[1]
            if i >= len(units):
                return
            issued[1] += 1
            s, r = i % N_SPLIT, i % N_RAW
            _, _, sz = size(units[i])
            for src, dst in units[i].phase.order(raw[:, r, 0:sz], sz):
                hi = act([landed[i], split_free[s]], dst(whi[:, s, 0:sz]), src, ACT.Copy)
                lo = dve([hi, split_free[s]], v.tensor_tensor, dst(wlo[:, s, 0:sz]), src,
                         dst(whi[:, s, 0:sz]).bitcast(F32), ALU.subtract)
            raw_free[r] = lo
            split_done[i] = [hi, lo]
            issue_load()

        pending, active = deque(), []
        deferred = deque()
        jobs = {"width": 3}

        def pump():
            for job in list(active):
                if next(job, "end") == "end":
                    active.remove(job)
            if pending and len(active) < jobs["width"]:
                job = pending.popleft()
                active.append(job)
                if next(job, "end") == "end":
                    active.remove(job)

        def drain_jobs():
            flush()
            while pending or active:
                pump()

        def run(phase):
            banks = {}
            for i in range(phase.first, phase.end):
                while issued[1] <= min(i + LEAD, len(units) - 1):
                    issue_split()
                u, s = units[i], i % N_SPLIT
                c0, n, sz = size(u)
                tiles = phase.groups[u.g][2]
                hi_w = whi[:, s, 0:sz].rearrange("p (k n) -> p k n", k=u.nk)
                lo_w = wlo[:, s, 0:sz].rearrange("p (k n) -> p k n", k=u.nk)
                PE.wait(split_done.pop(i))
                for m, tile in enumerate(tiles):
                    if u.k0 == 0:
                        banks[m] = proj_banks.next()
                        PE.wait(banks[m].free)
                    by_token = isinstance(tile, TokenTile)
                    dst = banks[m].ap[:, 0:tile.n if by_token else phase.n]
                    for k in range(u.nk):
                        kt = u.k0 + k
                        PE.wait(phase.ready(kt) if callable(phase.ready) else phase.ready)
                        x_hi, x_lo = phase.hi(kt), phase.lo(kt)
                        first, last = kt == 0, kt == phase.ktiles - 1
                        if by_token:
                            w_hi, w_lo = tile.columns(hi_w[:, k, :]), tile.columns(lo_w[:, k, :])
                            rows = slice(tile.block * P, (tile.block + 1) * P)
                            to = dst if len(w_hi.shape) == 2 else dst.rearrange("p (h x) -> p h x", x=P)
                            mm(to, x_hi[:, rows], w_hi, first, False)
                            mm(to, x_lo[:, rows], w_hi, False, False)
                            inst = mm(to, x_hi[:, rows], w_lo, False, last)
                        else:
                            mm(dst, tile(hi_w[:, k, :]), x_hi, first, False)
                            mm(dst, tile(hi_w[:, k, :]), x_lo, False, False)
                            inst = mm(dst, tile(lo_w[:, k, :]), x_hi, False, last)
                    if u.last or m == len(tiles) - 1:
                        done = PE.mark(inst)
                    for d in deferred:
                        d[0] -= 1
                    due = [d for d in deferred if d[0] <= 0]
                    for d in due:
                        deferred.remove(d)
                        d[1]()
                    if u.last:
                        banks[m].free = phase.evac(u.g, m, dst, done)
                split_free[s] = done
                if not (phase.hold and i == phase.end - 1):
                    while issued[1] <= min(i + N_SPLIT, len(units) - 1):
                        issue_split()
                if (i - phase.first) % phase.period == phase.period - 1:
                    pump()

        def later(step, tiles=4):
            deferred.append([tiles, step])

        def flush():
            while deferred:
                deferred.popleft()[1]()

        def plain(c0, groups, cols_=512):
            tiles = [(lambda w, m=m: w[:, m * P:(m + 1) * P]) for m in range(cols_ // P)]
            return [(c0 + g * cols_, cols_, tiles) for g in range(groups)]

        def row_factor(squares, done, n, width, rows=P, more=None, wait=1, keep=None):
            starts = [0] if width < P else list(range(0, width - P + 1, P))
            if width > P and width % P:
                starts.append(width - P)
            m = min(width, P)
            st, b = stats.next(), side_banks.next()
            PE.wait(b.free + [done])
            for j, lo in enumerate(starts):
                t = mm(b.ap[0:m, j:j + 1], squares[0:rows, lo:lo + m], c("ones")[0:rows, 0:1], True, more is None)
                if more is not None:
                    t = mm(b.ap[0:m, j:j + 1], more[0:rows, lo:lo + m], c("ones")[0:rows, 0:1], False, True)
            t = PE.mark(t)
            f = st.ap[0:m, 0:len(starts)]
            t = dve([t] + st.free, v.tensor_scalar, f, b.ap[0:m, 0:len(starts)], 1.0 / n, EPS, ALU.mult, ALU.add)
            b.free = [t]
            kept = f if keep is None else keep
            t = pool([t], gp.tensor_tensor, kept, f, c("neg_half")[0:m, :].to_broadcast([m, len(starts)]), ALU.pow)
            at = 0
            for j, lo in enumerate(starts):
                new = lo + m - at
                t1 = dve([t], v.tensor_scalar, squares[0:m, at:at + new], c("ident")[0:m, m - new:m],
                         kept[:, j:j + 1], None, ALU.mult)
                at += new
            st.free = [t1]
            for _ in range(wait):
                yield
            b = side_banks.next()
            PE.wait(b.free + [t1])
            at = 0
            for lo in starts:
                new = lo + m - at
                t = mm(b.ap[:, at:at + new], c("ones")[0:m, :], squares[0:m, at:at + new])
                at += new
            return b, PE.mark(t)

        def factor_job(dst, squares, done, n, width, marks, free=(), delay=0, keep=None, more=None):
            for _ in range(delay):
                yield
            b, t = yield from row_factor(squares, done, n, width, keep=keep, more=more)
            marks.append(dve([t, *free], v.tensor_copy, dst, b.ap[:, 0:width]))
            b.free = [marks[-1]]

        def add_square(acc, x, x_done, prev, w=S):
            if prev is None:
                return act([x_done], acc, x, ACT.Square)
            sq = scratch.next()
            t = act([x_done] + sq.free, sq.ap[:, 0:w], x, ACT.Square)
            t = pool([t, prev], gp.tensor_tensor, acc, acc, sq.ap[:, 0:w], ALU.add)
            sq.free = [t]
            return t

        def split_to(dst_hi, dst_lo, src, src_done, free, gain=None):
            if gain is None:
                hi = act(free + [src_done], dst_hi, src, ACT.Copy)
                lo = dve([hi, src_done], v.tensor_tensor, dst_lo, src, dst_hi.bitcast(F32), ALU.subtract)
            else:
                hi = act(free + [src_done], dst_hi, src, ACT.Copy, scale=gain)
                lo = dve([hi, src_done], v.scalar_tensor_tensor, dst_lo, src, gain, dst_hi.bitcast(F32),
                         ALU.mult, ALU.subtract)
            return [hi, lo]

        Q1, QR, K1, V1, G1 = (region(0, 16, H1, S), region(16, 8, H1 // 2, S), region(24, 16, H1, S),
                              region(40, 16, 2, D), region(56, 16, KT, S))
        LAT = V1[:, 0, :].rearrange("p (k n) -> p k n", k=8)
        OUT1 = region(40, 16, KT, S)
        GM = K1
        x_in = region(0, 16, 2, D)
        x_meta = region(16, 8, D)
        xT = G1
        XR = region(24, 16, KT, S)
        kr1 = sb("kr1", [P, S])
        prob = Ring([sb(f"prob{i}", [P, 416])[:, :] for i in range(2)])
        probT = Ring([sb(f"probT{i}", [P, 384])[:, :] for i in range(2)])

        hb = (lambda k: hb_hi[:, k, :], lambda k: hb_lo[:, k, :])
        ob = (lambda k: ob_hi[:, k, 0:S], lambda k: ob_lo[:, k, 0:S])
        ob_kv = (lambda k: ob_hi[:, k + 4, 0:S], lambda k: ob_lo[:, k + 4, 0:S])
        ob_main = (lambda k: ob_hi[:, k, NMETA:T], lambda k: ob_lo[:, k, NMETA:T])
        ob_all = (lambda k: ob_hi[:, k, :], lambda k: ob_lo[:, k, :])
        hb_b = (lambda k: hb_hi[:, k + 8, :], lambda k: hb_lo[:, k + 8, :])
        w1, w2 = a["w_in"], a["w_in_2"][0]
        HD = DN + RD

        def pair_order(w, n):
            view = w.rearrange("p (k h x) -> p k h x", h=2, x=HD)
            out_ = []
            for lo, hi, at in ((0, DN, 0), (DN, HD, 2 * DN)):
                out_.append((view[:, :, :, lo:hi],
                             lambda x, lo=lo, hi=hi, at=at: x.rearrange("p (k y) -> p k y", y=2 * HD)
                             [:, :, at:at + 2 * (hi - lo)].rearrange("p k (h x) -> p k h x", h=2)))
            return out_

        pair = plain(0, 1, 384)[0][2]
        one = [lambda w: w[:, 0:P]]

        evac = {}

        def ph(name, *args, **kw):
            p_ = Phase(*args, evac=lambda *e: evac[name](*e), **kw)
            return plan(p_)

        p_qa = ph("qa", w1, plain(C_QA, 1), KT, *hb, S)
        p_kv = ph("kva", w1, plain(C_KV, 1), KT, *hb, S)
        p_kr = ph("kr", w1, [(C_KR, P, one)], KT, *hb, S)
        p_q = ph("q", a["w_q_b"], [(g * 384, 384, pair) for g in range(8)], 4, *ob, S)
        p_q.order = pair_order
        v_of = lambda w: w.rearrange("p (h x) -> p h x", h=2)[:, :, P:2 * P]
        kv_tiles = [lambda w: w[:, 0:P], lambda w: w[:, 2 * P:3 * P], TokenTile(0, v_of, S), TokenTile(1, v_of, S)]
        p_k = ph("kv", a["w_kv_b"], [(g * 512, 512, kv_tiles) for g in range(8)], 4, *ob_kv, S)
        p_conv = []
        for j in range(4):
            for name, c0 in (("cin", C_CIN), ("cgate", C_C), ("bgate", C_B), ("zconv", C_ZCONV)):
                p_conv.append((j, ph(f"{name}{j}", w1, plain(c0 + 512 * j, 1), KT, *hb, S, period=3)))
        p_gc = ph("gconv", w1, plain(C_GCONV, 4), KT, *hb, S)
        p_oc = ph("oconv", a["w_o_conv"], plain(0, 4), KT, *ob, S)
        p_zm = ph("zmla", w1, plain(C_ZMLA, 4), KT, *hb, S)
        p_gm = ph("gmla", w1, plain(C_GMLA, 4), KT, *hb, S)
        p_om = ph("omla", a["w_o_mla"], plain(0, 4), KT, *ob, S)
        p_w = ph("wout", a["w_out"], plain(0, 4), KT, *hb, S)
        p2_qi = ph("qi", w2, plain(C2_QI, 2), KT, *ob_main, S)
        p2_ki = ph("ki", w2, [(C2_KI, P, one)], KT, *ob_all, T)
        p2_ka = ph("ka", w2, plain(C2_KA, 1), KT, *ob_all, T)
        p2_va = ph("va", w2, plain(C2_VA, 1), KT, *ob_all, T)
        p2_qa = ph("qa2", w2, plain(C2_QA, 2), KT, *ob_main, S)
        p2_fb = ph("fb", w2, plain(C2_FB, 2), KT, *ob_all, T)
        p2_ib = ph("ib", w2, plain(C2_IB, 2), KT, *ob_all, T)
        p2_qb = ph("qb", w2, plain(C2_QB, 2), KT, *ob_main, S)
        p2_ga = ph("ga", w2, plain(C2_G, 4), KT, *ob_main, S)
        p2_za = ph("za", w2, plain(C2_ZA, 2), KT, *ob_main, S)
        p2_ba = ph("ba", a["w_branch_2"][0, 0], plain(0, 4), 8, *hb, S)
        p2_zb = ph("zb", w2, plain(C2_ZB, 2), KT, *ob_main, S)
        p2_gb = ph("gb", w2, plain(C2_G + D, 4), KT, *ob_main, S)
        p2_bb = ph("bb", a["w_branch_2"][0, 1], plain(0, 4), 8, *hb_b, S)
        p2_w = ph("wout2", a["w_out_2"][0],
                  [(512 * g, 512, [TokenTile(blk, lambda w: w, 512) for blk in range(2)]) for g in range(4)],
                  KT, *ob, S)

        XC = 4
        ident_load = load(c("ident"), a["const_f"][:, 0:P], q=SC)
        x_load = [load(x_in[:, :, k * P:(k + XC) * P],
                       a["x"][0, :, k * P:(k + XC) * P].rearrange("(b p) n -> p b n", p=P), q=SC)
                  for k in range(0, KT, XC)]
        rows_in = region(24, 1, P)
        row_loads = []

        def rows_of(name, src, n):
            r = ROWS[name]
            row_loads.append(load(rows_in[r:r + n, 0:src.shape[1]], src, [rows_zero]))

        rows_zero = dve([], v.memset, rows_in, 0.0)
        r128 = lambda ap: ap.rearrange("(k p) -> k p", p=P)
        rows_of("pre", r128(a["pre_norm_g"]), 16)
        issue_load()
        con_load = load(con[:, P:], a["const_f"][:, P:CONSTS["resident"][1]])
        for _ in range(N_RAW - 1):
            issue_load()
        pos_i = region(25, 1, S)[0:1, :].bitcast(I32)
        pos_load = load(pos_i, a["positions"])
        rows_of("post", r128(a["post_norm_g"]), 16)
        rows_of("norm2", r128(a["norm_g_2"][0]), 16)
        rows_of("conv", a["conv_w"].rearrange("c (k p) -> (c k) p", p=P), 48)
        rows_of("qa", r128(a["q_a_norm_g"]), 4)
        rows_of("kva", r128(a["kv_a_norm_g"]), 4)
        rows_of("lb", a["hgrn_lb_logits_2"].rearrange("l (k p) -> (l k) p", p=P), 16)
        rows_of("qn", a["q_norm_g_2"], 1)
        rows_of("kn", a["k_norm_g_2"], 1)
        rows_of("on", a["hgrn_out_norm_g_2"], 1)
        rows_of("ikn", a["idx_k_norm_g_2"], 1)
        meta_load = load(x_meta[0:NMETA, :], a["meta_tokens_2"])

        def columns(n0, n, waits):
            b = side_banks.next()
            PE.wait([ident_load, *b.free, *waits])
            t = PE.mark(nc.tensor.transpose(b.ap[:, 0:n], rows_in[n0:n0 + n, :], c("ident")[n0:n0 + n, n0:n0 + n]))
            b.free = [dve([t], v.tensor_copy, cols[:, n0:n0 + n], b.ap[:, 0:n])]
            return b.free[0]

        pre_done = columns(0, 16, [row_loads[0]])

        x_marks, h_marks, x_sq, x_kept, x_in_free = [], [], [None], [], []
        x_dram = nc.dram_tensor("x_kept", [P, KT * S], F32, kind="Internal").ap()

        def x_lo(k):
            h_marks[k].append(dve([h_marks[k][0]], v.scalar_tensor_tensor, hb_lo[:, k, :], xT[:, k, :],
                                  col("pre", k), hb_hi[:, k, :].bitcast(F32), ALU.mult, ALU.subtract))

        def x_tile(k):
            b = side_banks.next()
            PE.wait([ident_load, x_load[k // XC], *b.free])
            for blk in range(2):
                t = nc.tensor.transpose(b.ap[:, blk * P:(blk + 1) * P], x_in[:, blk, k * P:(k + 1) * P], c("ident"))
            t = PE.mark(t)
            x_marks.append(dve([t], v.tensor_copy, xT[:, k, :], b.ap[:, 0:S]))
            b.free = [x_marks[-1]]
            h_marks.append([act([x_marks[-1], pre_done], hb_hi[:, k, :], xT[:, k, :], ACT.Copy, scale=col("pre", k))])
            x_sq[0] = add_square(acc_b, xT[:, k, :], x_marks[k], x_sq[0])
            if k:
                x_lo(k - 1)
            if k == KT - 1:
                x_lo(k)
                x_in_free.append(t)
                x_kept.append(load(x_dram, xT.rearrange("p k n -> p (k n)"), x_marks, q=SC))
                pending.appendleft(factor_job(factor[:, 0, 0:S], acc_b, x_sq[0], D, S, r1_marks, delay=1))

        r1_marks = []

        for k in range(KT):
            if k < 6:
                x_tile(k)
            else:
                later(lambda k=k: x_tile(k), 2 * (k - 5))
            if k in (2, 4):
                issue_split()
        h_ready = lambda kt: h_marks[kt]

        MAGIC = 1.5 * 2.0 ** 23
        cols_done, rope_done, tp_done = [], [], []
        pos_f = small[0:1, 0:S]
        cos1, sin1 = rope1[:, 0, :], rope1[:, 1, :]

        def vectors():
            for _ in range(5):
                yield
            b = side_banks.next()
            PE.wait([con_load, rows_zero, *row_loads, *b.free])
            t = PE.mark(nc.tensor.transpose(b.ap[:, 0:P], rows_in, c("ident")))
            cols_done.append(dve([t, pre_done], v.tensor_copy, cols[:, 16:P], b.ap[:, 16:P]))
            b.free = cols_done[0:1]
            tp_done.append(dve([pos_load], v.tensor_copy, pos_f, pos_i))
            yield
            bp = side_banks.next()
            PE.wait([*tp_done, con_load, *bp.free])
            tp = PE.mark(mm(bp.ap[:, 0:S], c("ones")[0:1, :], pos_f))
            tp_done.append(tp)
            ang, turns = scratch.next(), scratch.next()
            ta = dve([tp] + ang.free, v.tensor_scalar, ang.ap[:, 0:S], bp.ap[:, 0:S], c("inv_freq"), None, ALU.mult)
            bp.free = [ta]
            sines = []
            for which, shift in ((1, 0.0), (0, 0.25)):
                yield
                dst = rope1[:, which, :]
                k_ = turns.ap[:, 0:S]
                tk = dve([ta] + turns.free, v.tensor_scalar, k_, ang.ap[:, 0:S], 1.0 / (2 * np.pi), shift, ALU.mult, ALU.add)
                tk = dve([tk], v.tensor_scalar, k_, k_, MAGIC, MAGIC, ALU.add, ALU.subtract)
                yield
                tk = dve([tk], v.scalar_tensor_tensor, dst, k_, -6.28125, ang.ap[:, 0:S], ALU.mult, ALU.add)
                tk = dve([tk], v.scalar_tensor_tensor, dst, k_, -0.0019350051879882812, dst, ALU.mult, ALU.add)
                tk = dve([tk], v.scalar_tensor_tensor, dst, k_, -3.0199159819e-07, dst, ALU.mult, ALU.add)
                yield
                if shift:
                    tk = dve([tk], v.tensor_scalar, dst, dst, np.pi / 2, None, ALU.add)
                tk = dve([tk], v.tensor_scalar, dst, dst, 3.14159250, -3.14159250, ALU.min, ALU.max)
                sines.append(act([tk], dst, dst, ACT.Sin))
            ang.free = turns.free = [tk]
            rope_done.extend(sines)
            yield
            l0, l1 = cols[:, ROWS["lb"]:ROWS["lb"] + 8], cols[:, ROWS["lb"] + 8:ROWS["lb"] + 16]
            tl = dve([cols_done[0]], v.tensor_tensor, mx, l0, l1, ALU.max)
            tl = dve([tl], v.tensor_tensor, lbx[:, 0:8], l0, mx, ALU.subtract)
            tl = dve([tl], v.tensor_tensor, lbx[:, 8:16], l1, mx, ALU.subtract)
            tl = act([tl], lbx, lbx, ACT.Exp)
            yield
            yield
            tl = dve([tl], v.tensor_tensor, mx, lbx[:, 0:8], lbx[:, 8:16], ALU.add)
            tl = dve([tl], v.reciprocal, mx, mx)
            tl1 = dve([tl], v.tensor_tensor, lb, lbx[:, 0:8], mx, ALU.mult)
            lb_done.append(dve([tl1], v.tensor_tensor, oml, lbx[:, 8:16], mx, ALU.mult))
            yield from meta_transposes()

        small2, small3 = sb("small2", [P, 64]), sb("small3", [P, 2 * HI])
        lbx, lb, oml, mx = small2[:, 16:32], small2[:, 0:8], small2[:, 8:16], small2[:, 32:40]
        lb_done = []

        def constants():
            for q in (PE, VE, SC, GP):
                q.wait([con_load])
            yield

        pending.append(constants())
        pending.append(vectors())

        R_, RR, RQ = factor[:, 0, 0:S], factor[:, 1, 0:S], factor[:, 2, 0:S]
        RKV = RR

        lat_marks = {}
        lat_sq = {}
        rq_done, rkv_done = [], []
        rkv_col = small2[:, 56:58]

        def latent(which, base, gname, done_list, dst_factor):
            def f(g, m, ps, done):
                x = LAT[:, base + m, :]
                t = dve([done, r1_marks[0]], v.tensor_tensor, x, ps, R_, ALU.mult)
                acc = acc_a if which == "q" else acc_b
                tq = lat_sq[which] = add_square(acc, x, t, lat_sq.get(which))

                def split():
                    lat_marks[which, m] = split_to(ob_hi[:, base + m, 0:S], ob_lo[:, base + m, 0:S], x, t, [],
                                                   gain=col(gname, m))
                later(split)
                if m == 3:
                    pending.append(factor_job(dst_factor, acc, tq, LORA, S, done_list,
                                              delay=4, keep=None if which == "q" else rkv_col))
                return [t]
            return f

        evac["qa"] = latent("q", 0, "qa", rq_done, RQ)
        evac["kva"] = latent("kv", 4, "kva", rkv_done, RKV)

        kr_done = []

        def rope_tile(x, x_done, rot, cos, sin, rope_ready, width, dup=None, rows=P):
            b = side_banks.next()
            PE.wait(b.free + [x_done] + rope_ready)
            t = PE.mark(mm(b.ap[:, 0:width], rot[0:rows, :], x[0:rows, :]))
            s = scratch.next()
            t1 = dve([t] + s.free + rope_ready, v.tensor_tensor, s.ap[:, 0:width], b.ap[:, 0:width], sin, ALU.mult)
            b.free = [t1]
            if dup is not None:
                b = side_banks.next()
                PE.wait(b.free)
                t = PE.mark(mm(b.ap[:, 0:width], dup[0:rows, :], x[0:rows, :]))
                t2 = dve([t], v.tensor_tensor, x, b.ap[:, 0:width], cos, ALU.mult)
                b.free = [t2]
            else:
                t2 = pool([x_done, t] + rope_ready, gp.tensor_tensor, x, x, cos, ALU.mult)
            t = pool([t1, t2], gp.tensor_tensor, x, x, s.ap[:, 0:width], ALU.add)
            s.free = [t]
            return t

        def evac_kr(g, m, ps, done):
            t = dve([done], v.tensor_tensor, kr1[:, :], ps, R_, ALU.mult)

            def job():
                yield
                kr_done.append(rope_tile(kr1[:, :], t, c("rot_k1"), cos1, sin1, rope_done, S, dup=c("dup64")))
            pending.append(job())
            return [t]

        evac["kr"] = evac_kr
        q_done, qr_done, k_done, v_done = {}, {}, {}, {}

        def evac_q(g, m, ps, done):
            if m < 2:
                h = 2 * g + m
                t = q_done[h] = dve([done, *x_in_free, *rq_done], v.tensor_tensor, Q1[:, h, :], ps, RQ, ALU.mult)
                return [t]
            t = dve([done, *meta_free], v.tensor_tensor, QR[:, g, :], ps, RQ, ALU.mult)

            def job():
                yield
                qr_done[g] = rope_tile(QR[:, g, :], t, c("rot_q1"), cos1, sin1, rope_done, S)
                yield
            pending.append(job())
            return [t]

        evac["q"] = evac_q

        def evac_kvb(g, m, ps, done):
            if m < 2:
                h = 2 * g + m
                t = k_done[h] = dve([done, *rkv_done], v.tensor_tensor, K1[:, h, :], ps, RKV, ALU.mult)
            else:
                blk = m - 2
                t = act([done, *rkv_done, lat_free], V1[:, blk, g * S:(g + 1) * S], ps, ACT.Copy,
                        scale=rkv_col[:, blk:blk + 1])
                v_done[2 * g] = v_done[2 * g + 1] = t
            return [t]

        evac["kv"] = evac_kvb

        attn_done = {}

        def attention1(h):
            half = 64 * (h % 2)
            kr, qr = kr1[half:half + 64, :], QR[half:half + 64, h // 2, :]
            b = side_banks.next()
            PE.wait(b.free + [q_done[h], qr_done[h // 2], k_done[h], *kr_done])
            mm(b.ap[:, 0:P], Q1[:, h, 0:P], K1[:, h, 0:P], True, False)
            mm(b.ap[:, 0:P], qr[:, 0:P], kr[:, 0:P], False, True)
            mm(b.ap[:, P:3 * P], Q1[:, h, P:S], K1[:, h, :], True, False)
            t = PE.mark(mm(b.ap[:, P:3 * P], qr[:, P:S], kr, False, True))
            p, st = prob.next(), stats.next()
            dve([t] + p.free, v.scalar_tensor_tensor, p.ap[:, 0:P], b.ap[:, 0:P], SCALE1, c("mask1")[:, P:S],
                ALU.mult, ALU.add)
            t = dve([], v.scalar_tensor_tensor, p.ap[:, P:384], b.ap[:, P:384], SCALE1, c("mask1"),
                    ALU.mult, ALU.add)
            b.free = [t]
            parts = ((0, P), (P, 3 * P))
            done = softmax(p, st, parts, t)
            yield
            yield
            pt = probT.next()
            b = side_banks.next()
            PE.wait(b.free + done)
            for j in range(3):
                i = nc.tensor.transpose(b.ap[:, j * P:(j + 1) * P], p.ap[:, j * P:(j + 1) * P], c("ident"))
            t = PE.mark(i)
            p.free = [t]
            t = act([t] + pt.free, pt.ap[:, 0:384], b.ap[:, 0:384], ACT.Copy)
            b.free = [t]
            yield
            b = side_banks.next()
            PE.wait(b.free + [t, v_done[h]])
            mm(b.ap[:, 0:S], V1[:, 0, h * P:(h + 1) * P], pt.ap[:, 0:S], True, False)
            t = PE.mark(mm(b.ap[:, P:S], V1[:, 1, h * P:(h + 1) * P], pt.ap[:, S:384], False, True))
            pt.free = [t]
            attn_done[h] = act([t], Q1[:, h, :], b.ap[:, 0:S], ACT.Copy)
            b.free = [attn_done[h]]

        def softmax(p, st, parts, t):
            n = len(parts)
            tm = [dve([t] + st.free, v.tensor_reduce, st.ap[:, i:i + 1], p.ap[:, lo:hi], AX, ALU.max, negate=True)
                  for i, (lo, hi) in enumerate(parts)]
            te = [act([tm[i]], p.ap[:, lo:hi], p.ap[:, lo:hi], ACT.Exp, bias=st.ap[:, i:i + 1],
                      accum_out=st.ap[:, 2 + i:3 + i]) for i, (lo, hi) in enumerate(parts)]
            tr = dve(te, v.reciprocal, st.ap[:, 4:4 + n], st.ap[:, 2:2 + n])
            done = [dve([tr], v.tensor_scalar, p.ap[:, lo:hi], p.ap[:, lo:hi], st.ap[:, 4 + i:5 + i], None, ALU.mult)
                    for i, (lo, hi) in enumerate(parts)]
            st.free = done
            return done

        metaT = small
        meta_free, meta_done = [], []

        def meta_transposes():
            yield
            b = side_banks.next()
            PE.wait([meta_load, ident_load, *b.free])
            for k in range(KT):
                i = nc.tensor.transpose(b.ap[:, k * NMETA:(k + 1) * NMETA], x_meta[0:NMETA, k * P:(k + 1) * P],
                                        c("ident")[0:NMETA, 0:NMETA])
            meta_free.append(PE.mark(i))
            meta_done.append(act([*meta_free, *tp_done], metaT[:, :], b.ap[:, 0:KT * NMETA], ACT.Copy))
            b.free = [*meta_done]

        conv_t, cin_t = {}, {}
        u_t, gate_t = region(56, 4, 4, S), region(60, 4, 4, S)
        oc_marks, conv_free = {}, {}

        def conv_evacs(j):
            def cin(g, m, ps, done):
                cin_t[m] = dve([done, rr_done, *conv_free[m]], v.tensor_tensor, gate_t[:, m, :], ps, RR, ALU.mult)
                return [cin_t[m]]

            def cgate(g, m, ps, done):
                k = 4 * j + m
                s = scratch.next()
                u, y = s.ap[:, 0:S], u_t[:, m, :]
                tu = dve([done, cin_t[m]] + s.free, v.tensor_tensor, u, ps, gate_t[:, m, :], ALU.mult)
                t1 = act([tu, *conv_free[m]], y, u, ACT.Copy, scale=col("conv", 32 + k))

                def taps():
                    t = dve([t1, tu], v.scalar_tensor_tensor, y[:, 1:S], u[:, 0:S - 1], col("conv", 16 + k),
                            y[:, 1:S], ALU.mult, ALU.add)
                    t = dve([t], v.scalar_tensor_tensor, y[:, 2:S], u[:, 0:S - 2], col("conv", k), y[:, 2:S],
                            ALU.mult, ALU.add)
                    s.free = [t]
                    conv_t[m] = t
                later(taps, 5)
                return [tu]

            def bgate(g, m, ps, done):
                y = u_t[:, m, :]
                t = dve([done, conv_t[m]], v.tensor_tensor, y, ps, y, ALU.mult)
                conv_t[m] = pool([t], gp.tensor_tensor, y, y, R_, ALU.mult)
                return [t]

            def zconv(g, m, ps, done):
                k = 4 * j + m
                y = u_t[:, m, :]
                s, s2 = scratch.next(), head_factors.next()
                z, sg = s.ap[:, 0:S], s2.ap[:, 0:S]
                tz = dve([done] + s.free, v.tensor_tensor, z, ps, R_, ALU.mult)
                t = act([tz] + s2.free, sg, z, ACT.Sigmoid)
                t = pool([t, tz], gp.tensor_tensor, z, z, sg, ALU.mult)
                s2.free = [t]
                t = pool([t, conv_t[m]], gp.tensor_tensor, y, z, y, ALU.mult)
                s.free = [t]

                def split():
                    conv_free[m] = oc_marks[k] = split_to(ob_hi[:, k, 0:S], ob_lo[:, k, 0:S], y, t, lat_read)
                later(split, 7)
                return [tz]
            return cin, cgate, bgate, zconv


        for ph_ in (p_qa, p_kv, p_kr, *[x for _, x in p_conv], p_gc, p_zm, p_gm):
            ph_.ready = h_ready
        run(p_qa)
        run(p_kv)
        run(p_kr)
        conv_free.update({m: [x_sq[0], *x_kept, *h_marks[KT - 1]] for m in range(4)})
        flush()
        p_q.ready = lambda kt: lat_marks["q", kt]
        p_k.ready = lambda kt: lat_marks["kv", kt]
        run(p_q)
        lat_free = lat_marks["kv", 3][1]
        run(p_k)
        flush()
        rr_done = pool([r1_marks[0], k_done[15]], gp.tensor_tensor, RR, R_, R_, ALU.mult)
        lat_read = [(PE.sem, PE.count)]
        pending.extend(attention1(h) for h in range(H1))
        for j, p_ in p_conv:
            for name, f in zip(("cin", "cgate", "bgate", "zconv"), conv_evacs(j)):
                evac[f"{name}{j}"] = f
            run(p_)
        if pending or active:
            drain_jobs()

        def sigmoid_to(dst, factor_, fdone, marks, key, free=()):
            def f(g, m, ps, done):
                k = 4 * g + m
                s = scratch.next()
                tz = dve([done, fdone] + s.free, v.tensor_tensor, s.ap[:, 0:S], ps, factor_, ALU.mult)
                marks[key, k] = act([tz, *free], dst[:, k, :], s.ap[:, 0:S], ACT.Sigmoid)
                s.free = [marks[key, k]]
                return [tz]
            return f

        gate = {}
        evac["gconv"] = sigmoid_to(G1, R_, r1_marks[0], gate, "gc", sum(conv_free.values(), []))
        run(p_gc)

        def evac_oc(g, m, ps, done):
            k = 4 * g + m
            gate["yc", k] = dve([done, gate["gc", k]], v.tensor_tensor, G1[:, k, :], ps, G1[:, k, :], ALU.mult)
            return [gate["yc", k]]

        evac["oconv"] = evac_oc
        flush()
        p_oc.ready = lambda kt: oc_marks[kt]
        run(p_oc)
        oc_read = [(PE.sem, PE.count)]
        zm, zm_pool, zm_read = {}, {}, []

        def silu_times(ring, y, y_marks, factor_, fdone, dst_hi, dst_lo, free, marks, wait=0):
            def f(g, m, ps, done):
                k = 4 * g + m
                s, s2 = scratch.next(), ring.next()
                z, sg = s.ap[:, 0:S], s2.ap[:, 0:S]
                tz = dve([done, fdone] + s.free, v.tensor_tensor, z, ps, factor_, ALU.mult)
                t1 = act([tz] + s2.free, sg, z, ACT.Sigmoid)

                def gate_y():
                    t = pool([t1, tz], gp.tensor_tensor, z, z, sg, ALU.mult)
                    s2.free = [t]
                    t = zm_pool[k] = pool([t, y_marks[k]], gp.tensor_tensor, y[:, k, :], z, y[:, k, :], ALU.mult)
                    s.free = [t]

                def split():
                    marks[k] = split_to(dst_hi(k), dst_lo(k), y[:, k, :], zm_pool[k], free)
                    zm_read[:] = marks[k]
                if wait:
                    later(gate_y, wait)
                else:
                    gate_y()
                later(split, 7)
                return [tz]
            return f

        evac["zmla"] = silu_times(head_factors, Q1, attn_done, R_, r1_marks[0], *ob, oc_read, zm)
        run(p_zm)
        evac["gmla"] = sigmoid_to(GM, R_, r1_marks[0], gate, "gm", list(attn_done.values()))
        run(p_gm)
        hb_read = [(PE.sem, PE.count)]
        mg, gm_read = {}, []

        def evac_om(g, m, ps, done):
            k = 4 * g + m
            s = scratch.next()
            z, y = s.ap[:, 0:S], G1[:, k, :]
            tz = dve([done, gate["gm", k]] + s.free, v.tensor_tensor, z, ps, GM[:, k, :], ALU.mult)
            t = pool([tz, gate["yc", k]], gp.tensor_tensor, y, z, y, ALU.add)
            gm_read[:] = [tz]
            s.free = [t]

            def split():
                mg[k] = split_to(hb_hi[:, k, :], hb_lo[:, k, :], y, t, hb_read)
            later(split, 7)
            return [tz]

        evac["omla"] = evac_om
        p_om.ready = lambda kt: zm[kt]
        run(p_om)
        ob_read = [(PE.sem, PE.count)]
        out_t, sq_t = {}, [None]

        def evac_w(g, m, ps, done):
            k = 4 * g + m
            if k < KT - 1:
                t = sq_t[0] = add_square(acc_a, ps, done, sq_t[0])
            else:
                t = last_sq[0] = act([done], last_square, ps, ACT.Square)
            out_t[k] = act([done, *attn_done.values()], OUT1[:, k, :], ps, ACT.Copy, scale=col("post", k))
            return [t, out_t[k]]

        last_sq, last_slot = [None], head_factors.next()
        last_square = last_slot.ap[:, 0:S]
        evac["wout"] = evac_w
        p_w.ready = lambda kt: mg[kt]
        p_w.hold = True
        metaf = metaT[:, :].rearrange("p (k n) -> p k n", k=KT)
        meta_marks, acc_m = [], small2[:, 40:56]
        m_marks, lvl_marks = [], []
        F2 = factor[:, 1, :]

        def meta_operand():
            yield
            gains = cols[:, ROWS["norm2"]:ROWS["norm2"] + KT].unsqueeze(2).to_broadcast([P, KT, NMETA])
            s, s2 = scratch.next(), scratch.next()
            prod = s.ap[:, 0:S].rearrange("p (k n) -> p k n", k=KT)
            t = dve([meta_done[0]] + s.free, v.tensor_tensor, prod, metaf, gains, ALU.mult)
            tq = act([meta_done[0]] + s2.free, s2.ap[:, 0:S], metaT[:, :], ACT.Square)
            yield
            meta_marks.extend(split_to(ob_hi[:, :, 0:NMETA], ob_lo[:, :, 0:NMETA], prod, t, ob_read))
            s.free = [*meta_marks]
            tm = dve([tq], v.tensor_reduce, acc_m, s2.ap[:, 0:S].rearrange("p (k n) -> p n k", k=KT), AX, ALU.add)
            s2.free = [tm]
            yield
            yield from factor_job(F2[:, 0:NMETA], acc_m, tm, D, NMETA, m_marks)

        pending.append(meta_operand())
        x_again = load(XR.rearrange("p k n -> p (k n)"), x_dram, gm_read + x_kept)
        run(p_w)
        drain_jobs()
        hb2_read = [(PE.sem, PE.count)]

        PE.wait(last_sq)
        rp = []
        for _ in factor_job(RQ, acc_a, sq_t[0], D, S, rp, more=last_square):
            pass
        rp_done = rp[0]
        last_slot.free = [rp_done]
        x1_marks, h2_marks, sq2 = [], [], [None]
        f2, arena_free = [], []
        x1_dram = nc.dram_tensor("x1_kept", [P, KT * S], F32, kind="Internal").ap()

        scaled, squared = {}, {}

        def x1_scale(k):
            o = OUT1[:, k, :]
            if k < 2:
                scaled[k] = dve([rp_done, out_t[k]], v.tensor_tensor, o, o, RQ, ALU.mult)
            else:
                scaled[k] = pool([rp_done, out_t[k]], gp.tensor_tensor, o, o, RQ, ALU.mult)

        def x1_finish(k):
            sq, t = squared[k]
            if k == KT - 1:
                last_x1.append(t)
            elif sq2[0] is None:
                sq2[0] = pool([t], gp.tensor_copy, acc_b, sq.ap[:, 0:S])
            else:
                sq2[0] = pool([t, sq2[0]], gp.tensor_tensor, acc_b, acc_b, sq.ap[:, 0:S], ALU.add)
            if k < KT - 1:
                sq.free = [sq2[0]]
            h2_marks[k].append(dve([h2_marks[k][0], x1_marks[k]], v.scalar_tensor_tensor, ob_lo[:, k, NMETA:T],
                                   XR[:, k, :], col("norm2", k), ob_hi[:, k, NMETA:T].bitcast(F32),
                                   ALU.mult, ALU.subtract))

        def x1_tile(k):
            if k == 0:
                x1_scale(0)
            if k + 2 < KT:
                x1_scale(k + 2)
            x = XR[:, k, :]
            t = dve([scaled[k], x_again], v.tensor_tensor, x, OUT1[:, k, :], x, ALU.add)
            if k == 0:
                x1_scale(1)
            x1_marks.append(t)
            hi = act([t], ob_hi[:, k, NMETA:T], x, ACT.Copy, scale=col("norm2", k))
            h2_marks.append([hi, *meta_marks])
            sq = scratch.next()
            squared[k] = sq, act([t] + sq.free, sq.ap[:, 0:S], x, ACT.Square)
            if k:
                x1_finish(k - 1)
            if k == KT - 1:
                x1_finish(k)
                x1_kept = load(x1_dram, XR.rearrange("p k n -> p (k n)"), x1_marks)
                arena_free.extend([x1_marks[-1], sq2[0], x1_kept, h2_marks[-1][0], h2_marks[-1][-1]])
                x1_in_dram.append(x1_kept)
                pending.appendleft(factor2())

        x1_in_dram, last_x1 = [], []

        def factor2():
            yield
            PE.wait(last_x1)
            sq = squared[KT - 1][0]
            yield from factor_job(F2M, acc_b, sq2[0], D, S, f2, more=sq.ap)
            sq.free = [f2[0]]

        F2M = F2[:, NMETA:T]
        for k in range(KT):
            if k < 6:
                x1_tile(k)
            else:
                later(lambda k=k: x1_tile(k), 2 * (k - 5))

        QI, KI = region(0, 8, 8, S), region(8, 2, T)
        KA, QA, VA = region(9.25, 4.25, KVA, T), region(13.5, 8, HA, S), region(21.5, 6, 3, 512)
        FB, IB, QB = region(27.5, 8.5, HB, T), region(36, 12, 3, 1024), region(48, 8, HB, S)
        GA = region(56, 16, KT, S)
        L0 = CONSTS["late"][0]
        late = region(58, 6, CONSTS["late"][1] - L0)
        bias2, score2 = region(65, 2, 416), region(67, 2, 416)
        mg_split = [x for m in mg.values() for x in m]
        late_load = load(late, a["const_f"][:, L0:CONSTS["late"][1]], mg_split)
        n_lvl = len(LEVELS) * P // 2
        lvl = small[:, 0:n_lvl // 4].bitcast(U8)
        lvl_in = region(69, 2, n_lvl)
        lvl_load = load(lvl_in, a["const_lvl"], mg_split)

        def lc(name):
            lo, hi = CONSTS[name]
            return late[:, lo - L0:hi - L0]

        for p_ in (p2_ki, p2_qi, p2_ka, p2_va, p2_qa, p2_fb, p2_ib, p2_qb, p2_ga, p2_za, p2_zb, p2_gb):
            p_.ready = lambda kt: h2_marks[kt]

        wiT = small3[:, :]
        ki_done, wi_done, qi_done = [], [], {}

        def evac_ki(g, m, ps, done):
            t = dve([done, *f2, *m_marks, *arena_free], v.tensor_tensor, KI, ps, F2, ALU.mult)

            def job():
                yield
                b = side_banks.next()
                PE.wait(b.free + [t])
                for blk in range(2):
                    i = nc.tensor.transpose(b.ap[:, blk * P:(blk + 1) * P],
                                            KI[:, NMETA + blk * P:NMETA + (blk + 1) * P], c("ident"))
                t1 = PE.mark(i)
                wi_done.append(dve([t1], v.tensor_scalar, wiT.rearrange("p (b h) -> p b h", b=2),
                                   b.ap[:, 0:S].rearrange("p (b n) -> p b n", b=2)[:, :, DI:DI + HI],
                                   W_SCALE, None, ALU.mult))
                b.free = wi_done
                f = head_factors.next()
                tf = act(f.free + [t], f.ap[0:DI, :], KI[0:DI, :], ACT.Square)
                yield
                b, tf = yield from row_factor(f.ap, tf, DI, T, rows=DI, wait=2)
                t2 = dve([tf, t1], v.tensor_tensor, KI[0:DI, :], KI[0:DI, :], b.ap[0:DI, 0:T], ALU.mult)
                b.free = f.free = [t2]
                t2 = act([t2], KI[0:DI, :], KI[0:DI, :], ACT.Copy, scale=col("ikn")[0:DI, :])
                yield
                yield
                ki_done.append(rope_tile(KI, t2, lc("rot_i"), lc("cos_i"), lc("sin_i"), [late_load], T,
                                         dup=c("dup64"), rows=DI))
                pending.extend(index_head(h) for h in range(HI))
            pending.append(job())
            return [t]

        evac["ki"] = evac_ki

        def evac_qi(g, m, ps, done):
            k = 4 * g + m
            t = dve([done, *f2, *arena_free], v.tensor_tensor, QI[:, k, :], ps, F2M, ALU.mult)

            def job():
                yield
                qi_done[k] = rope_tile(QI[:, k, :], t, lc("rot_i1"), lc("cos_i")[:, NMETA:T],
                                       lc("sin_i")[:, NMETA:T], [late_load], S)
            pending.append(job())
            return [t]

        evac["qi"] = evac_qi

        def rms_rope_head(dst, ps, done, fac, width, lo, gname, marks, k):
            t = dve([done, *f2, *arena_free], v.tensor_tensor, dst, ps, fac, ALU.mult)

            def job():
                f = head_factors.next()
                tf = act(f.free + [t], f.ap[:, 0:width], dst, ACT.Square)
                yield
                b, tf = yield from row_factor(f.ap, tf, P, width, wait=2)
                t2 = dve([tf], v.scalar_tensor_tensor, dst, dst, col(gname), b.ap[:, 0:width], ALU.mult, ALU.mult)
                b.free = f.free = [t2]
                yield
                yield
                marks[k] = rope_tile(dst, t2, lc("rot_a"), lc("cos_a")[:, lo:T], lc("sin_a")[:, lo:T],
                                     [late_load], width)
            pending.append(job())
            return [t]

        ka_done, qa_done, va_done = {}, {}, {}
        evac["ka"] = lambda g, m, ps, done: rms_rope_head(KA[:, m, :], ps, done, F2, T, 0, "kn", ka_done, m)

        q_factor = sb("q_factor", [P, 2 * HA])
        q_gain = small2[:, 58:59]
        q_gain_done, q_factor_done = [], {}

        def evac_qa2(g, m, ps, done):
            h = 4 * g + m
            dst = QA[:, h, :]
            t = dve([done, *f2, *arena_free], v.tensor_tensor, dst, ps, F2M, ALU.mult)

            def job():
                if not q_gain_done:
                    q_gain_done.append(dve([], v.tensor_scalar, q_gain, col("qn"), SCALE2, None, ALU.mult))
                f, st = head_factors.next(), stats.next()
                tf = act(f.free + [t], f.ap[:, 0:S], dst, ACT.Square)
                t2 = act([tf, *q_gain_done], dst, dst, ACT.Copy, scale=q_gain)
                yield
                b = side_banks.next()
                PE.wait(b.free + [tf])
                for j in range(2):
                    i = mm(b.ap[:, j:j + 1], f.ap[:, j * P:(j + 1) * P], c("ones")[:, 0:1])
                t3 = PE.mark(i)
                f.free = [t3]
                t3 = dve([t3] + st.free, v.tensor_scalar, st.ap[:, 0:2], b.ap[:, 0:2], 1.0 / P, EPS, ALU.mult, ALU.add)
                b.free = [t3]
                q_factor_done[h] = pool([t3], gp.tensor_tensor, q_factor[:, 2 * h:2 * h + 2], st.ap[:, 0:2],
                                        c("neg_half").to_broadcast([P, 2]), ALU.pow)
                st.free = [q_factor_done[h]]
                yield
                qa_done[h] = rope_tile(dst, t2, lc("rot_a"), lc("cos_a")[:, NMETA:T], lc("sin_a")[:, NMETA:T],
                                       [late_load], S)
            pending.append(job())
            return [t]

        evac["qa2"] = evac_qa2

        def token_major(dst, marks):
            def f(g, m, ps, done):
                k = 4 * g + m
                s = scratch.next()
                t_out = dve([done, *f2, *arena_free] + s.free, v.tensor_tensor, s.ap, ps, F2, ALU.mult)

                def job():
                    b = side_banks.next()
                    PE.wait(b.free + [t_out])
                    for blk in range(2):
                        nc.tensor.transpose(b.ap[:, blk * P:(blk + 1) * P],
                                            s.ap[:, NMETA + blk * P:NMETA + (blk + 1) * P], c("ident"))
                    i = nc.tensor.transpose(b.ap[0:NMETA, S:S + P], s.ap[:, 0:NMETA], c("ident"))
                    t = PE.mark(i)
                    s.free = [t]
                    w = slice(k * P, (k + 1) * P)
                    act([t], dst[:, 1:3, w], b.ap[:, 0:S].rearrange("p (b n) -> p b n", b=2), ACT.Copy)
                    marks[k] = act([], dst[0:NMETA, 0, w], b.ap[0:NMETA, S:S + P], ACT.Copy)
                    b.free = [marks[k]]
                later(job, 4)
                return [t_out]
            return f

        evac["va"] = token_major(VA, va_done)
        ib_done = {}
        evac["ib"] = token_major(IB, ib_done)

        KEYS = (NMETA + P, T)
        PART = ((0, KEYS[0]), (KEYS[0], KEYS[0] + KEYS[1]))
        chain = {"score": None, "bias": None}

        def index_head(h):
            half = 64 * (h % 2)
            b = side_banks.next()
            PE.wait(b.free + [qi_done[h // 2], *ki_done])
            for blk, (lo, hi) in enumerate(PART):
                i = mm(b.ap[:, lo:hi], QI[half:half + 64, h // 2, blk * P:(blk + 1) * P],
                       KI[half:half + 64, 0:KEYS[blk]])
            t = PE.mark(i)
            p = prob.next()
            t = act([t] + p.free, p.ap, b.ap[:, 0:416], ACT.Relu)
            b.free = [t]
            yield
            for blk, (lo, hi) in enumerate(PART):
                w = wiT[:, blk * HI + h:blk * HI + h + 1]
                if h == 0:
                    ts = dve([t, *wi_done, *arena_free], v.tensor_scalar, score2[:, lo:hi], p.ap[:, lo:hi], w, None, ALU.mult)
                else:
                    ts = dve([t, chain["score"]], v.scalar_tensor_tensor, score2[:, lo:hi], p.ap[:, lo:hi], w,
                             score2[:, lo:hi], ALU.mult, ALU.add)
            p.free = [ts]
            chain["score"] = ts
            if h == HI - 1:
                pending.append(select())

        best = sb("best", [P, 16])

        def select():
            t = chain["score"]
            for blk, (lo, hi) in enumerate(PART):
                t = dve([t], v.memset, score2[0:CHUNK, hi - CHUNK:hi], MASKED)
            for r in range(TOPK // 8):
                yield
                for blk, (lo, hi) in enumerate(PART):
                    m8 = best[:, 8 * blk:8 * blk + 8]
                    t8 = dve([t], v.max, m8, score2[:, lo:hi])
                    t = dve([t8], v.match_replace, score2[:, lo:hi], m8, score2[:, lo:hi], TAKEN)
            chain["bias"] = dve([t], v.tensor_scalar, bias2, score2, (MASKED + TAKEN) / 2, NEG, ALU.is_gt, ALU.mult)
            pending.extend(attention2(h) for h in range(HA))

        ya_done = {}

        prob_meta = Ring([rope1[0:NMETA, i, :] for i in range(2)])

        def attention2(h):
            g = h // 2
            b = side_banks.next()
            PE.wait(b.free + [qa_done[h], ka_done[g]])
            for blk, (lo, hi) in enumerate(PART):
                i = mm(b.ap[:, lo:hi], QA[:, h, blk * P:(blk + 1) * P], KA[:, g, 0:KEYS[blk]])
            t = PE.mark(i)
            p, st = prob.next(), stats.next()
            for blk, (lo, hi) in enumerate(PART):
                t = dve([t, chain["bias"], q_factor_done[h]] + p.free, v.scalar_tensor_tensor, p.ap[:, lo:hi],
                        b.ap[:, lo:hi], q_factor[:, 2 * h + blk:2 * h + blk + 1], bias2[:, lo:hi], ALU.mult, ALU.add)
            b.free = [t]
            done = softmax(p, st, PART, t)
            yield
            yield
            pt = probT.next()
            b, b2 = side_banks.next(), side_banks.next()
            PE.wait(b.free + b2.free + done)
            lo0, lo1 = PART[0][0] + NMETA, PART[1][0] + NMETA
            for j, lo in enumerate((lo0, lo1, lo1 + P)):
                nc.tensor.transpose(b.ap[:, j * P:(j + 1) * P], p.ap[:, lo:lo + P], c("ident"))
            for blk in range(2):
                lo = PART[blk][0]
                i = nc.tensor.transpose(b2.ap[0:NMETA, blk * P:(blk + 1) * P], p.ap[:, lo:lo + NMETA], c("ident"))
            t = PE.mark(i)
            p.free = [t]
            t1 = act([t] + pt.free, pt.ap[:, 0:384], b.ap[:, 0:384], ACT.Copy)
            b.free = [t1]
            ptm = prob_meta.next()
            t = act(ptm.free, ptm.ap, b2.ap[0:NMETA, 0:S], ACT.Copy)
            b2.free = [t]
            yield
            b = side_banks.next()
            w = slice(g * P, (g + 1) * P)
            PE.wait(b.free + [t, va_done[g]])
            mm(b.ap[:, 0:S], VA[:, 1, w], pt.ap[:, 0:S], True, False)
            mm(b.ap[:, P:S], VA[:, 2, w], pt.ap[:, S:384], False, False)
            t = PE.mark(mm(b.ap[:, 0:S], VA[0:NMETA, 0, w], ptm.ap, False, True))
            pt.free = ptm.free = [t]
            ya_done[h] = act([t], QA[:, h, :], b.ap[:, 0:S], ACT.Copy)
            b.free = [ya_done[h]]

        fb_done, qb_done = {}, {}

        def evac_fb(g, m, ps, done):
            k = 4 * g + m
            s = scratch.next()
            t = dve([done, *f2] + s.free, v.tensor_tensor, s.ap, ps, F2, ALU.mult)
            t1 = act([t, *arena_free], FB[:, k, :], s.ap, ACT.Sigmoid)
            s.free = [t1]

            def forget():
                fb_done[k] = dve([t1, *lb_done], v.tensor_scalar, FB[:, k, :], FB[:, k, :], oml[:, k:k + 1],
                                 lb[:, k:k + 1], ALU.mult, ALU.add)
            later(forget, 2)
            return [t]

        evac["fb"] = evac_fb

        def evac_qb(g, m, ps, done):
            k = 4 * g + m
            s = scratch.next()
            t = dve([done, *f2, *arena_free], v.tensor_tensor, QB[:, k, :], ps, F2M, ALU.mult)
            t1 = act([t] + s.free, s.ap[:, 0:S], QB[:, k, :], ACT.Sigmoid)
            qb_done[k] = pool([t1], gp.tensor_tensor, QB[:, k, :], QB[:, k, :], s.ap[:, 0:S], ALU.mult)
            s.free = [qb_done[k]]
            return [t]

        evac["qb"] = evac_qb

        W2 = 2 * S

        def doubled(Cp, Rp, n, h, free):
            cv = Cp.rearrange("p (b x) -> p b x", x=2 * h)
            rv = Rp.rearrange("p (b x) -> p b x", x=2 * h)
            nb = n // (2 * h)
            t = dve(free, v.tensor_tensor, rv[:, :, 0:h], rv[:, :, 0:h],
                    cv[:, :, 2 * h - 1:2 * h].to_broadcast([P, nb, h]), ALU.mult)
            t = dve([t], v.tensor_tensor, cv[:, :, h:2 * h], cv[:, :, h:2 * h],
                    cv[:, :, h - 1:h].to_broadcast([P, nb, h]), ALU.mult)
            return t

        o_done = {}
        hg = {}

        def meta_state():
            C0, R0, kd = hg["C"], hg["R"], hg["kL"]
            n = HB * NMETA
            fm = FB[:, :, 0:NMETA]
            cv = C0[:, 0:n]
            t = dve([*fb_done.values(), *arena_free, *hg["free"]], v.tensor_copy, cv.rearrange("p (h x) -> p h x", h=HB), fm)
            t1 = dve([], v.memset, R0[:, 0:n], 1.0)
            t = dve([], v.tensor_scalar, kd[:, 0:n].rearrange("p (h x) -> p h x", h=HB), fm, -1.0, 1.0, ALU.mult, ALU.add)
            for h in (1, 2, 4, 8):
                t = doubled(cv, R0[:, 0:n], n, h, [t, t1])
            t = dve([t], v.tensor_tensor, kd[:, 0:n], kd[:, 0:n], R0[:, 0:n], ALU.mult)
            yield
            yield
            for half in range(2):
                b = side_banks.next()
                PE.wait(b.free + [t])
                for j in range(4):
                    h = 4 * half + j
                    i = nc.tensor.transpose(b.ap[0:NMETA, j * P:(j + 1) * P], kd[:, h * NMETA:(h + 1) * NMETA], c("ident"))
                t2 = PE.mark(i)
                t2 = act([t2], hg["kM"][0:NMETA, half * 512:(half + 1) * 512], b.ap[0:NMETA, :], ACT.Copy)
                b.free = [t2]
            hg["kM_done"] = t2
            hg["free"] = [(PE.sem, PE.count), (VE.sem, VE.count)]

        def recurrence(pr):
            Cb, Rb, kL, qL, A, kK = hg["C"], hg["R"], hg["kL"], hg["qL"], hg["A"], hg["kK"]
            F = FB[:, 2 * pr:2 * pr + 2, NMETA:T]
            q = QB[:, 2 * pr:2 * pr + 2, :].rearrange("p h x -> p (h x)")
            h2 = lambda x: x.rearrange("p (h x) -> p h x", h=2)
            t = dve(hg["free"] + [qb_done[2 * pr], qb_done[2 * pr + 1]], v.tensor_copy, h2(Cb), F)
            t1 = dve([], v.memset, Rb, 1.0)
            tk = dve([], v.tensor_scalar, h2(kK), F, -1.0, 1.0, ALU.mult, ALU.add)
            yield
            b = side_banks.next()
            PE.wait(b.free + [tk])
            for j in range(4):
                w = slice(j * P, (j + 1) * P)
                i = mm(b.ap[:, w], kK[:, w], q[:, w])
            tp = PE.mark(i)
            four = lambda x: x.rearrange("p (a b) -> p a b", a=4)
            tA = dve([tp], v.tensor_tensor, four(A), four(b.ap), c("ident").unsqueeze(1).to_broadcast([P, 4, P]), ALU.mult)
            b.free = [tA]
            tprev = None
            yield
            for li, h in enumerate(LEVELS):
                right = lambda x: x.rearrange("p (b x) -> p b x", x=2 * h)[:, :, h:2 * h]
                left = lambda x: x.rearrange("p (b x) -> p b x", x=2 * h)[:, :, 0:h]
                ws = [t, t1, tk, tprev, *hg["init"]]
                tb_ = pool(ws, gp.tensor_tensor, left(kL), left(kK), left(Rb), ALU.mult)
                ta_ = dve(ws, v.tensor_tensor, right(qL), right(q), right(Cb), ALU.mult)
                t = doubled(Cb, Rb, W2, h, [t, t1, tb_])
                yield
                b = side_banks.next()
                PE.wait(b.free + [ta_, tb_])
                half = P // 2
                for j in range(4):
                    i = mm(b.ap[:, j * half:(j + 1) * half], kL[:, j * P:(j + 1) * P], right(qL[:, j * P:(j + 1) * P]))
                tprev = PE.mark(i)
                pairs = lambda x: x.rearrange("p (b h) -> p b h", h=h)
                tA = dve([tprev, lvl_marks[-1], tA], v.copy_predicated,
                         A.rearrange("p (a b x) -> p a b x", a=4, x=2 * h)[:, :, :, h:2 * h],
                         pairs(lvl[:, li * half:(li + 1) * half]).unsqueeze(1).to_broadcast([P, 4, half // h, h]),
                         b.ap[:, 0:4 * half].rearrange("p (a b h) -> p a b h", a=4, h=h))
                b.free = [tA]
            tk2 = dve([t, tprev], v.tensor_tensor, h2(kL)[:, :, 0:P], h2(kK)[:, :, 0:P], h2(Rb)[:, :, 0:P], ALU.mult)
            tq2 = dve([t, tprev], v.tensor_tensor, qL, q, Cb, ALU.mult)
            yield
            b = side_banks.next()
            PE.wait(b.free + [tk2])
            for j in range(2):
                i = nc.tensor.transpose(b.ap[:, j * P:(j + 1) * P], kL[:, j * S:j * S + P], c("ident"))
            t3 = PE.mark(i)
            kd = hg["kd"]
            t3 = act([t3] + hg["kd_free"], kd, b.ap[:, 0:S], ACT.Copy)
            b.free = [t3]
            yield
            b = side_banks.next()
            PE.wait(b.free + [hg["kM_done"], t3, *ib_done.values()])
            for j in range(2):
                h = 2 * pr + j
                w = slice(h * P, (h + 1) * P)
                mm(b.ap[:, j * P:(j + 1) * P], hg["kM"][0:NMETA, w], IB[0:NMETA, 0, w])
                i = mm(b.ap[:, S + j * P:S + (j + 1) * P], kd[:, j * P:(j + 1) * P], IB[:, 1, w])
            t4 = PE.mark(i)
            St = hg["S"]
            t5 = act([t4] + hg["S_free"], St[:, 0:S], b.ap[:, 0:S], ACT.Copy)
            for j in range(2):
                t6 = dve([t5, t], v.scalar_tensor_tensor, St[:, S + j * P:S + (j + 1) * P], St[:, j * P:(j + 1) * P],
                         Cb[:, j * S + P - 1:j * S + P], b.ap[:, S + j * P:S + (j + 1) * P], ALU.mult, ALU.add)
            b.free = [t6]
            hg["kd_free"] = [t4]
            yield
            b = side_banks.next()
            PE.wait(b.free + [t6, tq2, tA])
            for j in range(2):
                w = slice((2 * pr + j) * P, (2 * pr + j + 1) * P)
                for blk in range(2):
                    x = slice(j * S + blk * P, j * S + (blk + 1) * P)
                    mm(b.ap[:, x], IB[:, 1 + blk, w], A[:, x], True, False)
                    i = mm(b.ap[:, x], St[:, blk * S + j * P:blk * S + (j + 1) * P], qL[:, x], False, True)
            t7 = PE.mark(i)
            hg["S_free"] = [t7]
            hg["free"] = [t7, t6]
            t8 = act([t7], QB[:, 2 * pr:2 * pr + 2, :].rearrange("p h x -> p (h x)"), b.ap, ACT.Copy)
            b.free = [t8]
            for j in range(2):
                pending.append(out_norm(2 * pr + j, t8))

        def out_norm(h, o):
            f = head_factors.next()
            t = act(f.free + [o], f.ap[:, 0:S], QB[:, h, :], ACT.Square)
            yield
            b, t = yield from row_factor(f.ap, t, P, S)
            o_done[h] = dve([t], v.scalar_tensor_tensor, QB[:, h, :], QB[:, h, :], col("on"), b.ap[:, 0:S],
                            ALU.mult, ALU.mult)
            b.free = f.free = [o_done[h]]

        def level_masks():
            for _ in range(10):
                yield
            lvl_marks.append(pool([lvl_load, *meta_marks], gp.tensor_copy, lvl, lvl_in))

        pending.append(level_masks())
        run(p2_qi)
        run(p2_ki)
        run(p2_ka)
        run(p2_va)
        run(p2_qa)
        jobs["width"] = 2
        run(p2_fb)
        run(p2_ib)
        run(p2_qb)
        attn2_over = []

        def recurrences():
            while len(ya_done) < HA:
                yield
            attn2_over.extend([*ya_done.values(), chain["bias"]])
            free = [(q.sem, q.count) for q in (PE, SC, VE, GP)]
            hg.update(C=region(0, 2, W2), R=region(2, 2, W2), kL=region(4, 2, W2), qL=region(6, 2, W2),
                      A=region(8, 2, W2), kK=region(10, 2, W2), kd=region(12, 1, S), S=region(21.5, 2, W2),
                      kM=region(23.5, 4, 1024), free=free, kd_free=[], S_free=[])
            hg["init"] = [dve(free, v.memset, hg["qL"], 0.0), dve([], v.memset, hg["kL"], 0.0)]
            hg["free"] = free + hg["init"]
            SC.wait(hg["free"])
            yield
            yield from meta_state()
            for pr in range(HB // 2):
                yield from recurrence(pr)

        pending.append(recurrences())
        g2 = {}
        evac["ga"] = sigmoid_to(GA, F2M, f2[0], g2, "ga", attn2_over)
        run(p2_ga)
        ya, yb = {}, {}
        gate_ring = Ring([])
        gate_ring.slots = prob.slots + probT.slots
        evac["za"] = silu_times(gate_ring, QA, ya_done, F2M, f2[0], *hb, hb2_read, ya, wait=2)
        run(p2_za)

        def evac_ba(g, m, ps, done):
            k = 4 * g + m
            g2["pa", k] = dve([done, g2["ga", k]], v.tensor_tensor, GA[:, k, :], ps, GA[:, k, :], ALU.mult)
            return [g2["pa", k]]

        evac["ba"] = evac_ba
        p2_ba.ready = lambda kt: ya[kt]
        run(p2_ba)
        drain_jobs()
        evac["zb"] = silu_times(gate_ring, QB, o_done, F2M, f2[0], *hb_b, hb2_read, yb)
        run(p2_zb)
        GB = region(29, 16, KT, S)
        zb_read = [*zm_read]
        rec_over = list(o_done.values()) + [(PE.sem, PE.count), (SC.sem, SC.count)]
        evac["gb"] = sigmoid_to(GB, F2M, f2[0], g2, "gb", rec_over)
        run(p2_gb)
        h2_read = [(PE.sem, PE.count)]
        mg2, gb_read = {}, []

        def evac_bb(g, m, ps, done):
            k = 4 * g + m
            s = scratch.next()
            z, y = s.ap[:, 0:S], GA[:, k, :]
            tz = dve([done, g2["gb", k]] + s.free, v.tensor_tensor, z, ps, GB[:, k, :], ALU.mult)
            t = pool([tz, g2["pa", k]], gp.tensor_tensor, y, z, y, ALU.add)
            gb_read[:] = [tz]
            s.free = [t]

            def split():
                mg2[k] = split_to(ob_hi[:, k, 0:S], ob_lo[:, k, 0:S], y, t, h2_read)
            later(split, 7)
            return [tz]

        evac["bb"] = evac_bb
        p2_bb.ready = lambda kt: yb[kt]
        run(p2_bb)

        stores = []
        xT2 = region(29, 16, KT, S)
        x1_back = load(xT2.rearrange("p k n -> p (k n)"), x1_dram, [*x1_in_dram, gb_read[0]])
        OT = region(0, 16, 2, D)
        bb_over = rec_over + zb_read
        turned = {}

        def turn_x1():
            yield
            yield
            yield
            yield
            for k in range(KT):
                b = side_banks.next()
                PE.wait(b.free + [x1_back])
                for blk in range(2):
                    i = nc.tensor.transpose(b.ap[:, blk * P:(blk + 1) * P], xT2[:, k, blk * P:(blk + 1) * P], c("ident"))
                t = PE.mark(i)
                turned[k] = act([t, *bb_over], OT[:, :, k * P:(k + 1) * P],
                                b.ap[:, 0:S].rearrange("p (b n) -> p b n", b=2), ACT.Copy)
                b.free = [turned[k]]
                if k % 2:
                    yield

        pending.append(turn_x1())

        def evac_w2(g, m, ps, done):
            w = slice(g * 512, (g + 1) * 512)
            t = dve([done, turned[4 * g + 3]], v.tensor_tensor, OT[:, m, w], ps, OT[:, m, w], ALU.add)
            stores.append(load(out[0, m * P:(m + 1) * P, w], OT[:, m, w], [t]))
            return [t]

        evac["wout2"] = evac_w2
        p2_w.ready = lambda kt: mg2[kt]
        run(p2_w)
        drain_jobs()
        SP.wait(stores)


_INS = ["x", "positions", "pre_norm_g", "w_in", "q_a_norm_g", "w_q_b", "kv_a_norm_g", "w_kv_b", "conv_w",
        "w_o_mla", "w_o_conv", "w_out", "post_norm_g", "meta_tokens_2", "hgrn_lb_logits_2", "norm_g_2",
        "w_in_2", "q_norm_g_2", "k_norm_g_2", "idx_k_norm_g_2", "hgrn_out_norm_g_2", "w_branch_2", "w_out_2"]


def kernel(**inputs):
    import concourse.bacc as _bacc
    from concourse.bass_utils import run_bass_kernel_spmd as _run

    nc = _bacc.Bacc("TRN2", target_bir_lowering=False, num_devices=1)
    arrays, aps = {}, {}
    given = {name: np.ascontiguousarray(inputs[name]) for name in _INS}
    given["const_f"], given["const_lvl"] = CONST_F, CONST_LVL
    for name, arr in given.items():
        arrays[f"in_{name}"] = arr
        aps[name] = nc.dram_tensor(f"in_{name}", arr.shape, mybir.dt.from_np(arr.dtype), kind="ExternalInput").ap()
    out = nc.dram_tensor("out_0", (1, S, D), F32, kind="ExternalOutput").ap()
    build(nc, aps, out)
    r = _run(nc, [arrays], core_ids=[0])
    return r.results[0]["out_0"]
```
